# Optimizing a Trainium2 kernel written in Bass

```python
import jax
import jax.numpy as jnp
from jax import lax
import numpy as np

D_MODEL = 1024
BATCH = 1
SEQ = 1024
DEPTH = 1

N_META = 16
RWKV_HEADS = 8
HEAD_SIZE = 64
RWKV_WIDTH = RWKV_HEADS * HEAD_SIZE
CONV_GROUPS = 8
CONV_WIDTH = D_MODEL // 2
CONV_K = 3
DECAY_LORA = 64
AAA_LORA = 64
GATE_LORA = 128
N_EXPERTS = 32
TOP_K = 4
D_FF = D_MODEL
SWIGLU_ALPHA = 1.702
SWIGLU_LIMIT = 7.0
MOE_BLOCK = 128
NORM_EPS = 1e-5
LNX_EPS = 64e-5
IN_COLS = 3 * RWKV_WIDTH + 3 * CONV_WIDTH + 2 * D_MODEL

kernel_name = "hybrid_rwkv7_shortconv_moe_block"

def _rmsnorm(x, g):
    xf = x.astype(jnp.float32)
    y = xf * lax.rsqrt(jnp.mean(xf * xf, axis=-1, keepdims=True) + NORM_EPS)
    return (y * g.astype(jnp.float32)).astype(x.dtype)

def _token_shift(z):
    return jnp.pad(z[:, :-1], ((0, 0), (1, 0), (0, 0)))

def _wkv7_scan(r, decay, k, v, kk, a):
    b, _, h, n = r.shape

    def step(S, inp):
        r_t, w_t, k_t, v_t, kk_t, a_t = inp
        sa = jnp.einsum('bhij,bhj->bhi', S, -kk_t)
        S = (S * w_t[:, :, None, :]
             + sa[..., None] * (kk_t * a_t)[:, :, None, :]
             + v_t[..., None] * k_t[:, :, None, :])
        y_t = jnp.einsum('bhij,bhj->bhi', S, r_t)
        return S, y_t

    s0 = jnp.zeros((b, h, n, n), jnp.float32)
    seq_major = tuple(jnp.moveaxis(z, 1, 0) for z in (r, decay, k, v, kk, a))
    _, y = lax.scan(step, s0, seq_major)
    return jnp.moveaxis(y, 0, 1)

def _rwkv7_branch(x_n, pr, pk, pv, mu_r, mu_k, mu_v, mu_w, mu_a, mu_g, w0, w_w1, w_w2,
                  a0, w_a1, w_a2, w_g1, w_g2, k_k, k_a, r_k, lnx_g, lnx_b, w_o_rwkv):
    b, L, _ = x_n.shape
    dt = x_n.dtype
    r = pr + (_token_shift(pr) - pr) * mu_r
    k = pk + (_token_shift(pk) - pk) * mu_k
    v = pv + (_token_shift(pv) - pv) * mu_v
    dx = _token_shift(x_n) - x_n
    xw = x_n + dx * mu_w
    xa = x_n + dx * mu_a
    xg = x_n + dx * mu_g
    w_log = -jax.nn.softplus(-(w0 + jnp.tanh(xw @ w_w1) @ w_w2)) - 0.5
    a = jax.nn.sigmoid(a0 + (xa @ w_a1) @ w_a2)
    g = jax.nn.sigmoid(xg @ w_g1) @ w_g2

    heads = lambda z: z.astype(jnp.float32).reshape(b, L, RWKV_HEADS, HEAD_SIZE)
    kk = heads(k * k_k)
    kk = kk / jnp.maximum(jnp.sqrt(jnp.sum(kk * kk, axis=-1, keepdims=True)), 1e-12)
    k = k * (1.0 + (a - 1.0) * k_a)
    r_h, k_h, v_h, a_h = heads(r), heads(k), heads(v), heads(a)
    decay = jnp.exp(-jnp.exp(heads(w_log)))

    y = _wkv7_scan(r_h, decay, k_h, v_h, kk, a_h)
    mean = jnp.mean(y, axis=-1, keepdims=True)
    var = jnp.mean((y - mean) ** 2, axis=-1, keepdims=True)
    yn = ((y - mean) * lax.rsqrt(var + LNX_EPS)).reshape(b, L, RWKV_WIDTH)
    yn = yn * lnx_g.astype(jnp.float32) + lnx_b.astype(jnp.float32)
    rk = r_k.astype(jnp.float32).reshape(RWKV_HEADS, HEAD_SIZE)
    bonus = (jnp.sum(r_h * k_h * rk, axis=-1, keepdims=True) * v_h).reshape(b, L, RWKV_WIDTH)
    return ((yn + bonus).astype(dt) * g) @ w_o_rwkv

def _short_conv_branch(cb, cc, ch, conv_w, w_o_conv):
    L = ch.shape[1]
    u = cc * ch
    upad = jnp.pad(u, ((0, 0), (CONV_K - 1, 0), (0, 0)))
    conv = sum(conv_w[j] * upad[:, j:j + L] for j in range(CONV_K))
    return (cb * conv) @ w_o_conv

def _moe(h, w_router, b_router, w_e_gate, b_e_gate, w_e_up, b_e_up, w_e_down, b_e_down):
    b, L, d = h.shape
    dt = h.dtype
    T = b * L
    xf = h.reshape(T, d)
    logits = (xf @ w_router + b_router).astype(jnp.float32)
    top_v, top_i = lax.top_k(logits, TOP_K)
    gates = jax.nn.softmax(top_v, axis=-1).astype(dt)

    n_assign = T * TOP_K
    flat_e = top_i.reshape(-1)
    flat_w = gates.reshape(-1)
    flat_tok = jnp.repeat(jnp.arange(T, dtype=jnp.int32), TOP_K)
    order = jnp.argsort(flat_e)
    sorted_e = flat_e[order]
    counts = jnp.bincount(flat_e, length=N_EXPERTS).astype(jnp.int32)
    padded = ((counts + MOE_BLOCK - 1) // MOE_BLOCK) * MOE_BLOCK
    start = jnp.cumsum(counts) - counts
    pend = jnp.cumsum(padded)
    pstart = pend - padded
    rank = jnp.arange(n_assign, dtype=jnp.int32) - start[sorted_e]
    dest = pstart[sorted_e] + rank
    P = -(-n_assign // MOE_BLOCK) * MOE_BLOCK + N_EXPERTS * MOE_BLOCK
    n_blk = P // MOE_BLOCK
    row_tok = jnp.zeros((P,), jnp.int32).at[dest].set(flat_tok[order])
    row_w = jnp.zeros((P,), dt).at[dest].set(flat_w[order])
    blk_start = jnp.arange(n_blk, dtype=jnp.int32) * MOE_BLOCK
    blk_e = jnp.minimum(jnp.searchsorted(pend, blk_start, side='right'), N_EXPERTS - 1)

    def expert_block(args):
        e, toks, wts = args
        xb = xf[toks]
        gt = jnp.minimum(xb @ w_e_gate[e] + b_e_gate[e], SWIGLU_LIMIT)
        up = jnp.clip(xb @ w_e_up[e] + b_e_up[e], -SWIGLU_LIMIT, SWIGLU_LIMIT)
        act = (up + 1.0) * (gt * jax.nn.sigmoid(gt * SWIGLU_ALPHA))
        return (act @ w_e_down[e] + b_e_down[e]) * wts[:, None]

    ys = lax.map(expert_block, (blk_e, row_tok.reshape(n_blk, MOE_BLOCK),
                                row_w.reshape(n_blk, MOE_BLOCK)))
    out = jnp.zeros((T, d), dt).at[row_tok].add(ys.reshape(P, d))
    return out.reshape(b, L, d)

def setup_inputs(seed: int = 0) -> dict:
    key = jax.random.key(seed)
    ks = iter(jax.random.split(key, 48))
    f32 = jnp.float32
    R, C, D = RWKV_WIDTH, CONV_WIDTH, D_MODEL

    def nrm(shape, scale):
        return scale * jax.random.normal(next(ks), shape, f32)

    def uni(shape):
        return jax.random.uniform(next(ks), shape, f32, 0.2, 0.8)

    n = jnp.arange(R, dtype=f32) / (R - 1)
    w0_base = (-6.5 + 5.0 * n ** 0.85)[None, :]
    return {
        "x": nrm((BATCH, SEQ, D), 1.0),
        "meta_tokens": nrm((N_META, D), 1.0),
        "ln1_g": 1.0 + nrm((DEPTH, D), 0.01),
        "w_in": nrm((DEPTH, D, IN_COLS), D ** -0.5),
        "mu_r": uni((DEPTH, R)),
        "mu_k": uni((DEPTH, R)),
        "mu_v": uni((DEPTH, R)),
        "mu_w": uni((DEPTH, D)),
        "mu_a": uni((DEPTH, D)),
        "mu_g": uni((DEPTH, D)),
        "w0": w0_base + nrm((DEPTH, R), 0.1),
        "w_w1": nrm((DEPTH, D, DECAY_LORA), D ** -0.5),
        "w_w2": nrm((DEPTH, DECAY_LORA, R), 0.1 * DECAY_LORA ** -0.5),
        "a0": nrm((DEPTH, R), 0.1),
        "w_a1": nrm((DEPTH, D, AAA_LORA), D ** -0.5),
        "w_a2": nrm((DEPTH, AAA_LORA, R), AAA_LORA ** -0.5),
        "w_g1": nrm((DEPTH, D, GATE_LORA), D ** -0.5),
        "w_g2": nrm((DEPTH, GATE_LORA, R), GATE_LORA ** -0.5),
        "k_k": 0.85 + nrm((DEPTH, R), 0.05),
        "k_a": 1.0 + nrm((DEPTH, R), 0.05),
        "r_k": nrm((DEPTH, R), 0.1),
        "lnx_g": 1.0 + nrm((DEPTH, R), 0.01),
        "lnx_b": nrm((DEPTH, R), 0.01),
        "w_o_rwkv": nrm((DEPTH, R, D), R ** -0.5),
        "conv_w": nrm((DEPTH, CONV_K, C), CONV_K ** -0.5),
        "w_o_conv": nrm((DEPTH, C, D), C ** -0.5),
        "w_o": nrm((DEPTH, D, D), D ** -0.5),
        "ln2_g": 1.0 + nrm((DEPTH, D), 0.01),
        "w_router": nrm((DEPTH, D, N_EXPERTS), D ** -0.5),
        "b_router": nrm((DEPTH, N_EXPERTS), 0.01),
        "w_e_gate": nrm((DEPTH, N_EXPERTS, D, D_FF), D ** -0.5),
        "b_e_gate": nrm((DEPTH, N_EXPERTS, D_FF), 0.01),
        "w_e_up": nrm((DEPTH, N_EXPERTS, D, D_FF), D ** -0.5),
        "b_e_up": nrm((DEPTH, N_EXPERTS, D_FF), 0.01),
        "w_e_down": nrm((DEPTH, N_EXPERTS, D_FF, D), D_FF ** -0.5),
        "b_e_down": nrm((DEPTH, N_EXPERTS, D), 0.01),
        "lnf_g": 1.0 + nrm((D,), 0.01),
    }

def reference(x, meta_tokens, ln1_g, w_in, mu_r, mu_k, mu_v, mu_w, mu_a, mu_g, w0, w_w1, w_w2,
              a0, w_a1, w_a2, w_g1, w_g2, k_k, k_a, r_k, lnx_g, lnx_b, w_o_rwkv, conv_w,
              w_o_conv, w_o, ln2_g, w_router, b_router, w_e_gate, b_e_gate, w_e_up, b_e_up,
              w_e_down, b_e_down, lnf_g):
    b = x.shape[0]
    R, C, D = RWKV_WIDTH, CONV_WIDTH, D_MODEL
    meta = jnp.broadcast_to(meta_tokens[None].astype(x.dtype), (b, N_META, D))
    h = jnp.concatenate([meta, x], axis=1)
    cuts = [R, 2 * R, 3 * R, 3 * R + C, 3 * R + 2 * C, 3 * R + 3 * C, 3 * R + 3 * C + D]
    for l in range(DEPTH):
        x_n = _rmsnorm(h, ln1_g[l])
        proj = x_n @ w_in[l]
        pr, pk, pv, cb, cc, ch, gate_a, gate_b = jnp.split(proj, cuts, axis=-1)
        y_a = _rwkv7_branch(x_n, pr, pk, pv, mu_r[l], mu_k[l], mu_v[l], mu_w[l], mu_a[l], mu_g[l],
                            w0[l], w_w1[l], w_w2[l], a0[l], w_a1[l], w_a2[l], w_g1[l], w_g2[l],
                            k_k[l], k_a[l], r_k[l], lnx_g[l], lnx_b[l], w_o_rwkv[l])
        y_b = _short_conv_branch(cb, cc, ch, conv_w[l], w_o_conv[l])
        merged = jax.nn.sigmoid(gate_a) * y_a + jax.nn.sigmoid(gate_b) * y_b
        h = h + merged @ w_o[l]
        h = h + _moe(_rmsnorm(h, ln2_g[l]), w_router[l], b_router[l], w_e_gate[l], b_e_gate[l],
                     w_e_up[l], b_e_up[l], w_e_down[l], b_e_down[l])
    h = _rmsnorm(h, lnf_g)
    return h[:, N_META:]


_drawn_inputs = setup_inputs


def setup_inputs(seed=0):
    import zlib

    import numpy as np

    out = dict(_drawn_inputs(seed))
    spreads = {}
    factors = {'mu_w': 8.0,
     'w_w1': 6.143,
     'w_w2': 4.264,
     'lnx_g': 13.944,
     'lnx_b': 13.353,
     'b_e_gate': 23.103,
     'b_e_up': 29.151,
     'b_e_down': 53.166,
     'lnf_g': 154.469,
     'ln2_g': 3.18,
     'b_router': 2.936}
    for name, (base, spread) in spreads.items():
        noise = np.random.default_rng([zlib.crc32(name.encode()), seed]).standard_normal(out[name].shape)
        drawn = base * np.exp(spread * noise) if base else spread * noise
        out[name] = jnp.asarray(drawn.astype(out[name].dtype))
    for name, factor in factors.items():
        out[name] = (out[name] * factor).astype(out[name].dtype)
    return out
```

```python
from contextlib import ExitStack

import concourse.bass as bass
from concourse import mybir


class Plan:

    def __init__(self, nc, at):
        self.nc, self.at = nc, at

    def __call__(self, name, shape, dt=mybir.dt.float32):
        size = 4
        for n in shape[1:]:
            size *= n
        t = self.nc.alloc_sbuf_tensor_at(name, shape, dt, offset=self.at)
        self.at += (size + 31) // 32 * 32
        return t[(slice(None),) * len(shape)]


def mixing_program(nc, ctx, a, bank, keep, shared):
    f32 = mybir.dt.float32
    f32r = mybir.dt.float32r
    u32 = mybir.dt.uint32
    ALU = mybir.AluOpType
    ACT = mybir.ActivationFunctionType
    AX = mybir.AxisListType

    D = 1024
    META = 16
    TOK = 1040
    NT = 10
    TP = TOK // NT
    KT = D // 128
    RW = 512
    NJ = RW // 128
    HS = 64
    NCH = 4
    CH = TOK // NCH
    NU = 2 * NT
    NB = NU // 4
    LEVELS = 7
    EPS = 1e-5
    LNX_EPS = 64e-5
    DECAY = 0.6065306597126334

    if True:
        def sem(name):
            return ctx.enter_context(nc.semaphore(name))

        ident, eps_t, h_all, zero_out, wo_add = shared['ident'], shared['eps_t'], shared['h_all'], shared['zero_out'], shared['wo_add']
        epsx_t = keep("epsx_t", [128, 1])
        dz = keep("dz", [128, 8])
        ones_t = keep("ones_t", [128, 1])
        START = shared['start']

        wk = Plan(nc, START)
        AT = wk("AT", [TP, NU, 4, TP])
        Tm = wk("Tm", [TP, NU, TP])
        Rm = wk("Rm", [TP, NU, TP])
        P1 = wk("P1", [TP, 2, 4, TP])
        Vt = wk("Vt", [TP, NT, 128])
        Bt = wk("Bt", [TP, NT, 128])
        Kt = wk("Kt", [TP, NT, 128])
        X = wk("X", [TP, NU, 128])
        x1t = wk("x1t", [128, NT, TP])
        mxt = wk("mxt", [128, NT, HS])
        np_ = wk("np_", [128, NT, HS])
        S = wk("S", [128, NT + 1, HS])
        U = wk("U", [TP, NU, HS])
        pr = Plan(nc, START)
        pb = pr("pb", [128, 3, TOK + 2])
        r_t = pr("r_t", [128, TOK])
        k_t = pr("k_t", [128, TOK])
        sg = pr("sg", [128, TOK])
        cs = pr("cs", [128, TOK])
        e0 = pr("e0", [128, TOK])
        e1 = pr("e1", [128, TOK])
        e2 = pr("e2", [128, TOK])
        a_t = pr("a_t", [128, TOK])
        kk = pr("kk", [128, TOK])
        tmp = pr("tmp", [128, TOK])
        nrm = pr("nrm", [128, TOK])
        assert pr.at <= wk.at
        s0 = Plan(nc, START)
        x_in = s0("x_in", [TP, 2, D])
        xn = s0("xn", [TP, 2, D])
        junk = s0("junk", [TP, D])
        ss = s0("ss", [TP, NT])
        rstd = s0("rstd", [TP, NT])
        lraw = s0("lraw", [128, KT, 256])
        lmu = s0("lmu", [128, KT, 256])
        o1 = s0("o1", [128, 2, TOK])
        o2 = s0("o2", [128, 2, TOK + 1])
        vrows = s0("vrows", [84, 128])
        assert s0.at <= wk.at
        s1 = Plan(nc, shared['after_h'])
        mT = s1("mT", [128, KT, TOK])
        cv = s1("cv", [128, NJ, TOK])
        assert s1.at <= wk.at
        s2 = Plan(nc, START)
        cpb = s2("cpb", [128, 3, TOK + 2])
        c1 = s2("c1", [128, TOK])
        gt = s2("gt", [128, 2, 2, CH])
        m1 = s2("m1", [128, 2, CH])
        assert s2.at <= START + 4 * NT * D

        com = Plan(nc, wk.at)
        xnT = com("xnT", [128, KT, TOK])
        yg = com("yg", [128, NJ, TOK])
        ring = com("ring", [128, 3, KT, 128])
        bones = com("bones", [128, 128])
        mask4 = com("mask4", [TP, 4, TP])
        mlev = com("mlev", [TP, LEVELS, 128])
        id2 = com("id2", [128, HS])
        vec = com("vec", [128, 84])
        vj = com("vj", [128, 12])
        pc = com("pc", [128, NT])
        J0 = com.at
        lw = com("lw", [128, TOK])
        lg = com("lg", [128, TOK])
        w2 = com("w2", [128, RW])
        wg2 = com("wg2", [128, RW])
        w2j = com("w2j", [128, 128])
        wg2j = com("wg2j", [128, 128])
        v_t = com("v_t", [128, TOK])
        rkb = com("rkb", [128, TOK])
        y_t = com("y_t", [128, TOK])
        ar = com("ar", [128, NT, 2, TP])
        zero = ar.rearrange("p c m t -> p (c m t)")
        bh = com("bh", [128, TOK])
        kh = com("kh", [128, TOK])
        wo_t = Plan(nc, J0)("wo_t", [128, KT, D])
        assert J0 + 4 * KT * D <= com.at

        VEC = {}
        at = 0
        for name, n in (('mu_w', 8), ('mu_a', 8), ('mu_g', 8), ('ln1_g', 8), ('mu_r', 4), ('mu_k', 4), ('mu_v', 4), ('w0', 4),
                        ('a0', 4), ('k_k', 4), ('k_a', 4), ('r_k', 4), ('lnx_g', 4), ('lnx_b', 4), ('conv_w', 12)):
            VEC[name] = at
            at += n
        assert at == 84
        JV = {name: i for i, name in enumerate(('mu_r', 'mu_k', 'mu_v', 'w0', 'a0', 'k_k', 'k_a', 'r_k', 'lnx_g', 'lnx_b'))}

        def pj(name):
            return vj[:, JV[name]:JV[name] + 1]

        TA = 'vbka'
        PE_J = ([('z', c) for c in range(NCH)] + [('p', i, c) for i in range(3) for c in range(NCH)]
                + [('n', c) for c in range(NCH)] + [('t', x, g) for x in TA for g in range(3)]
                + [('A', u) for u in range(NU)])
        for l in range(LEVELS):
            for s in range(NB + 1):
                if s < NB:
                    PE_J.append(('P', l, s))
                if s > 0:
                    PE_J.append(('D', l, s - 1))
        PE_J += ([('xa', g) for g in range(3)] + [('xc', g) for g in range(3)] + [('xb', g) for g in range(5)]
                 + [('m', g) for g in range(2)] + [('nn', g) for g in range(2)] + [('s', c) for c in range(1, NT)]
                 + [('u', g) for g in range(2)] + [('y', g) for g in range(3)]
                 + [('bs', c) for c in range(NCH)] + [('g', c) for c in range(NCH)]
                 + [('mean', c) for c in range(NCH)] + [('var', c) for c in range(NCH)])
        ACT_J = ([(x, c) for c in range(NCH) for x in 'za'] + [('p', i, c) for i in range(3) for c in range(NCH)]
                 + ['E1', 'E2', 'E0', 'sq'] + [('n', c) for c in range(NCH)] + [('t', x, g) for x in TA for g in range(3)]
                 + [('xa', g) for g in range(3)] + [('xc', g) for g in range(3)] + [('xb', g) for g in range(5)]
                 + [('y', g) for g in range(3)] + ['ysq'] + [('var', c) for c in range(NCH)])
        DVE_J = ([('cs', c) for c in range(NT)] + ['csx', 'r_d', 'r', 'k_d', 'k', 'kkr', 'v_d', 'v', 'km', 'kmod', 'rkb', 'rt', 'kh',
                                                   'pc', 'nmax', 'nrec', 'kk', 'at', 'ba', 'bh']
                 + [('A', u) for u in range(NU)])
        for l in range(LEVELS):
            for s in range(NB + 1):
                if s < NB:
                    DVE_J.append(('P', l, s))
                if s > 0:
                    DVE_J += [('T', l, s - 1), ('R', l, s - 1)]
        DVE_J += ([('m', g) for g in range(2)] + [('nn', g) for g in range(2)] + ['S0'] + [('S', c) for c in range(NT)]
                  + [('u', g, h) for g in range(2) for h in range(2)] + [('bo', c) for c in range(NCH)]
                  + [('yc', c) for c in range(NCH)] + ['yrec', 'yn', 'yaff', 'ysum'] + [('yg', c) for c in range(NCH)])
        POOL_J = ['vj', 'w2', 'wg2', 'T0', 'R0']

        class Order:
            def __init__(self, sem, labels):
                self.sem, self.labels, self.next = sem, {x: i for i, x in enumerate(labels)}, 0
                assert len(self.labels) == len(labels)

            def done(self, eng, label, j, passed=None):
                eng.wait_ge(self.sem, j * len(self.labels) + self.labels[label] + 1)
                if passed is not None:
                    eng.sem_inc(passed, 1)

            def mark(self, ins, label):
                assert self.labels[label] == self.next, label
                self.next = (self.next + 1) % len(self.labels)
                ins.then_inc(self.sem, 1)

        pe_j = Order(sem("pe_j"), PE_J)
        act_j = Order(sem("act_j"), ACT_J)
        dve_j = Order(sem("dve_j"), DVE_J)
        pool_j = Order(sem("pool_j"), POOL_J)

        vec_in = sem("vec_in")
        x_got = [sem("x_got0"), sem("x_got1")]
        lora_in = sem("lora_in")
        w2_in = sem("w2_in")
        ring_in = [sem(f"ring_in{s}") for s in range(3)]
        h_in = sem("h_in")
        wo_in = sem("wo_in")
        pool_c = sem("pool_c")
        dve_c = sem("dve_c")
        vec_ps = sem("vec_ps")
        vec_done = sem("vec_done")
        sq0_done = sem("sq0_done")
        std0_done = sem("std0_done")
        rstd0_done = sem("rstd0_done")
        xn_done = sem("xn_done")
        xnT_ps = sem("xnT_ps")
        xnT_done = sem("xnT_done")
        lmu_done = sem("lmu_done")
        lora_ps = sem("lora_ps")
        lora_ev = sem("lora_ev")
        lora_mix = sem("lora_mix")
        lora_done = sem("lora_done")
        conv_ps = sem("conv_ps")
        conv_ev = sem("conv_ev")
        conv_step = sem("conv_step")
        gate_ps = sem("gate_ps")
        gate_sig = sem("gate_sig")
        gate_mul = sem("gate_mul")
        wo_ps = sem("wo_ps")
        sp_passed = sem("sp_passed")
        pool_passed = sem("pool_passed")
        pe_passed = sem("pe_passed")
        col_free = sem("col_free")
        pbz = sem("pbz")


        w_in = a['w_in']

        def cols(w, c0, n=128):
            return w[:, bass.ds(c0, n)].rearrange("(k p) c -> p k c", p=128)

        def x_tile(t):
            if t == 0:
                return [((0, META), a['meta_tokens']), ((META, TP), a['x'][0:TP - META, :])]
            return [((0, TP), a['x'][TP * t - META:TP * (t + 1) - META, :])]

        def on_sync(sp):
            for name in ('mu_w', 'mu_a', 'mu_g', 'ln1_g', 'mu_r', 'mu_k', 'mu_v', 'w0', 'a0', 'k_k', 'k_a', 'r_k', 'lnx_g', 'lnx_b'):
                n = a[name].shape[0] // 128
                sp.dma_start(vrows[VEC[name]:VEC[name] + n, :], a[name].rearrange("(k p) -> k p", p=128)).then_inc(vec_in, 16)
            sp.dma_start(vrows[VEC['conv_w']:VEC['conv_w'] + 12, :], a['conv_w'].rearrange("w (k p) -> (w k) p", p=128)
                         ).then_inc(vec_in, 16)
            sp.wait_ge(dve_c, 6)
            sp.dma_start(shared['rowtok_d'], zero[0:shared['rounds'], 0:shared['slots']].bitcast(u32)).then_inc(zero_out, 16)
            for t in range(NT):
                if t >= 2:
                    sp.wait_ge(xn_done, t - 1)
                    sp.wait_ge(sq0_done, t - 1)
                for (p0, p1), src in x_tile(t):
                    sp.dma_start(x_in[p0:p1, t % 2, :], src).then_inc(x_got[t % 2], 16)
            sp.dma_start(lraw[:, :, 0:64], cols(a['w_w1'], 0, 64)).then_inc(lora_in, 16)
            sp.dma_start(lraw[:, :, 64:128], cols(a['w_a1'], 0, 64)).then_inc(lora_in, 16)
            sp.dma_start(lraw[:, :, 128:256], cols(a['w_g1'], 0, 128)).then_inc(lora_in, 16)
            sp.dma_start(w2[0:64, :], a['w_w2']).then_inc(w2_in, 16)
            sp.dma_start(w2[64:128, :], a['w_a2']).then_inc(w2_in, 16)
            sp.dma_start(wg2[:, :], a['w_g2']).then_inc(w2_in, 16)
            for rows in shared['ys_rest']:
                sp.dma_start(rows, zero[0:rows.shape[0], 0:rows.shape[1]]).then_inc(zero_out, 16)

            def load(i, c0):
                sp.dma_start(ring[:, i, :, :], cols(w_in, c0)).then_inc(ring_in[i], 16)

            for i in range(3):
                load(i, RW * i)
            with sp.Fori(0, NJ - 1) as j:
                for i in range(3):
                    pe_j.done(sp, ('p', i, NCH - 1), j, sp_passed)
                    load(i, (j + 1) * 128 + RW * i)
            for i in range(3):
                pe_j.done(sp, ('p', i, NCH - 1), NJ - 1)
                load(i, RW * (3 + i))
            with sp.Fori(0, NJ - 1) as j:
                for i in range(3):
                    sp.wait_ge(conv_ps, j * 12 + 4 * i + 4)
                    sp.sem_inc(sp_passed, 1)
                    load(i, (j + 1) * 128 + RW * (3 + i))

            def load_gates(d):
                for i in range(2):
                    load(i, d * 128 + 6 * RW + D * i)
                sp.dma_start(ring[:, 2, 0:4, :], cols(a['w_o_rwkv'], d * 128)).then_inc(ring_in[2], 16)
                sp.dma_start(ring[:, 2, 4:8, :], cols(a['w_o_conv'], d * 128)).then_inc(ring_in[2], 16)

            sp.wait_ge(conv_ps, NJ * 12)
            load_gates(0)
            with sp.Fori(0, KT - 1) as d:
                sp.wait_ge(gate_ps, d * 4 + 4)
                sp.sem_inc(sp_passed, 1)
                load_gates(d + 1)
            dve_j.done(sp, ('yg', NCH - 1), NJ - 1)
            sp.dma_start(wo_t[:, :, :], a['w_o'].rearrange("(k p) c -> p k c", p=128)).then_inc(wo_in, 16)
            sp.wait_ge(gate_mul, 3 * KT * NCH + 6)
            for t in range(NT):
                for (p0, p1), src in x_tile(t):
                    sp.dma_start(h_all[p0:p1, t, :], src).then_inc(h_in, 16)

        def on_gpsimd(pool):
            n = [0]

            def step(ins):
                n[0] += 1
                ins.then_inc(pool_c, 1)
                pool.wait_ge(pool_c, n[0])

            def select(out, op, base, pattern, cm, fill):
                step(nc.gpsimd.affine_select(out=out, in_=out, compare_op=op, fill=fill, base=base, pattern=pattern,
                                             channel_multiplier=cm))

            step(nc.gpsimd.memset(ident[:, :], 0.0))
            select(ident[:, :], ALU.not_equal, 0, [[-1, 128]], 1, 1.0)
            step(nc.gpsimd.memset(id2[:, :], 0.0))
            select(id2[:, :], ALU.not_equal, 0, [[-1, HS]], 1, 1.0)
            select(id2[:, :], ALU.not_equal, -HS, [[-1, HS]], 1, 1.0)
            step(nc.gpsimd.memset(bones[:, :], 0.0))
            step(nc.gpsimd.memset(bones[0:HS, 0:HS], 1.0))
            step(nc.gpsimd.memset(bones[HS:128, HS:128], 1.0))
            step(nc.gpsimd.memset(mask4[:, :, :], 1.0))
            for m in range(4):
                select(mask4[:, m, :], ALU.is_gt if m % 2 == 0 else ALU.is_ge, 0, [[1, TP]], -1, 0.0)
            step(nc.gpsimd.memset(mlev[:, :, :], 1.0))
            for l in range(LEVELS):
                b = 2 << l
                h = b // 2
                v = mlev[:, l, :]
                pat = [[-b, 128 // b], [0, b]]
                select(v, ALU.is_ge, -h, pat, 1, 0.0)
                select(v, ALU.is_gt, b, [[b, 128 // b], [0, b]], -1, 0.0)
                select(v, ALU.is_gt, h, [[0, 128 // b], [-1, b]], 0, 0.0)

            pool.wait_ge(vec_done, 1)
            pool.wait_ge(w2_in, 48)
            with pool.Fori(0, NJ) as j:
                pool.wait_ge(col_free, j + 1)
                pool.sem_inc(pool_passed, 1)
                pool_j.mark(nc.gpsimd.tensor_copy(vj[:, 0:10], vec[:, VEC['mu_r']:VEC['mu_r'] + 40].rearrange(
                    "p (a k) -> p a k", k=4)[:, :, bass.ds(j, 1)].rearrange("p a k -> p (a k)")), 'vj')
                pool_j.mark(nc.gpsimd.tensor_copy(w2j[:, :], w2[:, bass.ds(j * 128, 128)]), 'w2')
                pool_j.mark(nc.gpsimd.tensor_copy(wg2j[:, :], wg2[:, bass.ds(j * 128, 128)]), 'wg2')
                dve_j.done(pool, 'bh', j, pool_passed)
                for m, x in ((Tm, 'T0'), (Rm, 'R0')):
                    pool_j.mark(nc.gpsimd.tensor_copy(m[:, :, :], ident[0:TP, 0:TP].unsqueeze(1).to_broadcast([TP, NU, TP])), x)

        def evac_groups():
            return ((0, 4), (4, 8), (8, 10))

        def on_scalar(act):
            act.wait_ge(vec_ps, 1)
            nc.scalar.activation(vec[:, :], bank[7][:, 0:84], ACT.Copy).then_inc(vec_done, 1)
            for t in range(NT):
                act.wait_ge(x_got[t % 2], 16 * (t // 2 + 1 + (1 if t % 2 == 0 else 0)))
                if t:
                    act.wait_ge(sq0_done, t)
                nc.scalar.activation(junk[:, :], x_in[:, t % 2, :], ACT.Square, accum_out=ss[:, t:t + 1]).then_inc(sq0_done, 1)
                act.wait_ge(sq0_done, t + 1)
                act.wait_ge(dve_c, 6)
                nc.scalar.activation(rstd[:, t:t + 1], ss[:, t:t + 1], ACT.Sqrt, bias=eps_t[0:TP, :], scale=1.0 / D
                                     ).then_inc(std0_done, 1)
            for m in range(2):
                for c in range(NCH):
                    act.wait_ge(lora_ps, 4 * m + c + 1)
                    nc.scalar.activation(o1[:, m, CH * c:CH * (c + 1)], bank[c % 2][:, 0:CH], ACT.Copy).then_inc(lora_ev, 1)
                    nc.scalar.activation(o2[:, m, 1 + CH * c:1 + CH * (c + 1)], bank[2 + c % 2][:, 0:CH], ACT.Copy).then_inc(lora_ev, 1)
            act.wait_ge(lora_mix, 4)
            nc.scalar.activation(lw[0:64, :], o1[0:64, 0, :], ACT.Tanh).then_inc(lora_done, 1)
            nc.scalar.activation(lw[64:128, :], o1[64:128, 0, :], ACT.Copy).then_inc(lora_done, 1)
            nc.scalar.activation(lg[:, :], o1[:, 1, :], ACT.Sigmoid).then_inc(lora_done, 1)

            with act.Fori(0, NJ) as j:
                act.wait_ge(col_free, j + 1)
                pool_j.done(act, 'vj', j)
                for c in range(NCH):
                    pe_j.done(act, ('z', c), j)
                    act_j.mark(nc.scalar.activation(sg[:, CH * c:CH * (c + 1)], bank[2 + c % 2][:, 0:CH], ACT.Sigmoid,
                                                    bias=pj('w0')), ('z', c))
                    act_j.mark(nc.scalar.activation(a_t[:, CH * c:CH * (c + 1)], bank[4 + c % 2][:, 0:CH], ACT.Sigmoid,
                                                    bias=pj('a0')), ('a', c))
                for i in range(3):
                    for c in range(NCH):
                        pe_j.done(act, ('p', i, c), j)
                        act_j.mark(nc.scalar.activation(pb[:, i, 2 + CH * c:2 + CH * (c + 1)], bank[c % 2][:, 0:CH], ACT.Copy),
                                   ('p', i, c))
                dve_j.done(act, 'csx', j)
                act_j.mark(nc.scalar.activation(e1[:, :], cs[:, :], ACT.Exp, scale=-DECAY), 'E1')
                act_j.mark(nc.scalar.activation(e2[:, :], cs[:, :], ACT.Exp, scale=DECAY), 'E2')
                act_j.mark(nc.scalar.activation(e0[:, :], tmp[:, :], ACT.Exp, scale=-DECAY), 'E0')
                dve_j.done(act, 'kkr', j)
                act_j.mark(nc.scalar.activation(nrm[:, :], kk[:, :], ACT.Square), 'sq')
                pe_j.done(act, ('n', NCH - 1), j)
                for c in range(NCH):
                    act_j.mark(nc.scalar.activation(nrm[:, CH * c:CH * (c + 1)], bank[4 + c][:, 0:CH], ACT.Sqrt), ('n', c))
                dve_j.done(act, 'bh', j)
                q = 0
                for x in TA:
                    for g, (g0, g1) in enumerate(evac_groups()):
                        pe_j.done(act, ('t', x, g), j)
                        src = bank[2 + q % 2][0:TP, 0:128 * (g1 - g0)]
                        if x == 'a':
                            dst = X[:, 2 * g0:2 * g1, 0:HS]
                            src = src.rearrange("p (u n) -> p u n", n=HS)
                        else:
                            dst = dict(v=Vt, b=Bt, k=Kt)[x][:, g0:g1, :]
                            src = src.rearrange("p (c n) -> p c n", n=128)
                        act_j.mark(nc.scalar.activation(dst, src, ACT.Copy), ('t', x, g))
                        q += 1
                for g, (g0, g1) in enumerate(((0, 8), (8, 16), (16, 20))):
                    pe_j.done(act, ('xa', g), j)
                    act_j.mark(nc.scalar.activation(X[:, g0:g1, HS:128], bank[2 + g % 2][0:TP, 0:HS * (g1 - g0)].rearrange(
                        "p (u n) -> p u n", n=HS), ACT.Copy), ('xa', g))
                for g, (g0, g1) in enumerate(evac_groups()):
                    pe_j.done(act, ('xc', g), j)
                    act_j.mark(nc.scalar.activation(x1t[:, g0:g1, :], bank[4 + g % 2][:, 0:TP * (g1 - g0)].rearrange(
                        "p (c n) -> p c n", n=TP), ACT.Copy), ('xc', g))
                for g in range(5):
                    pe_j.done(act, ('xb', g), j)
                    act_j.mark(nc.scalar.activation(X[:, 4 * g:4 * g + 4, :], bank[6 + g % 2][0:TP, :].rearrange(
                        "p (u n) -> p u n", n=128), ACT.Copy), ('xb', g))
                for g, (g0, g1) in enumerate(evac_groups()):
                    pe_j.done(act, ('y', g), j)
                    act_j.mark(nc.scalar.activation(y_t[:, TP * g0:TP * g1], bank[6 + g % 2][:, 0:TP * (g1 - g0)], ACT.Copy),
                               ('y', g))
                dve_j.done(act, ('yc', NCH - 1), j)
                act_j.mark(nc.scalar.activation(tmp[:, :], y_t[:, :], ACT.Square), 'ysq')
                for c in range(NCH):
                    pe_j.done(act, ('var', c), j)
                    act_j.mark(nc.scalar.activation(nrm[:, CH * c:CH * (c + 1)], bank[4 + c % 2][:, 0:CH], ACT.Sqrt,
                                                    bias=epsx_t[:, :], scale=1.0 / HS), ('var', c))
            with act.Fori(0, NJ) as j:
                for i in range(3):
                    act.wait_ge(conv_step, j * 6 + 6)
                    for c in range(NCH):
                        act.wait_ge(conv_ps, j * 12 + 4 * i + c + 1)
                        nc.scalar.activation(cpb[:, i, 2 + CH * c:2 + CH * (c + 1)], bank[c % 2][:, 0:CH], ACT.Copy
                                             ).then_inc(conv_ev, 1)
            with act.Fori(0, KT) as d:
                for c in range(NCH):
                    s = c % 2
                    act.wait_ge(gate_mul, d * 12 + 3 * c + 3)
                    act.wait_ge(gate_ps, d * 4 + c + 1)
                    for m in range(2):
                        nc.scalar.activation(gt[:, s, m, :], bank[4 * s + m][:, 0:CH], ACT.Sigmoid).then_inc(gate_sig, 1)

        def on_vector(dve):
            def xnT_copy(t):
                dve.wait_ge(xnT_ps, t + 1)
                for h in range(2):
                    nc.vector.tensor_tensor(xnT[:, 4 * h:4 * h + 4, TP * t:TP * (t + 1)],
                                            bank[2 * (t % 2) + h][:, 0:4 * TP].rearrange("p (k t) -> p k t", k=4),
                                            vec[:, VEC['ln1_g'] + 4 * h:VEC['ln1_g'] + 4 * h + 4].unsqueeze(2).to_broadcast(
                                                [128, 4, TP]), ALU.mult).then_inc(xnT_done, 1)

            nc.vector.memset(eps_t[:, :], EPS).then_inc(dve_c, 1)
            nc.vector.memset(zero, 0.0).then_inc(dve_c, 1)
            nc.vector.memset(epsx_t[:, :], LNX_EPS).then_inc(dve_c, 1)
            nc.vector.memset(o2[:, :, 0:1], 0.0).then_inc(dve_c, 1)
            nc.vector.memset(ones_t[:, :], 1.0).then_inc(dve_c, 1)
            nc.vector.memset(pc[:, 1:2], 0.0).then_inc(col_free, 1)
            nc.vector.memset(pc[:, 2:3], 0.0).then_inc(dve_c, 1)
            for t in range(NT):
                dve.wait_ge(std0_done, t + 1)
                nc.vector.reciprocal(rstd[:, t:t + 1], rstd[:, t:t + 1]).then_inc(rstd0_done, 1)
                dve.wait_ge(rstd0_done, t + 1)
                if t >= 2:
                    dve.wait_ge(xnT_ps, t - 1)
                nc.vector.tensor_scalar(xn[:, t % 2, :], x_in[:, t % 2, :], rstd[:, t:t + 1], None, ALU.mult).then_inc(xn_done, 1)
                if t == 0:
                    dve.wait_ge(vec_done, 1)
                if t >= 1:
                    xnT_copy(t - 1)
            xnT_copy(NT - 1)
            dve.wait_ge(lora_in, 48)
            for m, (c0, c1_) in enumerate(((0, 64), (64, 128), (128, 256))):
                nc.vector.tensor_tensor(lmu[:, :, c0:c1_], lraw[:, :, c0:c1_],
                                        vec[:, 8 * m:8 * m + 8].unsqueeze(2).to_broadcast([128, KT, c1_ - c0]), ALU.mult
                                        ).then_inc(lmu_done, 1)
            for m in range(2):
                dve.wait_ge(lora_ev, 8 * (m + 1))
                nc.vector.tensor_tensor(o1[:, m, :], o1[:, m, :], o2[:, m, 1:TOK + 1], ALU.subtract).then_inc(lora_mix, 1)
                dve.wait_ge(lora_mix, 2 * m + 1)
                nc.vector.tensor_tensor(o1[:, m, :], o1[:, m, :], o2[:, m, 0:TOK], ALU.add).then_inc(lora_mix, 1)
            dve.wait_ge(lora_done, 3)
            dve.wait_ge(zero_out, 16 * (1 + len(shared['ys_rest'])))

            def tt(label, out, a_, b_, op):
                dve_j.mark(nc.vector.tensor_tensor(out, a_, b_, op), label)

            def stt(label, out, in0, s, in1, op0, op1):
                dve_j.mark(nc.vector.scalar_tensor_tensor(out=out, in0=in0, scalar=s, in1=in1, op0=op0, op1=op1), label)

            def chunks(x):
                return x.rearrange("p (c t) -> p c t", t=TP)

            with dve.Fori(0, NJ) as j:
                for c in range(NT):
                    act_j.done(dve, ('z', min(NCH - 1, (TP * (c + 1) - 1) // CH)), j)
                    dve_j.mark(nc.vector.tensor_tensor_scan(cs[:, TP * c:TP * (c + 1)], ones_t.to_broadcast([128, TP]), sg[:, TP * c:TP * (c + 1)],
                                                            0.0, ALU.mult, ALU.add), ('cs', c))
                dve_j.done(dve, ('cs', NT - 1), j)
                tt('csx', tmp[:, :], cs[:, :], sg[:, :], ALU.subtract)
                nc.vector.memset(pb[:, :, 0:2], 0.0).then_inc(pbz, 1)
                dve.wait_ge(pbz, j + 1)
                for i, (x, dst) in enumerate((('r', r_t), ('k', k_t), ('v', v_t))):
                    act_j.done(dve, ('p', i, NCH - 1), j)
                    if i == 0:
                        pool_j.done(dve, 'vj', j)
                    tt(x + '_d', dst[:, :], pb[:, i, 1:TOK + 1], pb[:, i, 2:TOK + 2], ALU.subtract)
                    dve_j.done(dve, x + '_d', j)
                    stt(x, dst[:, :], dst[:, :], pj('mu_' + x), pb[:, i, 2:TOK + 2], ALU.mult, ALU.add)
                    if x == 'k':
                        dve_j.done(dve, 'k', j)
                        dve_j.mark(nc.vector.tensor_scalar(kk[:, :], k_t[:, :], pj('k_k'), None, ALU.mult), 'kkr')
                act_j.done(dve, ('a', NCH - 1), j)
                dve_j.mark(nc.vector.tensor_scalar(pb[:, 0, 2:], a_t[:, :], 1.0, pj('k_a'), ALU.subtract, ALU.mult), 'km')
                dve_j.done(dve, 'km', j)
                stt('kmod', k_t[:, :], pb[:, 0, 2:], 1.0, k_t[:, :], ALU.add, ALU.mult)
                dve_j.done(dve, 'kmod', j)
                stt('rkb', rkb[:, :], r_t[:, :], pj('r_k'), k_t[:, :], ALU.mult, ALU.mult)
                act_j.done(dve, 'E0', j)
                tt('rt', ar[:, :, 1, :], chunks(r_t[:, :]), chunks(e1[:, :]), ALU.mult)
                tt('kh', kh[:, :], k_t[:, :], e2[:, :], ALU.mult)
                dve_j.mark(nc.vector.tensor_copy(pc[:, :], chunks(e1[:, :])[:, :, TP - 1]), 'pc')
                act_j.done(dve, ('n', NCH - 1), j)
                dve_j.mark(nc.vector.tensor_scalar(nrm[:, :], nrm[:, :], 1e-12, None, ALU.max), 'nmax')
                dve_j.done(dve, 'nmax', j)
                dve_j.mark(nc.vector.reciprocal(nrm[:, :], nrm[:, :]), 'nrec')
                dve_j.done(dve, 'nrec', j)
                tt('kk', kk[:, :], kk[:, :], nrm[:, :], ALU.mult)
                dve_j.done(dve, 'kk', j)
                stt('at', ar[:, :, 0, :], chunks(kk[:, :]), -1.0, chunks(e0[:, :]), ALU.mult, ALU.mult)
                tt('ba', tmp[:, :], kk[:, :], a_t[:, :], ALU.mult)
                dve_j.done(dve, 'ba', j)
                tt('bh', bh[:, :], tmp[:, :], e2[:, :], ALU.mult)
                for u in range(NU):
                    pe_j.done(dve, ('A', u), j)
                    if u == 0:
                        dve_j.done(dve, 'bh', j)
                    tt(('A', u), AT[:, u, :, :], bank[4 + u % 4][0:TP, 0:4 * TP].rearrange("p (m t) -> p m t", m=4), mask4[:, :, :],
                       ALU.mult)
                for l in range(LEVELS):
                    for s in range(NB + 1):
                        if s < NB:
                            pe_j.done(dve, ('P', l, s), j)
                            tt(('P', l, s), P1[:, s % 2, :, :], bank[2 + s % 2][0:TP, 0:4 * TP].rearrange("p (m t) -> p m t", m=4),
                               mlev[:, l, 0:TP].unsqueeze(1).to_broadcast([TP, 4, TP]), ALU.mult)
                        if s > 0:
                            b = s - 1
                            pe_j.done(dve, ('D', l, b), j)
                            if l > 0:
                                dve_j.done(dve, ('R', l - 1, b), j)
                            else:
                                pool_j.done(dve, 'R0', j)
                            for x, m, bk in (('T', Tm, 4), ('R', Rm, 6)):
                                tt((x, l, b), m[:, 4 * b:4 * b + 4, :], bank[bk + b % 2][0:TP, 0:4 * TP].rearrange(
                                    "p (m t) -> p m t", m=4), m[:, 4 * b:4 * b + 4, :], ALU.add)
                for g in range(2):
                    pe_j.done(dve, ('m', g), j)
                    tt(('m', g), mxt[:, 5 * g:5 * g + 5, :], bank[2 + g][:, 0:5 * HS].rearrange("p (c n) -> p c n", n=HS),
                       id2.unsqueeze(1).to_broadcast([128, 5, HS]), ALU.add)
                for g in range(2):
                    pe_j.done(dve, ('nn', g), j)
                    tt(('nn', g), np_[:, 5 * g:5 * g + 5, :], bank[4 + g][:, 0:5 * HS].rearrange("p (c n) -> p c n", n=HS),
                       pc[:, 5 * g:5 * g + 5].unsqueeze(2).to_broadcast([128, 5, HS]), ALU.mult)
                dve_j.mark(nc.vector.memset(S[:, 0, :], 0.0), 'S0')
                dve_j.done(dve, ('nn', 0), j)
                dve_j.mark(nc.vector.tensor_copy(S[:, 1, :], np_[:, 0, :]), ('S', 0))
                for c in range(1, NT):
                    pe_j.done(dve, ('s', c), j)
                    if c == 5:
                        dve_j.done(dve, ('nn', 1), j)
                    stt(('S', c), S[:, c + 1, :], bank[6 + c % 2][:, 0:HS], pc[:, c:c + 1], np_[:, c, :], ALU.mult, ALU.add)
                for g in range(2):
                    pe_j.done(dve, ('u', g), j)
                    for h in range(2):
                        tt(('u', g, h), U.rearrange("p (c h) n -> p c h n", h=2)[:, 5 * g:5 * g + 5, h, :],
                           bank[2 + 2 * g + h][0:TP, 0:5 * HS].rearrange("p (c n) -> p c n", n=HS),
                           X.rearrange("p (c h) n -> p c h n", h=2)[:, 5 * g:5 * g + 5, h, HS:128], ALU.add)
                for c in range(NCH):
                    pe_j.done(dve, ('bs', c), j)
                    tt(('bo', c), kk[:, CH * c:CH * (c + 1)], bank[2 + c][:, 0:CH], v_t[:, CH * c:CH * (c + 1)], ALU.mult)
                for c in range(NCH):
                    pe_j.done(dve, ('mean', c), j)
                    stt(('yc', c), y_t[:, CH * c:CH * (c + 1)], bank[2 + c][:, 0:CH], -1.0 / HS, y_t[:, CH * c:CH * (c + 1)],
                        ALU.mult, ALU.add)
                act_j.done(dve, ('var', NCH - 1), j)
                dve_j.mark(nc.vector.reciprocal(nrm[:, :], nrm[:, :]), 'yrec')
                dve_j.done(dve, 'yrec', j)
                tt('yn', y_t[:, :], y_t[:, :], nrm[:, :], ALU.mult)
                dve_j.done(dve, 'yn', j)
                dve_j.mark(nc.vector.tensor_scalar(y_t[:, :], y_t[:, :], pj('lnx_g'), pj('lnx_b'), ALU.mult, ALU.add), 'yaff')
                dve_j.done(dve, 'yaff', j)
                tt('ysum', y_t[:, :], y_t[:, :], kk[:, :], ALU.add)
                dve_j.done(dve, 'ysum', j)
                for c in range(NCH):
                    pe_j.done(dve, ('g', c), j)
                    tt(('yg', c), yg[:, bass.ds(j, 1), CH * c:CH * (c + 1)].rearrange("p a t -> p (a t)"),
                       bank[(0, 1, 6, 7)[c]][:, 0:CH], y_t[:, CH * c:CH * (c + 1)], ALU.mult)
                nc.vector.memset(dz[:, 0:1], 0.0).then_inc(col_free, 1)
            nc.vector.memset(cpb[:, :, 0:2], 0.0).then_inc(conv_step, 2)
            nc.vector.memset(dz[:, 1:2], 0.0).then_inc(conv_step, 4)
            with dve.Fori(0, NJ) as j:
                dve.wait_ge(conv_ev, j * 12 + 12)
                nc.vector.tensor_tensor(cpb[:, 1, 2:], cpb[:, 1, 2:], cpb[:, 2, 2:], ALU.mult).then_inc(conv_step, 1)
                dve.wait_ge(conv_step, j * 6 + 7)
                for w in range(3):
                    scal = vec[:, VEC['conv_w'] + 4 * w:VEC['conv_w'] + 4 * w + 4][:, bass.ds(j, 1)]
                    if w == 0:
                        ins = nc.vector.tensor_scalar(c1[:, :], cpb[:, 1, 0:TOK], scal, None, ALU.mult)
                    else:
                        ins = nc.vector.scalar_tensor_tensor(out=c1[:, :], in0=cpb[:, 1, w:w + TOK], scalar=scal, in1=c1[:, :],
                                                             op0=ALU.mult, op1=ALU.add)
                    ins.then_inc(conv_step, 1)
                    dve.wait_ge(conv_step, j * 6 + 8 + w)
                nc.vector.tensor_tensor(cv[:, bass.ds(j, 1), :].rearrange("p a t -> p (a t)"), cpb[:, 0, 2:], c1[:, :], ALU.mult
                                        ).then_inc(conv_step, 2)
            nc.vector.memset(dz[:, 2:3], 0.0).then_inc(gate_mul, 6)
            with dve.Fori(0, KT) as d:
                for c in range(NCH):
                    s = c % 2
                    dve.wait_ge(gate_sig, d * 8 + 2 * c + 2)
                    for m in range(2):
                        nc.vector.tensor_tensor(gt[:, s, m, :], gt[:, s, m, :], bank[4 * s + 2 + m][:, 0:CH], ALU.mult
                                                ).then_inc(gate_mul, 1)
                    dve.wait_ge(gate_mul, d * 12 + 3 * c + 8)
                    nc.vector.tensor_tensor(mT[:, bass.ds(d, 1), CH * c:CH * (c + 1)].rearrange("p a t -> p (a t)"),
                                            gt[:, s, 0, :], gt[:, s, 1, :], ALU.add).then_inc(gate_mul, 1)
            dve.wait_ge(h_in, 16 * (NT + 1))
            for t in range(NT):
                for n in range(2):
                    dve.wait_ge(wo_ps, 2 * t + n + 1)
                    nc.vector.tensor_tensor(h_all[:, t, 512 * n:512 * (n + 1)], bank[2 * (t % 2) + n][0:TP, :],
                                            h_all[:, t, 512 * n:512 * (n + 1)], ALU.add).then_inc(wo_add, 1)

        def on_tensor(pe):
            pe.wait_ge(pool_c, 2)
            pe.wait_ge(vec_in, 16 * 15)
            nc.tensor.transpose(bank[7][:, 0:84], vrows[:, :], ident[0:84, 0:84]).then_inc(vec_ps, 1)
            for t in range(NT):
                pe.wait_ge(xn_done, t + 1)
                if t >= 2:
                    pe.wait_ge(xnT_done, 2 * (t - 1))
                for k in range(KT):
                    ins = nc.tensor.transpose(bank[2 * (t % 2) + k // 4][:, (k % 4) * TP:(k % 4 + 1) * TP],
                                              xn[:, t % 2, 128 * k:128 * (k + 1)], ident[0:TP, 0:TP])
                ins.then_inc(xnT_ps, 1)
            pe.wait_ge(xnT_done, 2 * NT)
            pe.wait_ge(lmu_done, 3)
            for m in range(2):
                for c in range(NCH):
                    if 4 * m + c >= 2:
                        pe.wait_ge(lora_ev, 2 * (4 * m + c) - 2)
                    for w, b in ((lraw, 0), (lmu, 2)):
                        for k in range(KT):
                            ins = nc.tensor.matmul(bank[b + c % 2][:, 0:CH], w[:, k, 128 * m:128 * (m + 1)],
                                                   xnT[:, k, CH * c:CH * (c + 1)], start=k == 0, stop=k == KT - 1)
                    ins.then_inc(lora_ps, 1)
            pe.wait_ge(lora_done, 3)

            def mm(ps, lhsT, rhs, start=True, stop=True):
                return nc.tensor.matmul(ps, lhsT, rhs, start=start, stop=stop)

            def hp(h):
                return slice(HS * h, HS * (h + 1))

            def tp(c):
                return slice(TP * c, TP * (c + 1))

            with pe.Fori(0, NJ) as j:
                pool_j.done(pe, 'wg2', j)
                pe.wait_ge(col_free, j + 1)
                for c in range(NCH):
                    if c >= 2:
                        act_j.done(pe, ('a', c - 2), j)
                    mm(bank[2 + c % 2][:, 0:CH], w2j[0:64, :], lw[0:64, CH * c:CH * (c + 1)])
                    pe_j.mark(mm(bank[4 + c % 2][:, 0:CH], w2j[64:128, :], lw[64:128, CH * c:CH * (c + 1)]), ('z', c))
                for i in range(3):
                    pe.wait_ge(ring_in[i], j * 16 + 16)
                    for c in range(NCH):
                        if 4 * i + c >= 2:
                            q = 4 * i + c - 2
                            act_j.done(pe, ('p', q // 4, q % 4), j)
                        for k in range(KT):
                            ins = mm(bank[c % 2][:, 0:CH], ring[:, i, k, :], xnT[:, k, CH * c:CH * (c + 1)], k == 0, k == KT - 1)
                        pe_j.mark(ins, ('p', i, c))
                act_j.done(pe, 'sq', j)
                for c in range(NCH):
                    pe_j.mark(mm(bank[4 + c][:, 0:CH], bones[:, :], nrm[:, CH * c:CH * (c + 1)]), ('n', c))
                dve_j.done(pe, 'bh', j)
                q = 0
                for x in TA:
                    for g, (g0, g1) in enumerate(evac_groups()):
                        if q >= 2:
                            act_j.done(pe, ('t', TA[(q - 2) // 3], (q - 2) % 3), j)
                        for c in range(g0, g1):
                            src = dict(v=v_t, b=bh, k=kh)[x][:, tp(c)] if x != 'a' else ar[:, c, 0, :]
                            ins = nc.tensor.transpose(bank[2 + q % 2][0:TP, 128 * (c - g0):128 * (c - g0 + 1)], src, ident[:, :])
                        pe_j.mark(ins, ('t', x, g))
                        q += 1
                for u in range(NU):
                    c, h = u // 2, u % 2
                    if u >= 4:
                        dve_j.done(pe, ('A', u - 4), j)
                    b = bank[4 + u % 4]
                    mm(b[0:TP, 0:2 * TP], bh[hp(h), tp(c)], ar[hp(h), c, :, :].rearrange("p m t -> p (m t)"))
                    pe_j.mark(mm(b[0:TP, 2 * TP:4 * TP], kh[hp(h), tp(c)], ar[hp(h), c, :, :].rearrange("p m t -> p (m t)")),
                              ('A', u))
                dve_j.done(pe, ('A', NU - 1), j)
                act_j.done(pe, ('t', 'a', 2), j)
                pool_j.done(pe, 'R0', j)
                for l in range(LEVELS):
                    for s in range(NB + 1):
                        if s < NB:
                            if l > 0:
                                dve_j.done(pe, ('T', l - 1, s), j)
                                if s < 2:
                                    dve_j.done(pe, ('P', l - 1, 4 - s), j)
                            if s >= 2:
                                dve_j.done(pe, ('P', l, s - 2), j)
                            for m in range(4):
                                u = 4 * s + m
                                ins = mm(bank[2 + s % 2][0:TP, TP * m:TP * (m + 1)], AT[:, u, 0, :], Tm[:, u, :])
                            pe_j.mark(ins, ('P', l, s))
                        if s > 0:
                            b = s - 1
                            dve_j.done(pe, ('P', l, b), j)
                            if b >= 2:
                                dve_j.done(pe, ('R', l, b - 2), j)
                            elif l > 0:
                                dve_j.done(pe, ('R', l - 1, 4 - b), j)
                            for m in range(4):
                                u = 4 * b + m
                                mm(bank[4 + b % 2][0:TP, TP * m:TP * (m + 1)], Rm[:, u, :], P1[:, b % 2, m, :])
                                ins = mm(bank[6 + b % 2][0:TP, TP * m:TP * (m + 1)], P1[:, b % 2, m, :], Rm[:, u, :])
                            pe_j.mark(ins, ('D', l, b))
                dve_j.done(pe, ('R', LEVELS - 1, NB - 1), j)
                for g, (g0, g1) in enumerate(((0, 8), (8, 16), (16, 20))):
                    if g == 2:
                        act_j.done(pe, ('xa', 0), j)
                    for u in range(g0, g1):
                        ins = mm(bank[2 + g % 2][0:TP, HS * (u - g0):HS * (u - g0 + 1)], AT[:, u, 2, :], Vt[:, u // 2, hp(u % 2)])
                    pe_j.mark(ins, ('xa', g))
                for g, (g0, g1) in enumerate(evac_groups()):
                    if g == 2:
                        act_j.done(pe, ('xc', 0), j)
                    for c in range(g0, g1):
                        for h in range(2):
                            ins = mm(bank[4 + g % 2][hp(h), TP * (c - g0):TP * (c - g0 + 1)], X[:, 2 * c + h, 0:HS],
                                     Rm[:, 2 * c + h, :])
                    pe_j.mark(ins, ('xc', g))
                act_j.done(pe, ('xa', 2), j)
                for g in range(5):
                    if g >= 2:
                        act_j.done(pe, ('xb', g - 2), j)
                    for m in range(4):
                        u = 4 * g + m
                        ins = mm(bank[6 + g % 2][0:TP, 128 * m:128 * (m + 1)], Rm[:, u, :], X[:, u, :])
                    pe_j.mark(ins, ('xb', g))
                act_j.done(pe, ('xb', 4), j)
                for g in range(2):
                    for c in range(5 * g, 5 * g + 5):
                        for h in range(2):
                            ins = mm(bank[2 + g][hp(h), HS * (c % 5):HS * (c % 5 + 1)], X[:, 2 * c + h, 0:HS], Bt[:, c, hp(h)])
                    pe_j.mark(ins, ('m', g))
                for g in range(2):
                    for c in range(5 * g, 5 * g + 5):
                        for h in range(2):
                            o = bank[4 + g][hp(h), HS * (c % 5):HS * (c % 5 + 1)]
                            mm(o, Bt[:, c, hp(h)], X[:, 2 * c + h, HS:128], True, False)
                            ins = mm(o, Kt[:, c, hp(h)], Vt[:, c, hp(h)], False, True)
                    pe_j.mark(ins, ('nn', g))
                dve_j.done(pe, ('m', 1), j)
                for c in range(1, NT):
                    dve_j.done(pe, ('S', c - 1), j, pe_passed)
                    for h in range(2):
                        ins = mm(bank[6 + c % 2][hp(h), 0:HS], mxt[hp(h), c, :], S[hp(h), c, :])
                    pe_j.mark(ins, ('s', c))
                dve_j.done(pe, ('nn', 1), j)
                for g in range(2):
                    for c in range(5 * g, 5 * g + 5):
                        for h in range(2):
                            ins = mm(bank[2 + 2 * g + h][0:TP, HS * (c % 5):HS * (c % 5 + 1)], x1t[hp(h), c, :], S[hp(h), c, :])
                    pe_j.mark(ins, ('u', g))
                dve_j.done(pe, ('u', 1, 1), j, pe_passed)
                for g, (g0, g1) in enumerate(evac_groups()):
                    if g == 2:
                        act_j.done(pe, ('y', 0), j, pe_passed)
                    for c in range(g0, g1):
                        for h in range(2):
                            u = 2 * c + h
                            o = bank[6 + g % 2][hp(h), TP * (c - g0):TP * (c - g0 + 1)]
                            mm(o, S[hp(h), c, :], ar[hp(h), c, 1, :], True, False)
                            mm(o, U[:, u, :], AT[:, u, 1, :], False, False)
                            ins = mm(o, Vt[:, c, hp(h)], AT[:, u, 3, :], False, True)
                    pe_j.mark(ins, ('y', g))
                for c in range(NCH):
                    pe_j.mark(mm(bank[2 + c][:, 0:CH], bones[:, :], rkb[:, CH * c:CH * (c + 1)]), ('bs', c))
                act_j.done(pe, ('y', 2), j)
                for c in range(NCH):
                    pe_j.mark(mm(bank[(0, 1, 6, 7)[c]][:, 0:CH], wg2j[:, :], lg[:, CH * c:CH * (c + 1)]), ('g', c))
                for c in range(NCH):
                    dve_j.done(pe, ('bo', c), j)
                    pe_j.mark(mm(bank[2 + c][:, 0:CH], bones[:, :], y_t[:, CH * c:CH * (c + 1)]), ('mean', c))
                act_j.done(pe, 'ysq', j)
                for c in range(NCH):
                    if c >= 2:
                        act_j.done(pe, ('var', c - 2), j)
                    pe_j.mark(mm(bank[4 + c % 2][:, 0:CH], bones[:, :], tmp[:, CH * c:CH * (c + 1)]), ('var', c))
            pe.wait_ge(col_free, NJ + 1)
            with pe.Fori(0, NJ) as j:
                for i in range(3):
                    pe.wait_ge(ring_in[i], j * 16 + 16 + 16 * NJ)
                    for c in range(NCH):
                        if 4 * i + c >= 2:
                            pe.wait_ge(conv_ev, j * 12 + 4 * i + c - 1)
                        for k in range(KT):
                            ins = mm(bank[c % 2][:, 0:CH], ring[:, i, k, :], xnT[:, k, CH * c:CH * (c + 1)], k == 0, k == KT - 1)
                        ins.then_inc(conv_ps, 1)
                pe.wait_ge(conv_ev, j * 12 + 12)
            pe.wait_ge(conv_step, 6 * NJ + 6)
            with pe.Fori(0, KT) as d:
                for i in range(2):
                    pe.wait_ge(ring_in[i], d * 16 + 16 + 32 * NJ)
                pe.wait_ge(ring_in[2], d * 32 + 32 + 32 * NJ)
                for c in range(NCH):
                    b = 4 * (c % 2)
                    pe.wait_ge(gate_mul, d * 12 + 3 * c + 3)
                    t = slice(CH * c, CH * (c + 1))
                    for i in range(2):
                        for k in range(KT):
                            mm(bank[b + i][:, 0:CH], ring[:, i, k, :], xnT[:, k, t], k == 0, k == KT - 1)
                    for i, src in enumerate((yg, cv)):
                        for k in range(4):
                            ins = mm(bank[b + 2 + i][:, 0:CH], ring[:, 2, 4 * i + k, :], src[:, k, t], k == 0, k == 3)
                    ins.then_inc(gate_ps, 1)
            pe.wait_ge(gate_mul, 12 * KT + 6)
            pe.wait_ge(wo_in, 16)
            for t in range(NT):
                for n in range(2):
                    if t >= 2:
                        pe.wait_ge(wo_add, 2 * (t - 2) + n + 1)
                    for k in range(KT):
                        ins = mm(bank[2 * (t % 2) + n][0:TP, :], mT[:, k, tp(t)], wo_t[:, k, 512 * n:512 * (n + 1)], k == 0, k == KT - 1)
                    ins.then_inc(wo_ps, 1)



    return on_sync, on_gpsimd, on_scalar, on_vector, on_tensor


def experts_program(nc, ctx, a, bank, shared, out):
    f32 = mybir.dt.float32
    f32r = mybir.dt.float32r
    u32 = mybir.dt.uint32
    ALU = mybir.AluOpType
    ACT = mybir.ActivationFunctionType
    AX = mybir.AxisListType

    D = 1024
    META = 16
    TOK = 1040
    NT = 10
    TP = TOK // NT
    KT = D // 128
    E = 32
    TOPK = 4
    LIMIT = 7.0
    ALPHA = 1.702
    EPS = 1e-5
    SLOTS = 192
    HALF = SLOTS // 2
    MAXR = E + TOK * TOPK // SLOTS + 1
    MINR = TOK * TOPK // SLOTS
    PC = 256
    NPIECE = 3 * D // PC
    NRAW = 6
    NSPLIT = 4

    if True:
        ident, eps_t, h_all, zero_out, wo_add = shared['ident'], shared['eps_t'], shared['h_all'], shared['zero_out'], shared['wo_add']
        ln2_g, w_router, b_router, lnf_g = a['ln2_g'], a['w_router'], a['b_router'], a['lnf_g']
        w_gate, b_gate, w_up, b_up, w_down, b_down = (a[x] for x in ('w_e_gate', 'b_e_gate', 'w_e_up', 'b_e_up', 'w_e_down', 'b_e_down'))
        hn_d, ys_d, rowtok_d = shared['hn_d'], shared['ys_d'], shared['rowtok_all']

        def sem(name):
            return ctx.enter_context(nc.semaphore(name))


        gate_ps, up_ps, y_ps, tx_ps, ty_ps = bank[0:2], bank[2:4], bank[4:6], bank[6], bank[7]

        sb = Plan(nc, shared['after_h'])
        bias_all = sb("bias_all", [128, E, 3 * KT])
        gates, dest = shared["gates"], shared["dest"]
        tok_id = sb("tok_id", [TP, NT], u32)
        table = sb("table", [1, MAXR + 2], u32)
        fss = sb("fss", [TP, NT])
        frs = sb("frs", [TP, NT])

        dump = sb("dump_e", [128, 8])

        if True:
            rt = Plan(nc, sb.at)
            hn = rt("hn", [TP, 2, D])
            junk = rt("junk_e", [TP, D])
            g2_b = rt("g2_b", [TP, D])
            bias_rows = rt("bias_rows", [E, 3, D])
            wr_t = rt("wr_t", [128, KT, E])
            hnT = rt("hnT", [128, 2, KT, TP])
            ss = rt("ss_e", [TP, NT])
            rstd = rt("rstd_e", [TP, NT])
            top_v = rt("top_v", [TP, NT, 8])
            top_i = rt("top_i", [TP, NT, 8], u32)
            lg = rt("lg", [TP, 2, E])
            br_b = rt("br_b", [TP, E])
            iota_e = rt("iota_e", [TP, E])
            onehot = rt("onehot", [TP, NT * TOPK, E])
            chosen = rt("chosen", [TP, NT, E])
            before = rt("before", [TP, NT + 1, E])
            rank = rt("rank", [TP, NT, E])
            tri = rt("tri", [TP, TP])
            ones = rt("ones", [TP, 128])
            top_f = rt("top_f", [TP, NT * TOPK])
            cnt = rt("cnt", [TP, E])
            over = rt("over", [TP, E])
            nr = rt("nr", [TP, E])
            rend = rt("rend", [TP, E])
            rbase = rt("rbase", [TP, E])
            dest_f = rt("dest_f", [TP, NT * TOPK])
            gsum = rt("gsum", [TP, NT])
            iota_q = rt("iota_q", [1, MAXR + 1])
            ended = rt("ended", [1, MAXR + 1, E])
            table_f = rt("table_f", [1, MAXR + 1])

        if True:
            ex = Plan(nc, sb.at)
            raw = ex("raw", [128, NRAW, KT, PC])
            w_hi = ex("w_hi", [128, NSPLIT, KT, PC], f32r)
            w_lo = ex("w_lo", [128, NSPLIT, KT, PC], f32r)
            x_rows = ex("x_rows", [HALF, 2, D])
            x_hi = ex("x_hi", [128, KT, SLOTS], f32r)
            x_lo = ex("x_lo", [128, KT, SLOTS], f32r)
            g_t = ex("g_t", [128, 2 * SLOTS])
            s_t = ex("s_t", [128, 2 * SLOTS])
            u_t = ex("u_t", [128, 2 * SLOTS])
            a_t = ex("a_t", [128, 2 * SLOTS])
            a_hi = ex("a_hi", [128, KT, SLOTS], f32r)
            a_lo = ex("a_lo", [128, KT, SLOTS], f32r)
            y_T = ex("y_T", [128, 2, 2, SLOTS])
            y_rows = ex("y_rows", [HALF, 2, D])
            bias_gu = ex("bias_gu", [128, 2 * KT])
            bias_dn = ex("bias_dn", [128, KT])
            idx_t = ex("idx_t", [HALF, 2], u32)

        if True:
            fi = Plan(nc, sb.at)
            y_got = fi("y_got", [TP, 2, TOPK, D])
            fin_junk = fi("fin_junk", [TP, D])
            gf_b = fi("gf_b", [TP, D])
            fin = fi("fin", [TP, 2, D])

        const_in = sem("const_in")
        bias_in = sem("bias_in")
        pool_const = sem("pool_const")
        dve_const = sem("dve_const")
        sq_done = sem("sq_done")
        std_done = sem("std_done")
        rstd_done = sem("rstd_done")
        hn_done = sem("hn_done")
        hn_out = [sem("hn_out0"), sem("hn_out1")]
        hnT_ps = sem("hnT_ps")
        hnT_done = sem("hnT_done")
        logit_ps = sem("logit_ps")
        lg_read = sem("lg_read")
        top_done = sem("top_done")
        route = sem("route")
        gexp_in = sem("gexp_in")
        gexp_done = sem("gexp_done")
        chosen_done = sem("chosen_done")
        rank_ps = sem("rank_ps")
        dest_done = sem("dest_done")
        table_done = sem("table_done")
        scattered = sem("scattered")
        biasT_ps = sem("biasT_ps")
        biasT_done = sem("biasT_done")

        raw_in = [sem(f"raw_in{s}") for s in range(NRAW)]
        hi_done = sem("hi_done")
        lo_done = sem("lo_done")
        piece_used = sem("piece_used")
        bias_gu_done = sem("bias_gu_done")
        bias_dn_done = sem("bias_dn_done")
        gt_read = sem("gt_read")
        sig_done = sem("sig_done")
        up_read = sem("up_read")
        glu = sem("glu")
        ahi_done = sem("ahi_done")
        alo_done = sem("alo_done")
        sp_passed = sem("sp_passed_e")
        pool_passed = sem("pool_passed_e")
        idx_in = sem("idx_in")
        rows_in = sem("rows_in")
        xT_ps = sem("xT_ps")
        xhi_done = sem("xhi_done")
        xlo_done = sem("xlo_done")
        yT_ps = sem("yT_ps")
        yT_done = sem("yT_done")
        yrow_ps = sem("yrow_ps")
        yrow_done = sem("yrow_done")
        y_out = sem("y_out")

        gf_in = sem("gf_in")
        got_in = [sem("got_in0"), sem("got_in1")]
        sum_done = sem("sum_done")
        fsq_done = sem("fsq_done")
        fstd_done = sem("fstd_done")
        frs_done = sem("frs_done")
        fin_done = sem("fin_done")
        out_done = [sem("out_done0"), sem("out_done1")]


        def kp(w, e_reg, c0, w_):
            return w[bass.ds(e_reg, 1), :, c0:c0 + w_].rearrange("a (k p) c -> p (a k) c", p=128)

        def on_sync(sp):
            sp.wait_ge(wo_add, 2 * NT)
            sp.dma_start(g2_b, ln2_g.partition_broadcast(TP)).then_inc(const_in, 16)
            sp.dma_start(br_b, b_router.partition_broadcast(TP)).then_inc(const_in, 16)
            sp.dma_start(wr_t, w_router.rearrange("(k p) e -> p k e", p=128)).then_inc(const_in, 16)
            for a, b in enumerate((b_gate, b_up, b_down)):
                sp.dma_start(bias_rows[:, a, :], b).then_inc(bias_in, 16)
            for t in range(NT):
                sp.wait_ge(hn_done, t + 1)
                sp.dma_start(hn_d[TP * t:TP * (t + 1), :], hn[:, t % 2, :]).then_inc(hn_out[t % 2], 16)
            sp.wait_ge(table_done, 1)
            rounds = sp.value_load(table[0:1, MAXR + 1:MAXR + 2], min_val=1, max_val=MAXR - 1)
            sp.wait_ge(hn_out[0], 16 * (NT // 2))
            sp.wait_ge(hn_out[1], 16 * (NT // 2))

            def load(e_reg, n, j):
                w = (w_gate, w_up)[j % 2] if j < 8 else w_down
                c = j // 2 if j < 8 else j - 8
                sp.wait_ge(lo_done, n + 1)
                sp.sem_inc(sp_passed, 1)
                sp.dma_start(raw[:, j % NRAW, :, :], kp(w, e_reg, c * PC, PC)).then_inc(raw_in[j % NRAW], 16)

            e0 = sp.value_load(table[0:1, 0:1], min_val=0, max_val=E - 1)
            for j in range(NSPLIT):
                load(e0, j, j)
            with sp.Fori(0, rounds) as q:
                e = sp.value_load(table[0:1, bass.ds(q, 1)], min_val=0, max_val=E - 1)
                e_next = sp.value_load(table[0:1, bass.ds(q + 1, 1)], min_val=0, max_val=E - 1)
                for j in range(NPIECE):
                    if j + NSPLIT < NPIECE:
                        load(e, q * NPIECE + j + NSPLIT, j + NSPLIT)
                    else:
                        load(e_next, q * NPIECE + j + NSPLIT, j + NSPLIT - NPIECE)
            sp.wait_ge(piece_used, rounds * NPIECE + NSPLIT)
            sp.dma_start(gf_b, lnf_g.partition_broadcast(TP)).then_inc(gf_in, 16)
            for t in range(NT):
                sp.wait_ge(fin_done, t + 1)
                if t == 0:
                    sp.dma_start(out[0:TP - META, :], fin[META:TP, 0, :]).then_inc(out_done[0], 16)
                else:
                    sp.dma_start(out[TP * t - META:TP * (t + 1) - META, :], fin[:, t % 2, :]).then_inc(out_done[t % 2], 16)
            sp.wait_ge(out_done[0], 16 * (NT // 2))
            sp.wait_ge(out_done[1], 16 * (NT // 2))

        def on_gpsimd(pool):
            pool.wait_ge(wo_add, 2 * NT)
            nc.gpsimd.memset(tri, 1.0).then_inc(pool_const, 1)
            pool.wait_ge(pool_const, 1)
            nc.gpsimd.affine_select(out=tri, in_=tri, compare_op=ALU.is_gt, fill=0.0, base=0,
                                    pattern=[[1, TP]], channel_multiplier=-1).then_inc(pool_const, 1)
            nc.gpsimd.iota(tok_id[:, :], pattern=[[TP, NT]], base=0, channel_multiplier=1).then_inc(pool_const, 1)
            nc.gpsimd.iota(iota_e, pattern=[[1, E]], base=0, channel_multiplier=0,
                           allow_small_or_imprecise_dtypes=True).then_inc(pool_const, 1)
            nc.gpsimd.iota(iota_q, pattern=[[1, MAXR + 1]], base=0, channel_multiplier=0,
                           allow_small_or_imprecise_dtypes=True).then_inc(pool_const, 1)
            pool.wait_ge(zero_out, 16 * (MAXR - MINR + 1))
            pool.wait_ge(dest_done, 1)
            pool.wait_ge(pool_const, 5)
            for t in range(NT):
                for k in range(TOPK):
                    a = t * TOPK + k
                    nc.gpsimd.indirect_dma_start(out=rowtok_d, out_offset=bass.IndirectOffsetOnAxis(ap=dest[:, a:a + 1], axis=0),
                                                 in_=tok_id[:, t:t + 1], in_offset=None).then_inc(scattered, 16)
            pool.wait_ge(table_done, 1)
            rounds = pool.value_load(table[0:1, MAXR + 1:MAXR + 2], min_val=1, max_val=MAXR - 1)
            pool.wait_ge(scattered, 16 * NT * TOPK)
            pool.wait_ge(hn_out[0], 16 * (NT // 2))
            pool.wait_ge(hn_out[1], 16 * (NT // 2))

            def gather(q_next):
                pool.dma_start(idx_t[:, :], rowtok_d[bass.ds(q_next * SLOTS, SLOTS), :].rearrange("(p b) a -> p (b a)", b=2)
                               ).then_inc(idx_in, 16)
                pool.wait_ge(idx_in, q_next * 16 + 16)
                pool.sem_inc(pool_passed, 1)
                for b in range(2):
                    nc.gpsimd.indirect_dma_start(out=x_rows[:, b, :], out_offset=None, in_=hn_d,
                                                 in_offset=bass.IndirectOffsetOnAxis(ap=idx_t[:, b:b + 1], axis=0)
                                                 ).then_inc(rows_in, 16)

            gather(0)
            with pool.Fori(0, rounds) as q:
                pool.wait_ge(xT_ps, q * 4 + 4)
                pool.wait_ge(rows_in, q * 32 + 32)
                gather(q + 1)
            pool.wait_ge(y_out, rounds * 16 + 16)
            pool.wait_ge(lo_done, rounds * NPIECE + NSPLIT + NRAW)
            pool.sem_inc(pool_passed, 1)
            for t in range(NT):
                if t >= 2:
                    pool.wait_ge(sum_done, TOPK * (t - 1))
                for k in range(TOPK):
                    a = t * TOPK + k
                    nc.gpsimd.indirect_dma_start(out=y_got[:, t % 2, k, :], out_offset=None, in_=ys_d,
                                                 in_offset=bass.IndirectOffsetOnAxis(ap=dest[:, a:a + 1], axis=0)
                                                 ).then_inc(got_in[t % 2], 16)

        def on_scalar(act):
            for t in range(NT):
                act.wait_ge(wo_add, 2 * NT)
                if t >= 1:
                    act.wait_ge(sq_done, t)
                nc.scalar.activation(junk, h_all[:, t, :], ACT.Square, accum_out=ss[:, t:t + 1]).then_inc(sq_done, 1)
            act.wait_ge(sq_done, NT)
            nc.scalar.activation(rstd[:, :], ss[:, :], ACT.Sqrt, bias=eps_t[0:TP, :], scale=1.0 / D).then_inc(std_done, 1)
            act.wait_ge(biasT_ps, 2)
            for h in range(2):
                nc.scalar.activation(bias_all[:, :, 12 * h:12 * h + 12].rearrange("p e a -> p a e"),
                                     bank[h][:, 0:12 * E].rearrange("p (a e) -> p a e", e=E), ACT.Copy).then_inc(biasT_done, 1)
            for t in range(NT):
                act.wait_ge(hnT_ps, t + 1)
                if t >= 2:
                    act.wait_ge(logit_ps, t - 1)
                for h in range(2):
                    nc.scalar.activation(hnT[:, t % 2, 4 * h:4 * h + 4, :],
                                         bank[2 + 2 * (t % 2) + h][:, 0:4 * TP].rearrange("p (k t) -> p k t", k=4),
                                         ACT.Copy).then_inc(hnT_done, 1)
            act.wait_ge(gexp_in, 1)
            nc.scalar.activation(gates[:, :, :], gates[:, :, :], ACT.Exp).then_inc(gexp_done, 1)

            act.wait_ge(table_done, 1)
            rounds = act.value_load(table[0:1, MAXR + 1:MAXR + 2], min_val=1, max_val=MAXR - 1)

            def split_hi(n, use, j):
                act.wait_ge(raw_in[j % NRAW], use)
                act.wait_ge(piece_used, n + 1)
                nc.scalar.activation(w_hi[:, j % NSPLIT, :, :], raw[:, j % NRAW, :, :], ACT.Copy).then_inc(hi_done, 1)

            def x_hi_part(n, t):
                act.wait_ge(xT_ps, n + 1)
                nc.scalar.activation(x_hi[:, 2 * t:2 * t + 2, :], tx_ps[:, 0:2 * SLOTS].rearrange("p (k s) -> p k s", k=2),
                                     ACT.Copy).then_inc(xhi_done, 1)

            def y_evac(n, c):
                act.wait_ge(yrow_ps, n + 1)
                nc.scalar.activation(y_rows[:, :, c * PC:(c + 1) * PC], ty_ps[0:HALF, :].rearrange("p (b c) -> p b c", b=2),
                                     ACT.Copy).then_inc(yrow_done, 1)

            for t in range(4):
                x_hi_part(t, t)
            for j in range(NSPLIT):
                split_hi(j, 16, j)
            with act.Fori(0, rounds) as q:
                e = act.value_load(table[0:1, bass.ds(q, 1)], min_val=0, max_val=E - 1)
                for j in range(NPIECE):
                    jn = j + NSPLIT
                    n = q * NPIECE + jn
                    use = q * 32 + 16 * (jn // NRAW) + 16
                    if j < 8:
                        split_hi(n, use, jn % NPIECE)
                        c = j // 2
                        if j % 2 == 0:
                            act.wait_ge(gt_read, q * 4 + c + 3)
                            nc.scalar.activation(s_t[:, :], g_t[:, :], ACT.Sigmoid, scale=ALPHA).then_inc(sig_done, 1)
                        else:
                            act.wait_ge(glu, q * 12 + 3 * c + 3)
                            nc.scalar.activation(a_hi[:, 2 * c:2 * c + 2, :], a_t[:, :].rearrange("p (k s) -> p k s", k=2),
                                                 ACT.Copy).then_inc(ahi_done, 1)
                    else:
                        c = j - 8
                        if c == 0:
                            nc.scalar.activation(bias_dn[:, :], bias_all[:, bass.ds(e, 1), 2 * KT:3 * KT].rearrange("p a k -> p (a k)"),
                                                 ACT.Copy).then_inc(bias_dn_done, 1)
                        x_hi_part(q * 4 + 4 + c, c)
                        for d in range(2):
                            if d == 0:
                                act.wait_ge(yT_ps, q * 4 + c + 1)
                            else:
                                split_hi(n, use, jn % NPIECE)
                            if c == 0:
                                act.wait_ge(bias_dn_done, q + 1)
                            nc.scalar.activation(y_T[:, c % 2, d, :], y_ps[d][:, 0:SLOTS], ACT.Identity,
                                                 bias=bias_dn[:, 2 * c + d:2 * c + d + 1]).then_inc(yT_done, 1)
                        if c == 1:
                            act.wait_ge(y_out, q * 16 + 16)
                        if c >= 1:
                            y_evac(q * 4 + c - 1, c - 1)
                        if c == 3:
                            y_evac(q * 4 + 3, 3)
                            act.wait_ge(yrow_done, q * 4 + 5)
                            act.dma_start(ys_d[bass.ds(q * SLOTS, SLOTS), :].rearrange("(p b) d -> p (b d)", b=2),
                                          y_rows[:, :, :].rearrange("p b d -> p (b d)")).then_inc(y_out, 16)
            for t in range(NT):
                act.wait_ge(sum_done, TOPK * (t + 1))
                if t >= 1:
                    act.wait_ge(fsq_done, t)
                nc.scalar.activation(fin_junk, h_all[:, t, :], ACT.Square, accum_out=fss[:, t:t + 1]).then_inc(fsq_done, 1)
                act.wait_ge(fsq_done, t + 1)
                nc.scalar.activation(frs[:, t:t + 1], fss[:, t:t + 1], ACT.Sqrt, bias=eps_t[0:TP, :], scale=1.0 / D
                                     ).then_inc(fstd_done, 1)

        def on_vector(dve):
            steps = [0]

            def link(ins):
                steps[0] += 1
                ins.then_inc(route, 1)
                dve.wait_ge(route, steps[0])

            dve.wait_ge(wo_add, 2 * NT)
            nc.vector.memset(ones, 1.0).then_inc(dve_const, 1)
            for i, (s, n) in enumerate(((lo_done, NRAW), (piece_used, NSPLIT), (gt_read, 2), (up_read, 2), (yT_done, 2),
                                        (yrow_done, 1), (y_out, 16))):
                nc.vector.memset(dump[:, i:i + 1], 0.0).then_inc(s, n)
            dve.wait_ge(std_done, 1)
            nc.vector.reciprocal(rstd[:, :], rstd[:, :]).then_inc(rstd_done, 1)
            dve.wait_ge(rstd_done, 1)
            dve.wait_ge(const_in, 48)
            for t in range(NT):
                if t >= 2:
                    dve.wait_ge(hn_out[t % 2], 16 * (t // 2))
                    dve.wait_ge(hnT_ps, t - 1)
                nc.vector.scalar_tensor_tensor(out=hn[:, t % 2, :], in0=h_all[:, t, :], scalar=rstd[:, t:t + 1], in1=g2_b,
                                               op0=ALU.mult, op1=ALU.mult).then_inc(hn_done, 1)
                if t >= 1:
                    u = t - 1
                    dve.wait_ge(logit_ps, u + 1)
                    nc.vector.tensor_tensor(lg[:, u % 2, :], bank[6 + u % 2][0:TP, 0:E], br_b, ALU.add).then_inc(lg_read, 1)
                    dve.wait_ge(lg_read, u + 1)
                    link(nc.vector.max(top_v[:, u, :], lg[:, u % 2, :]))
                    nc.vector.max_index(top_i[:, u, :], top_v[:, u, :], lg[:, u % 2, :]).then_inc(top_done, 1)
            u = NT - 1
            dve.wait_ge(logit_ps, u + 1)
            nc.vector.tensor_tensor(lg[:, u % 2, :], bank[6 + u % 2][0:TP, 0:E], br_b, ALU.add).then_inc(lg_read, 1)
            dve.wait_ge(lg_read, u + 1)
            link(nc.vector.max(top_v[:, u, :], lg[:, u % 2, :]))
            nc.vector.max_index(top_i[:, u, :], top_v[:, u, :], lg[:, u % 2, :]).then_inc(top_done, 1)
            dve.wait_ge(top_done, NT)
            nc.vector.tensor_tensor(gates[:, :, :], top_v[:, :, 0:TOPK], top_v[:, :, 0:1].to_broadcast([TP, NT, TOPK]),
                                    ALU.subtract).then_inc(gexp_in, 1)
            link(nc.vector.tensor_copy(top_f.rearrange("p (t k) -> p t k", k=TOPK), top_i[:, :, 0:TOPK]))
            dve.wait_ge(pool_const, 5)
            link(nc.vector.tensor_tensor(onehot, iota_e.unsqueeze(1).to_broadcast([TP, NT * TOPK, E]),
                                         top_f.unsqueeze(2).to_broadcast([TP, NT * TOPK, E]), ALU.is_equal))
            link(nc.vector.tensor_reduce(chosen, onehot.rearrange("p (t k) e -> p t e k", k=TOPK), axis=AX.X, op=ALU.add))
            link(nc.vector.memset(before[:, 0, :], 0.0))
            for t in range(NT):
                ins = nc.vector.tensor_tensor(before[:, t + 1, :], before[:, t, :], chosen[:, t, :], ALU.add)
                if t == NT - 1:
                    ins.then_inc(chosen_done, 1)
                else:
                    link(ins)
            dve.wait_ge(gexp_done, 1)
            link(nc.vector.tensor_reduce(gsum, gates[:, :, :], axis=AX.X, op=ALU.add))
            link(nc.vector.reciprocal(gsum, gsum))
            link(nc.vector.tensor_tensor(gates[:, :, :], gates[:, :, :], gsum.unsqueeze(2).to_broadcast([TP, NT, TOPK]),
                                         ALU.mult))
            dve.wait_ge(rank_ps, 2)
            link(nc.vector.tensor_copy(cnt, bank[1][0:TP, 0:E]))
            link(nc.vector.tensor_copy(rank, bank[0][0:TP, 0:NT * E].rearrange("p (t e) -> p t e", e=E)))
            link(nc.vector.tensor_scalar(nr, cnt, 0.0, None, ALU.is_gt))
            for m in range(1, (TOK + SLOTS - 1) // SLOTS):
                link(nc.vector.scalar_tensor_tensor(out=nr, in0=cnt, scalar=float(m * SLOTS), in1=nr, op0=ALU.is_gt, op1=ALU.add))
            link(nc.vector.memset(over, 1.0))
            link(nc.vector.tensor_tensor_scan(rend, over, nr, 0.0, ALU.mult, ALU.add))
            link(nc.vector.tensor_tensor(rbase, rend, nr, ALU.subtract))
            link(nc.vector.tensor_scalar(rbase, rbase, float(SLOTS), None, ALU.mult))
            link(nc.vector.tensor_tensor(rank, rank, rbase.unsqueeze(1).to_broadcast([TP, NT, E]), ALU.add))
            oh4 = onehot.rearrange("p (t k) e -> p t k e", k=TOPK)
            for t in range(NT):
                link(nc.vector.tensor_tensor(oh4[:, t, :, :], oh4[:, t, :, :],
                                             rank[:, t, :].unsqueeze(1).to_broadcast([TP, TOPK, E]), ALU.mult))
            link(nc.vector.tensor_reduce(dest_f, onehot, axis=AX.X, op=ALU.add))
            nc.vector.tensor_copy(dest[:, :], dest_f).then_inc(dest_done, 1)
            link(nc.vector.tensor_tensor(ended, iota_q.unsqueeze(2).to_broadcast([1, MAXR + 1, E]),
                                         rend[0:1, :].unsqueeze(1).to_broadcast([1, MAXR + 1, E]), ALU.is_ge))
            link(nc.vector.tensor_reduce(table_f, ended, axis=AX.X, op=ALU.add))
            link(nc.vector.tensor_scalar(table[0:1, 0:MAXR + 1], table_f, float(E - 1), None, ALU.min))
            nc.vector.tensor_copy(table[0:1, MAXR + 1:MAXR + 2], rend[0:1, E - 1:E]).then_inc(table_done, 1)
            dve.wait_ge(table_done, 1)
            rounds = dve.value_load(table[0:1, MAXR + 1:MAXR + 2], min_val=1, max_val=MAXR - 1)

            def split_lo(n, j):
                dve.wait_ge(hi_done, n + 1)
                nc.vector.tensor_tensor(w_lo[:, j % NSPLIT, :, :], raw[:, j % NRAW, :, :],
                                        w_hi[:, j % NSPLIT, :, :].bitcast(f32), ALU.subtract).then_inc(lo_done, 1)

            def x_lo_part(n, t):
                dve.wait_ge(xhi_done, n + 1)
                nc.vector.tensor_tensor(x_lo[:, 2 * t:2 * t + 2, :], tx_ps[:, 0:2 * SLOTS].rearrange("p (k s) -> p k s", k=2),
                                        x_hi[:, 2 * t:2 * t + 2, :].bitcast(f32), ALU.subtract).then_inc(xlo_done, 1)

            for t in range(4):
                x_lo_part(t, t)
            for j in range(NSPLIT):
                split_lo(j, j)
            with dve.Fori(0, rounds) as q:
                e = dve.value_load(table[0:1, bass.ds(q, 1)], min_val=0, max_val=E - 1)
                nc.vector.tensor_copy(bias_gu[:, :], bias_all[:, bass.ds(e, 1), 0:2 * KT].rearrange("p a k -> p (a k)")
                                      ).then_inc(bias_gu_done, 1)
                for j in range(NPIECE):
                    n = q * NPIECE + j + NSPLIT
                    jn = (j + NSPLIT) % NPIECE
                    c = j // 2
                    if j < 8 and j % 2 == 0:
                        dve.wait_ge(piece_used, q * NPIECE + j + 1 + NSPLIT)
                        if j == 0:
                            dve.wait_ge(bias_gu_done, q + 1)
                        for f in range(2):
                            ins = nc.vector.tensor_scalar(g_t[:, f * SLOTS:(f + 1) * SLOTS],
                                                          gate_ps[c % 2][:, f * SLOTS:(f + 1) * SLOTS],
                                                          bias_gu[:, 2 * c + f:2 * c + f + 1], LIMIT, ALU.add, ALU.min)
                        ins.then_inc(gt_read, 1)
                        split_lo(n, jn)
                    elif j < 8:
                        dve.wait_ge(piece_used, q * NPIECE + j + 1 + NSPLIT)
                        for f in range(2):
                            ins = nc.vector.tensor_scalar(u_t[:, f * SLOTS:(f + 1) * SLOTS],
                                                          up_ps[c % 2][:, f * SLOTS:(f + 1) * SLOTS],
                                                          bias_gu[:, KT + 2 * c + f:KT + 2 * c + f + 1], LIMIT, ALU.add, ALU.min)
                        ins.then_inc(up_read, 1)
                        dve.wait_ge(up_read, q * 4 + c + 3)
                        nc.vector.tensor_scalar(u_t[:, :], u_t[:, :], -LIMIT, 1.0, ALU.max, ALU.add).then_inc(glu, 1)
                        dve.wait_ge(sig_done, q * 4 + c + 1)
                        nc.vector.tensor_tensor(g_t[:, :], g_t[:, :], s_t[:, :], ALU.mult).then_inc(glu, 1)
                        dve.wait_ge(glu, q * 12 + 3 * c + 2)
                        nc.vector.tensor_tensor(a_t[:, :], g_t[:, :], u_t[:, :], ALU.mult).then_inc(glu, 1)
                        dve.wait_ge(ahi_done, q * 4 + c + 1)
                        nc.vector.tensor_tensor(a_lo[:, 2 * c:2 * c + 2, :], a_t[:, :].rearrange("p (k s) -> p k s", k=2),
                                                a_hi[:, 2 * c:2 * c + 2, :].bitcast(f32), ALU.subtract).then_inc(alo_done, 1)
                        split_lo(n, jn)
                    else:
                        x_lo_part(q * 4 + 4 + j - 8, j - 8)
                        split_lo(n, jn)
            dve.wait_ge(gf_in, 16)

            def finish(t):
                dve.wait_ge(fstd_done, t + 1)
                nc.vector.reciprocal(frs[:, t:t + 1], frs[:, t:t + 1]).then_inc(frs_done, 1)
                dve.wait_ge(frs_done, t + 1)
                if t >= 2:
                    dve.wait_ge(out_done[t % 2], 16 * (t // 2))
                nc.vector.scalar_tensor_tensor(out=fin[:, t % 2, :], in0=h_all[:, t, :], scalar=frs[:, t:t + 1], in1=gf_b,
                                               op0=ALU.mult, op1=ALU.mult).then_inc(fin_done, 1)

            for t in range(NT):
                dve.wait_ge(got_in[t % 2], 16 * TOPK * (t // 2 + 1))
                for k in range(TOPK):
                    if t or k:
                        dve.wait_ge(sum_done, TOPK * t + k)
                    ins = nc.vector.scalar_tensor_tensor(out=h_all[:, t, :], in0=y_got[:, t % 2, k, :], scalar=gates[:, t, k:k + 1],
                                                         in1=h_all[:, t, :], op0=ALU.mult, op1=ALU.add)
                    ins.then_inc(sum_done, 1)
                if t >= 1:
                    finish(t - 1)
            finish(NT - 1)

        def on_tensor(pe):
            pe.wait_ge(wo_add, 2 * NT)
            pe.wait_ge(bias_in, 48)
            for a in range(3 * KT):
                ins = nc.tensor.transpose(bank[a // 12][:, (a % 12) * E:(a % 12 + 1) * E],
                                          bias_rows[:, a // KT, (a % KT) * 128:(a % KT + 1) * 128], ident[0:E, 0:E])
                if a % 12 == 11:
                    ins.then_inc(biasT_ps, 1)
            pe.wait_ge(const_in, 48)
            for t in range(NT):
                pe.wait_ge(hn_done, t + 1)
                if t >= 2:
                    pe.wait_ge(hnT_done, 2 * (t - 1))
                for k in range(KT):
                    ins = nc.tensor.transpose(bank[2 + 2 * (t % 2) + k // 4][:, (k % 4) * TP:(k % 4 + 1) * TP],
                                              hn[:, t % 2, k * 128:(k + 1) * 128], ident[0:TP, 0:TP])
                ins.then_inc(hnT_ps, 1)
                pe.wait_ge(hnT_done, 2 * (t + 1))
                if t >= 2:
                    pe.wait_ge(lg_read, t - 1)
                for k in range(KT):
                    ins = nc.tensor.matmul(bank[6 + t % 2][0:TP, 0:E], hnT[:, t % 2, k, :], wr_t[:, k, :],
                                           start=k == 0, stop=k == KT - 1)
                ins.then_inc(logit_ps, 1)
            pe.wait_ge(chosen_done, 1)
            pe.wait_ge(pool_const, 2)
            pe.wait_ge(dve_const, 1)
            pe.wait_ge(biasT_done, 2)
            nc.tensor.matmul(bank[0][0:TP, 0:NT * E], tri, chosen.rearrange("p t e -> p (t e)"), start=True, stop=False)
            nc.tensor.matmul(bank[0][0:TP, 0:NT * E], ones[:, 0:TP], before[:, 0:NT, :].rearrange("p t e -> p (t e)"),
                             start=False, stop=True).then_inc(rank_ps, 1)
            nc.tensor.matmul(bank[1][0:TP, 0:E], ones[:, 0:TP], before[:, NT, :], start=True, stop=True).then_inc(rank_ps, 1)
            pe.wait_ge(table_done, 1)
            rounds = pe.value_load(table[0:1, MAXR + 1:MAXR + 2], min_val=1, max_val=MAXR - 1)

            def x_part(n, t, first):
                if not first:
                    pe.wait_ge(xlo_done, n)
                for k in range(2):
                    for b in range(2):
                        ins = nc.tensor.transpose(tx_ps[:, k * SLOTS + b * HALF:k * SLOTS + (b + 1) * HALF],
                                                  x_rows[:, b, (2 * t + k) * 128:(2 * t + k + 1) * 128], ident[0:HALF, 0:HALF])
                ins.then_inc(xT_ps, 1)

            def three(ps, s, k, col, mhi, mlo, start, stop):
                whi = w_hi[:, s, k, col:col + 128]
                nc.tensor.matmul(ps, whi, mhi, start=start, stop=False)
                nc.tensor.matmul(ps, whi, mlo, start=False, stop=False)
                return nc.tensor.matmul(ps, w_lo[:, s, k, col:col + 128], mhi, start=False, stop=stop)

            pe.wait_ge(rows_in, 32)
            for t in range(4):
                x_part(t, t, t == 0)
            with pe.Fori(0, rounds) as q:
                for j in range(8):
                    c = j // 2
                    ps = (gate_ps, up_ps)[j % 2][c % 2]
                    pe.wait_ge(lo_done, q * NPIECE + j + 1 + NRAW)
                    if j == 0:
                        pe.wait_ge(xlo_done, q * 4 + 4)
                    pe.wait_ge((gt_read, up_read)[j % 2], q * 4 + c + 1)
                    for f in range(2):
                        for k in range(KT):
                            ins = three(ps[:, f * SLOTS:(f + 1) * SLOTS], j % NSPLIT, k, f * 128, x_hi[:, k, :], x_lo[:, k, :],
                                        k == 0, k == KT - 1)
                    ins.then_inc(piece_used, 1)
                def y_part(c):
                    pe.wait_ge(yT_done, q * 8 + 2 * c + 4)
                    pe.wait_ge(yrow_done, q * 4 + c + 1)
                    for d in range(2):
                        for b in range(2):
                            ins = nc.tensor.transpose(ty_ps[0:HALF, b * PC + d * 128:b * PC + (d + 1) * 128],
                                                      y_T[:, c % 2, d, b * HALF:(b + 1) * HALF], ident[:, :])
                    ins.then_inc(yrow_ps, 1)

                pe.wait_ge(rows_in, q * 32 + 64)
                for c in range(4):
                    j = 8 + c
                    x_part(q * 4 + 4 + c, c, False)
                    pe.wait_ge(lo_done, q * NPIECE + j + 1 + NRAW)
                    cuts = ((0, 6), (6, 8)) if c == 0 else ((0, 8),)
                    for k0, k1 in cuts:
                        if c == 0:
                            pe.wait_ge(alo_done, q * 4 + (3 if k0 == 0 else 4))
                        for d in range(2):
                            if k0 == 0:
                                pe.wait_ge(yT_done, q * 8 + 2 * c + d + 1)
                            for k in range(k0, k1):
                                ins = three(y_ps[d][:, 0:SLOTS], j % NSPLIT, k, d * 128, a_hi[:, k, :], a_lo[:, k, :],
                                            k == 0, k == KT - 1)
                            if k1 == 8:
                                if d == 0:
                                    ins.then_inc(yT_ps, 1)
                                else:
                                    ins.then_inc(piece_used, 1)
                    if c >= 1:
                        y_part(c - 1)
                y_part(3)



    return on_sync, on_gpsimd, on_scalar, on_vector, on_tensor


def program(nc, a, out):
    f32 = mybir.dt.float32
    u32 = mybir.dt.uint32
    TOK, D, E, TOPK, SLOTS = 1040, 1024, 32, 4, 192
    TP, NT = 104, 10
    MAXR = E + TOK * TOPK // SLOTS + 1
    MINR = TOK * TOPK // SLOTS
    with ExitStack() as ctx:
        bank = [ctx.enter_context(nc.psum_tensor(f"bank{i}", [128, 512], f32)) for i in range(8)]
        hn_d = nc.dram_tensor("hn_d", (TOK, D), f32).ap()
        ys_d = nc.dram_tensor("ys_d", (MAXR * SLOTS, D), f32).ap()
        rowtok_d = nc.dram_tensor("rowtok_d", (MAXR * SLOTS, 1), u32).ap()
        keep = Plan(nc, (nc.sbuf_base + 63) // 64 * 64)
        shared = dict(ident=keep("ident", [128, 128]), eps_t=keep("eps_t", [128, 1]))
        shared.update(gates=keep("gates", [TP, NT, TOPK]), dest=keep("dest", [TP, NT * TOPK], u32))
        shared['start'] = keep.at + 256
        at_h = Plan(nc, shared['start'])
        shared['h_all'] = at_h("h_all", [TP, NT, D])
        shared['after_h'] = at_h.at
        shared['zero_out'] = ctx.enter_context(nc.semaphore("zero_out"))
        shared['wo_add'] = ctx.enter_context(nc.semaphore("wo_add"))
        shared.update(hn_d=hn_d, ys_d=ys_d, rowtok_all=rowtok_d, rounds=MAXR, slots=SLOTS,
                      rowtok_d=rowtok_d.rearrange("(q s) a -> q (s a)", s=SLOTS),
                      ys_rest=[ys_d[r * SLOTS:(r + 1) * SLOTS, :].rearrange("(p b) d -> p (b d)", b=2) for r in range(MINR, MAXR)])
        mixing = mixing_program(nc, ctx, a, bank, keep, shared)
        assert keep.at <= shared['start']
        experts = experts_program(nc, ctx, a, bank, shared, out)

        block = ctx.enter_context(nc.Block())

        @block.sync
        def _(sp):
            for part in (mixing, experts):
                part[0](sp)

        @block.gpsimd
        def _(pool):
            for part in (mixing, experts):
                part[1](pool)

        @block.scalar
        def _(act):
            for part in (mixing, experts):
                part[2](act)

        @block.vector
        def _(dve):
            for part in (mixing, experts):
                part[3](dve)

        @block.tensor
        def _(pe):
            for part in (mixing, experts):
                part[4](pe)


_INS = ['x', 'meta_tokens', 'ln1_g', 'w_in', 'mu_r', 'mu_k', 'mu_v', 'mu_w', 'mu_a', 'mu_g', 'w0', 'w_w1', 'w_w2', 'a0', 'w_a1', 'w_a2',
        'w_g1', 'w_g2', 'k_k', 'k_a', 'r_k', 'lnx_g', 'lnx_b', 'w_o_rwkv', 'conv_w', 'w_o_conv', 'w_o', 'ln2_g', 'w_router', 'b_router',
        'w_e_gate', 'b_e_gate', 'w_e_up', 'b_e_up', 'w_e_down', 'b_e_down', 'lnf_g']


def kernel(**inputs):
    import numpy as _np
    import concourse.bacc as _bacc
    from concourse import mybir as _mybir
    from concourse.bass_utils import run_bass_kernel_spmd as _run

    nc = _bacc.Bacc("TRN2", target_bir_lowering=False, num_devices=1)
    arrays, a = {}, {}
    for name in _INS:
        x = _np.ascontiguousarray(inputs[name])
        arrays[f"in_{name}"] = x
        ap = nc.dram_tensor(f"in_{name}", x.shape, _mybir.dt.from_np(x.dtype), kind="ExternalInput").ap()
        a[name] = ap if name in ('meta_tokens', 'lnf_g') else ap[0]
    out = nc.dram_tensor("out_0", (1024, 1024), _mybir.dt.float32, kind="ExternalOutput").ap()
    program(nc, a, out)
    r = _run(nc, [arrays], core_ids=[0])
    return r.results[0]["out_0"].reshape(1, 1024, 1024)
```

```python
from contextlib import ExitStack

import concourse.bass as bass
from concourse import mybir


class Plan:

    def __init__(self, nc, at):
        self.nc, self.at = nc, at

    def __call__(self, name, shape, dt=mybir.dt.float32):
        size = 4
        for n in shape[1:]:
            size *= n
        t = self.nc.alloc_sbuf_tensor_at(name, shape, dt, offset=self.at)
        self.at += (size + 31) // 32 * 32
        return t[(slice(None),) * len(shape)]


def mixing_program(nc, ctx, a, bank, keep, shared):
    f32 = mybir.dt.float32
    f32r = mybir.dt.float32r
    u32 = mybir.dt.uint32
    ALU = mybir.AluOpType
    ACT = mybir.ActivationFunctionType
    AX = mybir.AxisListType

    D = 1024
    META = 16
    TOK = 1040
    NT = 10
    TP = TOK // NT
    KT = D // 128
    RW = 512
    NJ = RW // 128
    HS = 64
    NCH = 4
    CH = TOK // NCH
    NU = 2 * NT
    NB = NU // 4
    LEVELS = 7
    EPS = 1e-5
    LNX_EPS = 64e-5
    DECAY = 0.6065306597126334

    if True:
        def sem(name):
            return ctx.enter_context(nc.semaphore(name))

        ident, eps_t, h_all, zero_out, wo_add = shared['ident'], shared['eps_t'], shared['h_all'], shared['zero_out'], shared['wo_add']
        epsx_t = keep("epsx_t", [128, 1])
        dz = keep("dz", [128, 8])
        ones_t = keep("ones_t", [128, 1])
        START = shared['start']

        wk = Plan(nc, START)
        AT = wk("AT", [TP, NU, 4, TP])
        Tm = wk("Tm", [TP, NU, TP])
        Rm = wk("Rm", [TP, NU, TP])
        P1 = wk("P1", [TP, 2, 4, TP])
        Vt = wk("Vt", [TP, NT, 128])
        Bt = wk("Bt", [TP, NT, 128])
        Kt = wk("Kt", [TP, NT, 128])
        X = wk("X", [TP, NU, 128])
        x1t = wk("x1t", [128, NT, TP])
        mxt = wk("mxt", [128, NT, HS])
        np_ = wk("np_", [128, NT, HS])
        S = wk("S", [128, NT + 1, HS])
        U = wk("U", [TP, NU, HS])
        pr = Plan(nc, START)
        pb = pr("pb", [128, 3, TOK + 2])
        r_t = pr("r_t", [128, TOK])
        k_t = pr("k_t", [128, TOK])
        sg = pr("sg", [128, TOK])
        cs = pr("cs", [128, TOK])
        e0 = pr("e0", [128, TOK])
        e1 = pr("e1", [128, TOK])
        e2 = pr("e2", [128, TOK])
        a_t = pr("a_t", [128, TOK])
        kk = pr("kk", [128, TOK])
        tmp = pr("tmp", [128, TOK])
        nrm = pr("nrm", [128, TOK])
        assert pr.at <= wk.at
        s0 = Plan(nc, START)
        x_in = s0("x_in", [TP, 2, D])
        xn = s0("xn", [TP, 2, D])
        junk = s0("junk", [TP, D])
        ss = s0("ss", [TP, NT])
        rstd = s0("rstd", [TP, NT])
        lraw = s0("lraw", [128, KT, 256])
        lmu = s0("lmu", [128, KT, 256])
        o1 = s0("o1", [128, 2, TOK])
        o2 = s0("o2", [128, 2, TOK + 1])
        vrows = s0("vrows", [84, 128])
        assert s0.at <= wk.at
        s1 = Plan(nc, shared['after_h'])
        mT = s1("mT", [128, KT, TOK])
        cv = s1("cv", [128, NJ, TOK])
        assert s1.at <= wk.at
        s2 = Plan(nc, START)
        cpb = s2("cpb", [128, 3, TOK + 2])
        c1 = s2("c1", [128, TOK])
        gt = s2("gt", [128, 2, 2, CH])
        m1 = s2("m1", [128, 2, CH])
        assert s2.at <= START + 4 * NT * D

        com = Plan(nc, wk.at)
        xnT = com("xnT", [128, KT, TOK])
        yg = com("yg", [128, NJ, TOK])
        ring = com("ring", [128, 3, KT, 128])
        bones = com("bones", [128, 128])
        mask4 = com("mask4", [TP, 4, TP])
        mlev = com("mlev", [TP, LEVELS, 128])
        id2 = com("id2", [128, HS])
        vec = com("vec", [128, 84])
        vj = com("vj", [128, 12])
        pc = com("pc", [128, NT])
        J0 = com.at
        lw = com("lw", [128, TOK])
        lg = com("lg", [128, TOK])
        w2 = com("w2", [128, RW])
        wg2 = com("wg2", [128, RW])
        w2j = com("w2j", [128, 128])
        wg2j = com("wg2j", [128, 128])
        v_t = com("v_t", [128, TOK])
        rkb = com("rkb", [128, TOK])
        y_t = com("y_t", [128, TOK])
        ar = com("ar", [128, NT, 2, TP])
        zero = ar.rearrange("p c m t -> p (c m t)")
        bh = com("bh", [128, TOK])
        kh = com("kh", [128, TOK])
        wo_t = Plan(nc, J0)("wo_t", [128, KT, D])
        assert J0 + 4 * KT * D <= com.at

        VEC = {}
        at = 0
        for name, n in (('mu_w', 8), ('mu_a', 8), ('mu_g', 8), ('ln1_g', 8), ('mu_r', 4), ('mu_k', 4), ('mu_v', 4), ('w0', 4),
                        ('a0', 4), ('k_k', 4), ('k_a', 4), ('r_k', 4), ('lnx_g', 4), ('lnx_b', 4), ('conv_w', 12)):
            VEC[name] = at
            at += n
        assert at == 84
        JV = {name: i for i, name in enumerate(('mu_r', 'mu_k', 'mu_v', 'w0', 'a0', 'k_k', 'k_a', 'r_k', 'lnx_g', 'lnx_b'))}

        def pj(name):
            return vj[:, JV[name]:JV[name] + 1]

        TA = 'bkav'
        PE_J = ([('z', c) for c in range(NCH)] + [('p', 'r', 0), ('p', 'r', 1)] + [('n', c) for c in range(NCH)]
                + [('p', 'r', 2), ('p', 'r', 3)] + [('p', 'v', c) for c in range(NCH)] + [('t', x, g) for x in TA for g in range(3)]
                + [('A', u) for u in range(NU)])
        for l in range(LEVELS):
            for s in range(NB + 1):
                if s < NB:
                    PE_J.append(('P', l, s))
                if s > 0:
                    PE_J.append(('D', l, s - 1))
        PE_J += ([('xa', g) for g in range(3)] + [('xc', g) for g in range(3)] + [('xb', g) for g in range(5)]
                 + [('m', g) for g in range(2)] + [('nn', g) for g in range(2)] + [('s', c) for c in range(1, NT)]
                 + [('u', g) for g in range(2)] + [('y', g) for g in range(3)]
                 + [('bs', c) for c in range(NCH)] + [('g', c) for c in range(NCH)]
                 + [('mean', c) for c in range(NCH)] + [('var', c) for c in range(NCH)])
        ACT_J = ([('p', 'k', c) for c in range(NCH)] + [(x, c) for c in range(NCH) for x in 'za'] + ['sq', ('p', 'r', 0), ('p', 'r', 1)]
                 + [('n', c) for c in range(NCH)] + [('p', 'r', 2), ('p', 'r', 3), ('p', 'v', 0), ('p', 'v', 1)]
                 + ['E1', 'E2', 'E0', ('p', 'v', 2), ('p', 'v', 3)] + [('t', x, g) for x in TA for g in range(3)]
                 + [('xa', g) for g in range(3)] + [('xc', g) for g in range(3)] + [('xb', g) for g in range(5)]
                 + [('y', g) for g in range(3)] + ['ysq'] + [('var', c) for c in range(NCH)])
        DVE_J = (['k_d', 'k', 'kkr'] + [('cs', c) for c in range(NT)]
                 + ['csx', 'km', 'kmod', 'nmax', 'nrec', 'kk', 'at', 'ba', 'bh', 'kh', 'pc', 'r_d', 'r', 'rkb', 'rt', 'v_d', 'v']
                 + [('A', u) for u in range(NU)])
        for l in range(LEVELS):
            for s in range(NB + 1):
                if s < NB:
                    DVE_J.append(('P', l, s))
                if s > 0:
                    DVE_J += [('T', l, s - 1)] * (l < LEVELS - 1) + [('R', l, s - 1)]
        DVE_J += ([('m', g) for g in range(2)] + [('nn', g) for g in range(2)] + ['S0'] + [('S', c) for c in range(NT)]
                  + [('u', g, h) for g in range(2) for h in range(2)] + [('bo', c) for c in range(NCH)]
                  + [('yc', c) for c in range(NCH)] + ['yrec', 'yn', 'yaff', 'ysum'] + [('yg', c) for c in range(NCH)])
        POOL_J = ['vj', 'w2', 'wg2', 'T0', 'R0']

        class Order:
            def __init__(self, sem, labels):
                self.sem, self.labels, self.next = sem, {x: i for i, x in enumerate(labels)}, 0
                assert len(self.labels) == len(labels)

            def done(self, eng, label, j, passed=None):
                eng.wait_ge(self.sem, j * len(self.labels) + self.labels[label] + 1)
                if passed is not None:
                    eng.sem_inc(passed, 1)

            def mark(self, ins, label):
                assert self.labels[label] == self.next, label
                self.next = (self.next + 1) % len(self.labels)
                ins.then_inc(self.sem, 1)

        pe_j = Order(sem("pe_j"), PE_J)
        act_j = Order(sem("act_j"), ACT_J)
        dve_j = Order(sem("dve_j"), DVE_J)
        pool_j = Order(sem("pool_j"), POOL_J)

        vec_in = sem("vec_in")
        x_got = [sem("x_got0"), sem("x_got1")]
        lora_in = sem("lora_in")
        w2_in = sem("w2_in")
        ring_in = [sem(f"ring_in{s}") for s in range(3)]
        h_in = sem("h_in")
        wo_in = sem("wo_in")
        pool_c = sem("pool_c")
        dve_c = sem("dve_c")
        vec_ps = sem("vec_ps")
        vec_done = sem("vec_done")
        sq0_done = sem("sq0_done")
        std0_done = sem("std0_done")
        rstd0_done = sem("rstd0_done")
        xn_done = sem("xn_done")
        xnT_ps = sem("xnT_ps")
        xnT_done = sem("xnT_done")
        lmu_done = sem("lmu_done")
        lora_ps = sem("lora_ps")
        lora_ev = sem("lora_ev")
        lora_mix = sem("lora_mix")
        lora_done = sem("lora_done")
        conv_ps = sem("conv_ps")
        conv_ev = sem("conv_ev")
        conv_step = sem("conv_step")
        gate_ps = sem("gate_ps")
        gate_sig = sem("gate_sig")
        gate_mul = sem("gate_mul")
        wo_ps = sem("wo_ps")
        sp_passed = sem("sp_passed")
        pool_passed = sem("pool_passed")
        pe_passed = sem("pe_passed")
        col_free = sem("col_free")
        k_ps = sem("k_ps")
        late_free = sem("late_free")
        pbz = sem("pbz")


        w_in = a['w_in']

        def cols(w, c0, n=128):
            return w[:, bass.ds(c0, n)].rearrange("(k p) c -> p k c", p=128)

        def x_tile(t):
            if t == 0:
                return [((0, META), a['meta_tokens']), ((META, TP), a['x'][0:TP - META, :])]
            return [((0, TP), a['x'][TP * t - META:TP * (t + 1) - META, :])]

        def on_sync(sp):
            for name in ('mu_w', 'mu_a', 'mu_g', 'ln1_g', 'mu_r', 'mu_k', 'mu_v', 'w0', 'a0', 'k_k', 'k_a', 'r_k', 'lnx_g', 'lnx_b'):
                n = a[name].shape[0] // 128
                sp.dma_start(vrows[VEC[name]:VEC[name] + n, :], a[name].rearrange("(k p) -> k p", p=128)).then_inc(vec_in, 16)
            sp.dma_start(vrows[VEC['conv_w']:VEC['conv_w'] + 12, :], a['conv_w'].rearrange("w (k p) -> (w k) p", p=128)
                         ).then_inc(vec_in, 16)
            sp.wait_ge(dve_c, 6)
            sp.dma_start(shared['rowtok_rows'], zero[0:shared['rowtok_rows'].shape[0], 0:shared['rowtok_rows'].shape[1]].bitcast(u32)).then_inc(zero_out, 16)
            for t in range(NT):
                if t >= 2:
                    sp.wait_ge(xn_done, t - 1)
                    sp.wait_ge(sq0_done, t - 1)
                for (p0, p1), src in x_tile(t):
                    sp.dma_start(x_in[p0:p1, t % 2, :], src).then_inc(x_got[t % 2], 16)
            sp.dma_start(lraw[:, :, 0:64], cols(a['w_w1'], 0, 64)).then_inc(lora_in, 16)
            sp.dma_start(lraw[:, :, 64:128], cols(a['w_a1'], 0, 64)).then_inc(lora_in, 16)
            sp.dma_start(lraw[:, :, 128:256], cols(a['w_g1'], 0, 128)).then_inc(lora_in, 16)
            sp.dma_start(w2[0:64, :], a['w_w2']).then_inc(w2_in, 16)
            sp.dma_start(w2[64:128, :], a['w_a2']).then_inc(w2_in, 16)
            sp.dma_start(wg2[:, :], a['w_g2']).then_inc(w2_in, 16)
            for rows in shared['ys_rest']:
                sp.dma_start(rows, zero[0:rows.shape[0], 0:rows.shape[1]]).then_inc(zero_out, 16)

            def load(i, c0):
                sp.dma_start(ring[:, i, :, :], cols(w_in, c0)).then_inc(ring_in[i], 16)

            for i in range(3):
                load(i, RW * i)
            with sp.Fori(0, NJ - 1) as j:
                sp.wait_ge(k_ps, j * NCH + NCH)
                sp.sem_inc(sp_passed, 1)
                load(1, (j + 1) * 128 + RW)
                for i, x in ((0, 'r'), (2, 'v')):
                    pe_j.done(sp, ('p', x, NCH - 1), j, sp_passed)
                    load(i, (j + 1) * 128 + RW * i)
            sp.wait_ge(k_ps, NJ * NCH)
            load(1, RW * (3 + 1))
            for i, x in ((0, 'r'), (2, 'v')):
                pe_j.done(sp, ('p', x, NCH - 1), NJ - 1)
                load(i, RW * (3 + i))
            with sp.Fori(0, NJ - 1) as j:
                for i in range(3):
                    sp.wait_ge(conv_ps, j * 12 + 4 * i + 4)
                    sp.sem_inc(sp_passed, 1)
                    load(i, (j + 1) * 128 + RW * (3 + i))

            def load_gates(d):
                for i in range(2):
                    load(i, d * 128 + 6 * RW + D * i)
                sp.dma_start(ring[:, 2, 0:4, :], cols(a['w_o_rwkv'], d * 128)).then_inc(ring_in[2], 16)
                sp.dma_start(ring[:, 2, 4:8, :], cols(a['w_o_conv'], d * 128)).then_inc(ring_in[2], 16)

            sp.wait_ge(conv_ps, NJ * 12)
            load_gates(0)
            with sp.Fori(0, KT - 1) as d:
                sp.wait_ge(gate_ps, d * 4 + 4)
                sp.sem_inc(sp_passed, 1)
                load_gates(d + 1)
            dve_j.done(sp, ('yg', NCH - 1), NJ - 1)
            sp.dma_start(wo_t[:, :, :], a['w_o'].rearrange("(k p) c -> p k c", p=128)).then_inc(wo_in, 16)
            sp.wait_ge(gate_mul, 3 * KT * NCH + 6)
            for t in range(NT):
                for (p0, p1), src in x_tile(t):
                    sp.dma_start(h_all[p0:p1, t, :], src).then_inc(h_in, 16)

        def on_gpsimd(pool):
            n = [0]

            def step(ins):
                n[0] += 1
                ins.then_inc(pool_c, 1)
                pool.wait_ge(pool_c, n[0])

            def select(out, op, base, pattern, cm, fill):
                step(nc.gpsimd.affine_select(out=out, in_=out, compare_op=op, fill=fill, base=base, pattern=pattern,
                                             channel_multiplier=cm))

            step(nc.gpsimd.memset(ident[:, :], 0.0))
            select(ident[:, :], ALU.not_equal, 0, [[-1, 128]], 1, 1.0)
            step(nc.gpsimd.memset(id2[:, :], 0.0))
            select(id2[:, :], ALU.not_equal, 0, [[-1, HS]], 1, 1.0)
            select(id2[:, :], ALU.not_equal, -HS, [[-1, HS]], 1, 1.0)
            step(nc.gpsimd.memset(bones[:, :], 0.0))
            step(nc.gpsimd.memset(bones[0:HS, 0:HS], 1.0))
            step(nc.gpsimd.memset(bones[HS:128, HS:128], 1.0))
            step(nc.gpsimd.memset(mask4[:, :, :], 1.0))
            for m in range(4):
                select(mask4[:, m, :], ALU.is_gt if m % 2 == 0 else ALU.is_ge, 0, [[1, TP]], -1, 0.0)
            step(nc.gpsimd.memset(mlev[:, :, :], 1.0))
            for l in range(LEVELS):
                b = 2 << l
                h = b // 2
                v = mlev[:, l, :]
                pat = [[-b, 128 // b], [0, b]]
                select(v, ALU.is_ge, -h, pat, 1, 0.0)
                select(v, ALU.is_gt, b, [[b, 128 // b], [0, b]], -1, 0.0)
                select(v, ALU.is_gt, h, [[0, 128 // b], [-1, b]], 0, 0.0)

            pool.wait_ge(vec_done, 1)
            pool.wait_ge(w2_in, 48)
            with pool.Fori(0, NJ) as j:
                pool.wait_ge(col_free, j + 1)
                pool.sem_inc(pool_passed, 1)
                pool_j.mark(nc.gpsimd.tensor_copy(vj[:, 0:10], vec[:, VEC['mu_r']:VEC['mu_r'] + 40].rearrange(
                    "p (a k) -> p a k", k=4)[:, :, bass.ds(j, 1)].rearrange("p a k -> p (a k)")), 'vj')
                pool_j.mark(nc.gpsimd.tensor_copy(w2j[:, :], w2[:, bass.ds(j * 128, 128)]), 'w2')
                pool_j.mark(nc.gpsimd.tensor_copy(wg2j[:, :], wg2[:, bass.ds(j * 128, 128)]), 'wg2')
                dve_j.done(pool, 'v', j, pool_passed)
                for m, x in ((Tm, 'T0'), (Rm, 'R0')):
                    pool_j.mark(nc.gpsimd.tensor_copy(m[:, :, :], ident[0:TP, 0:TP].unsqueeze(1).to_broadcast([TP, NU, TP])), x)

        def evac_groups():
            return ((0, 4), (4, 8), (8, 10))

        def on_scalar(act):
            act.wait_ge(vec_ps, 1)
            nc.scalar.activation(vec[:, :], bank[7][:, 0:84], ACT.Copy).then_inc(vec_done, 1)
            for t in range(NT):
                act.wait_ge(x_got[t % 2], 16 * (t // 2 + 1 + (1 if t % 2 == 0 else 0)))
                if t:
                    act.wait_ge(sq0_done, t)
                nc.scalar.activation(junk[:, :], x_in[:, t % 2, :], ACT.Square, accum_out=ss[:, t:t + 1]).then_inc(sq0_done, 1)
                act.wait_ge(sq0_done, t + 1)
                act.wait_ge(dve_c, 6)
                nc.scalar.activation(rstd[:, t:t + 1], ss[:, t:t + 1], ACT.Sqrt, bias=eps_t[0:TP, :], scale=1.0 / D
                                     ).then_inc(std0_done, 1)
            for m in range(2):
                for c in range(NCH):
                    act.wait_ge(lora_ps, 4 * m + c + 1)
                    nc.scalar.activation(o1[:, m, CH * c:CH * (c + 1)], bank[c % 2][:, 0:CH], ACT.Copy).then_inc(lora_ev, 1)
                    nc.scalar.activation(o2[:, m, 1 + CH * c:1 + CH * (c + 1)], bank[2 + c % 2][:, 0:CH], ACT.Copy).then_inc(lora_ev, 1)
            act.wait_ge(lora_mix, 4)
            nc.scalar.activation(lw[0:64, :], o1[0:64, 0, :], ACT.Tanh).then_inc(lora_done, 1)
            nc.scalar.activation(lw[64:128, :], o1[64:128, 0, :], ACT.Copy).then_inc(lora_done, 1)
            nc.scalar.activation(lg[:, :], o1[:, 1, :], ACT.Sigmoid).then_inc(lora_done, 1)

            with act.Fori(0, NJ) as j:
                act.wait_ge(col_free, j + 1)
                pool_j.done(act, 'vj', j)

                def project_out(x, c, bk):
                    act_j.mark(nc.scalar.activation(pb[:, 'rkv'.index(x), 2 + CH * c:2 + CH * (c + 1)], bank[bk][:, 0:CH], ACT.Copy),
                               ('p', x, c))

                for c in range(NCH):
                    act.wait_ge(k_ps, j * NCH + c + 1)
                    project_out('k', c, 2 + c)
                for c in range(NCH):
                    pe_j.done(act, ('z', c), j)
                    act_j.mark(nc.scalar.activation(sg[:, CH * c:CH * (c + 1)], bank[c % 2][:, 0:CH], ACT.Sigmoid,
                                                    bias=pj('w0')), ('z', c))
                    act_j.mark(nc.scalar.activation(a_t[:, CH * c:CH * (c + 1)], bank[6 + c % 2][:, 0:CH], ACT.Sigmoid,
                                                    bias=pj('a0')), ('a', c))
                dve_j.done(act, 'kkr', j)
                act_j.mark(nc.scalar.activation(nrm[:, :], kk[:, :], ACT.Square), 'sq')
                for c in range(NCH):
                    if c == 2:
                        pe_j.done(act, ('n', NCH - 1), j)
                        for b in range(NCH):
                            act_j.mark(nc.scalar.activation(nrm[:, CH * b:CH * (b + 1)], bank[4 + b][:, 0:CH], ACT.Sqrt), ('n', b))
                    pe_j.done(act, ('p', 'r', c), j)
                    project_out('r', c, c % 2)
                for c in range(NCH):
                    if c == 2:
                        dve_j.done(act, 'csx', j)
                        act_j.mark(nc.scalar.activation(e1[:, :], cs[:, :], ACT.Exp, scale=-DECAY), 'E1')
                        act_j.mark(nc.scalar.activation(e2[:, :], cs[:, :], ACT.Exp, scale=DECAY), 'E2')
                        act_j.mark(nc.scalar.activation(e0[:, :], tmp[:, :], ACT.Exp, scale=-DECAY), 'E0')
                    pe_j.done(act, ('p', 'v', c), j)
                    project_out('v', c, c % 2)
                dve_j.done(act, 'v', j)
                q = 0
                for x in TA:
                    for g, (g0, g1) in enumerate(evac_groups()):
                        pe_j.done(act, ('t', x, g), j)
                        src = bank[2 + q % 2][0:TP, 0:128 * (g1 - g0)]
                        if x == 'a':
                            dst = X[:, 2 * g0:2 * g1, 0:HS]
                            src = src.rearrange("p (u n) -> p u n", n=HS)
                        else:
                            dst = dict(v=Vt, b=Bt, k=Kt)[x][:, g0:g1, :]
                            src = src.rearrange("p (c n) -> p c n", n=128)
                        act_j.mark(nc.scalar.activation(dst, src, ACT.Copy), ('t', x, g))
                        q += 1
                for g, (g0, g1) in enumerate(((0, 8), (8, 16), (16, 20))):
                    pe_j.done(act, ('xa', g), j)
                    act_j.mark(nc.scalar.activation(X[:, g0:g1, HS:128], bank[2 + g % 2][0:TP, 0:HS * (g1 - g0)].rearrange(
                        "p (u n) -> p u n", n=HS), ACT.Copy), ('xa', g))
                for g, (g0, g1) in enumerate(evac_groups()):
                    pe_j.done(act, ('xc', g), j)
                    act_j.mark(nc.scalar.activation(x1t[:, g0:g1, :], bank[4 + g % 2][:, 0:TP * (g1 - g0)].rearrange(
                        "p (c n) -> p c n", n=TP), ACT.Copy), ('xc', g))
                for g in range(5):
                    pe_j.done(act, ('xb', g), j)
                    act_j.mark(nc.scalar.activation(X[:, 4 * g:4 * g + 4, :], bank[6 + g % 2][0:TP, :].rearrange(
                        "p (u n) -> p u n", n=128), ACT.Copy), ('xb', g))
                for g, (g0, g1) in enumerate(evac_groups()):
                    pe_j.done(act, ('y', g), j)
                    act_j.mark(nc.scalar.activation(y_t[:, TP * g0:TP * g1], bank[6 + g % 2][:, 0:TP * (g1 - g0)], ACT.Copy),
                               ('y', g))
                dve_j.done(act, ('yc', NCH - 1), j)
                act_j.mark(nc.scalar.activation(tmp[:, :], y_t[:, :], ACT.Square), 'ysq')
                for c in range(NCH):
                    pe_j.done(act, ('var', c), j)
                    act_j.mark(nc.scalar.activation(nrm[:, CH * c:CH * (c + 1)], bank[4 + c % 2][:, 0:CH], ACT.Sqrt,
                                                    bias=epsx_t[:, :], scale=1.0 / HS), ('var', c))
            with act.Fori(0, NJ) as j:
                for i in range(3):
                    act.wait_ge(conv_step, j * 6 + 6)
                    for c in range(NCH):
                        act.wait_ge(conv_ps, j * 12 + 4 * i + c + 1)
                        nc.scalar.activation(cpb[:, i, 2 + CH * c:2 + CH * (c + 1)], bank[c % 2][:, 0:CH], ACT.Copy
                                             ).then_inc(conv_ev, 1)
            with act.Fori(0, KT) as d:
                for c in range(NCH):
                    s = c % 2
                    act.wait_ge(gate_mul, d * 12 + 3 * c + 3)
                    act.wait_ge(gate_ps, d * 4 + c + 1)
                    for m in range(2):
                        nc.scalar.activation(gt[:, s, m, :], bank[4 * s + m][:, 0:CH], ACT.Sigmoid).then_inc(gate_sig, 1)

        def on_vector(dve):
            def xnT_copy(t):
                dve.wait_ge(xnT_ps, t + 1)
                for h in range(2):
                    nc.vector.tensor_tensor(xnT[:, 4 * h:4 * h + 4, TP * t:TP * (t + 1)],
                                            bank[2 * (t % 2) + h][:, 0:4 * TP].rearrange("p (k t) -> p k t", k=4),
                                            vec[:, VEC['ln1_g'] + 4 * h:VEC['ln1_g'] + 4 * h + 4].unsqueeze(2).to_broadcast(
                                                [128, 4, TP]), ALU.mult).then_inc(xnT_done, 1)

            nc.vector.memset(eps_t[:, :], EPS).then_inc(dve_c, 1)
            nc.vector.memset(zero, 0.0).then_inc(dve_c, 1)
            nc.vector.memset(epsx_t[:, :], LNX_EPS).then_inc(dve_c, 1)
            nc.vector.memset(o2[:, :, 0:1], 0.0).then_inc(dve_c, 1)
            nc.vector.memset(ones_t[:, :], 1.0).then_inc(dve_c, 1)
            nc.vector.memset(pc[:, 1:2], 0.0).then_inc(col_free, 1)
            nc.vector.memset(pc[:, 2:3], 0.0).then_inc(dve_c, 1)
            for t in range(NT):
                dve.wait_ge(std0_done, t + 1)
                nc.vector.reciprocal(rstd[:, t:t + 1], rstd[:, t:t + 1]).then_inc(rstd0_done, 1)
                dve.wait_ge(rstd0_done, t + 1)
                if t >= 2:
                    dve.wait_ge(xnT_ps, t - 1)
                nc.vector.tensor_scalar(xn[:, t % 2, :], x_in[:, t % 2, :], rstd[:, t:t + 1], None, ALU.mult).then_inc(xn_done, 1)
                if t == 0:
                    dve.wait_ge(vec_done, 1)
                if t >= 1:
                    xnT_copy(t - 1)
            xnT_copy(NT - 1)
            dve.wait_ge(lora_in, 48)
            for m, (c0, c1_) in enumerate(((0, 64), (64, 128), (128, 256))):
                nc.vector.tensor_tensor(lmu[:, :, c0:c1_], lraw[:, :, c0:c1_],
                                        vec[:, 8 * m:8 * m + 8].unsqueeze(2).to_broadcast([128, KT, c1_ - c0]), ALU.mult
                                        ).then_inc(lmu_done, 1)
            for m in range(2):
                dve.wait_ge(lora_ev, 8 * (m + 1))
                nc.vector.tensor_tensor(o1[:, m, :], o1[:, m, :], o2[:, m, 1:TOK + 1], ALU.subtract).then_inc(lora_mix, 1)
                dve.wait_ge(lora_mix, 2 * m + 1)
                nc.vector.tensor_tensor(o1[:, m, :], o1[:, m, :], o2[:, m, 0:TOK], ALU.add).then_inc(lora_mix, 1)
            dve.wait_ge(lora_done, 3)
            dve.wait_ge(zero_out, shared['zeroed'])

            def tt(label, out, a_, b_, op):
                dve_j.mark(nc.vector.tensor_tensor(out, a_, b_, op), label)

            def stt(label, out, in0, s, in1, op0, op1):
                dve_j.mark(nc.vector.scalar_tensor_tensor(out=out, in0=in0, scalar=s, in1=in1, op0=op0, op1=op1), label)

            def chunks(x):
                return x.rearrange("p (c t) -> p c t", t=TP)

            with dve.Fori(0, NJ) as j:
                nc.vector.memset(pb[:, :, 0:2], 0.0).then_inc(pbz, 1)
                dve.wait_ge(pbz, j + 1)

                def shift_mix(x, dst):
                    i = 'rkv'.index(x)
                    act_j.done(dve, ('p', x, NCH - 1), j)
                    tt(x + '_d', dst[:, :], pb[:, i, 1:TOK + 1], pb[:, i, 2:TOK + 2], ALU.subtract)
                    dve_j.done(dve, x + '_d', j)
                    stt(x, dst[:, :], dst[:, :], pj('mu_' + x), pb[:, i, 2:TOK + 2], ALU.mult, ALU.add)

                pool_j.done(dve, 'vj', j)
                shift_mix('k', k_t)
                dve_j.done(dve, 'k', j)
                dve_j.mark(nc.vector.tensor_scalar(kk[:, :], k_t[:, :], pj('k_k'), None, ALU.mult), 'kkr')
                for c in range(NT):
                    act_j.done(dve, ('z', min(NCH - 1, (TP * (c + 1) - 1) // CH)), j)
                    dve_j.mark(nc.vector.tensor_tensor_scan(cs[:, TP * c:TP * (c + 1)], ones_t.to_broadcast([128, TP]), sg[:, TP * c:TP * (c + 1)],
                                                            0.0, ALU.mult, ALU.add), ('cs', c))
                dve_j.done(dve, ('cs', NT - 1), j)
                tt('csx', tmp[:, :], cs[:, :], sg[:, :], ALU.subtract)
                act_j.done(dve, ('a', NCH - 1), j)
                dve_j.mark(nc.vector.tensor_scalar(pb[:, 1, 2:], a_t[:, :], 1.0, pj('k_a'), ALU.subtract, ALU.mult), 'km')
                dve_j.done(dve, 'km', j)
                stt('kmod', k_t[:, :], pb[:, 1, 2:], 1.0, k_t[:, :], ALU.add, ALU.mult)
                act_j.done(dve, ('n', NCH - 1), j)
                dve_j.mark(nc.vector.tensor_scalar(nrm[:, :], nrm[:, :], 1e-12, None, ALU.max), 'nmax')
                dve_j.done(dve, 'nmax', j)
                dve_j.mark(nc.vector.reciprocal(nrm[:, :], nrm[:, :]), 'nrec')
                dve_j.done(dve, 'nrec', j)
                tt('kk', kk[:, :], kk[:, :], nrm[:, :], ALU.mult)
                dve_j.done(dve, 'kk', j)
                act_j.done(dve, 'E0', j)
                stt('at', ar[:, :, 0, :], chunks(kk[:, :]), -1.0, chunks(e0[:, :]), ALU.mult, ALU.mult)
                tt('ba', tmp[:, :], kk[:, :], a_t[:, :], ALU.mult)
                dve_j.done(dve, 'ba', j)
                tt('bh', bh[:, :], tmp[:, :], e2[:, :], ALU.mult)
                tt('kh', kh[:, :], k_t[:, :], e2[:, :], ALU.mult)
                dve_j.mark(nc.vector.tensor_copy(pc[:, :], chunks(e1[:, :])[:, :, TP - 1]), 'pc')
                shift_mix('r', r_t)
                dve_j.done(dve, 'r', j)
                stt('rkb', rkb[:, :], r_t[:, :], pj('r_k'), k_t[:, :], ALU.mult, ALU.mult)
                tt('rt', ar[:, :, 1, :], chunks(r_t[:, :]), chunks(e1[:, :]), ALU.mult)
                shift_mix('v', v_t)
                for u in range(NU):
                    pe_j.done(dve, ('A', u), j)
                    if u == 0:
                        dve_j.done(dve, 'v', j)
                    tt(('A', u), AT[:, u, :, :], bank[4 + u % 4][0:TP, 0:4 * TP].rearrange("p (m t) -> p m t", m=4), mask4[:, :, :],
                       ALU.mult)
                for l in range(LEVELS):
                    for s in range(NB + 1):
                        if s < NB:
                            pe_j.done(dve, ('P', l, s), j)
                            if l == 0 and s >= 2:
                                dve_j.done(dve, ('T', 0, s - 2), j)
                            elif l == 1 and s < 2:
                                dve_j.done(dve, ('T', 0, 4 - s), j)
                            tt(('P', l, s), P1[:, s % 2, :, :], bank[2 + s % 2][0:TP, 0:4 * TP].rearrange("p (m t) -> p m t", m=4),
                               mlev[:, l, 0:TP].unsqueeze(1).to_broadcast([TP, 4, TP]), ALU.mult)
                        if s > 0:
                            b = s - 1
                            pe_j.done(dve, ('D', l, b), j)
                            if l > 0:
                                dve_j.done(dve, ('R', l - 1, b), j)
                            else:
                                pool_j.done(dve, 'R0', j)
                            for x, m, bk in (('T', Tm, 4), ('R', Rm, 6)):
                                if l == LEVELS - 1 and x == 'T':
                                    continue
                                new = bank[bk + b % 2][0:TP, 0:4 * TP].rearrange("p (m t) -> p m t", m=4)
                                if l == 0 and x == 'T':
                                    new = P1[:, b % 2, :, :]
                                    dve_j.done(dve, ('P', l, b), j)
                                tt((x, l, b), m[:, 4 * b:4 * b + 4, :], new, m[:, 4 * b:4 * b + 4, :], ALU.add)
                for g in range(2):
                    pe_j.done(dve, ('m', g), j)
                    tt(('m', g), mxt[:, 5 * g:5 * g + 5, :], bank[2 + g][:, 0:5 * HS].rearrange("p (c n) -> p c n", n=HS),
                       id2.unsqueeze(1).to_broadcast([128, 5, HS]), ALU.add)
                for g in range(2):
                    pe_j.done(dve, ('nn', g), j)
                    tt(('nn', g), np_[:, 5 * g:5 * g + 5, :], bank[4 + g][:, 0:5 * HS].rearrange("p (c n) -> p c n", n=HS),
                       pc[:, 5 * g:5 * g + 5].unsqueeze(2).to_broadcast([128, 5, HS]), ALU.mult)
                dve_j.mark(nc.vector.memset(S[:, 0, :], 0.0), 'S0')
                dve_j.done(dve, ('nn', 0), j)
                dve_j.mark(nc.vector.tensor_copy(S[:, 1, :], np_[:, 0, :]), ('S', 0))
                for c in range(1, NT):
                    pe_j.done(dve, ('s', c), j)
                    if c == 5:
                        dve_j.done(dve, ('nn', 1), j)
                    stt(('S', c), S[:, c + 1, :], bank[6 + c % 2][:, 0:HS], pc[:, c:c + 1], np_[:, c, :], ALU.mult, ALU.add)
                for g in range(2):
                    pe_j.done(dve, ('u', g), j)
                    for h in range(2):
                        tt(('u', g, h), U.rearrange("p (c h) n -> p c h n", h=2)[:, 5 * g:5 * g + 5, h, :],
                           bank[2 + 2 * g + h][0:TP, 0:5 * HS].rearrange("p (c n) -> p c n", n=HS),
                           X.rearrange("p (c h) n -> p c h n", h=2)[:, 5 * g:5 * g + 5, h, HS:128], ALU.add)
                for c in range(NCH):
                    pe_j.done(dve, ('bs', c), j)
                    tt(('bo', c), kk[:, CH * c:CH * (c + 1)], bank[2 + c][:, 0:CH], v_t[:, CH * c:CH * (c + 1)], ALU.mult)
                for c in range(NCH):
                    pe_j.done(dve, ('mean', c), j)
                    stt(('yc', c), y_t[:, CH * c:CH * (c + 1)], bank[2 + c][:, 0:CH], -1.0 / HS, y_t[:, CH * c:CH * (c + 1)],
                        ALU.mult, ALU.add)
                act_j.done(dve, ('var', NCH - 1), j)
                nc.vector.memset(dz[:, 3:4], 0.0).then_inc(late_free, 1)
                dve_j.mark(nc.vector.reciprocal(nrm[:, :], nrm[:, :]), 'yrec')
                dve_j.done(dve, 'yrec', j)
                tt('yn', y_t[:, :], y_t[:, :], nrm[:, :], ALU.mult)
                dve_j.done(dve, 'yn', j)
                dve_j.mark(nc.vector.tensor_scalar(y_t[:, :], y_t[:, :], pj('lnx_g'), pj('lnx_b'), ALU.mult, ALU.add), 'yaff')
                dve_j.done(dve, 'yaff', j)
                tt('ysum', y_t[:, :], y_t[:, :], kk[:, :], ALU.add)
                dve_j.done(dve, 'ysum', j)
                for c in range(NCH):
                    pe_j.done(dve, ('g', c), j)
                    tt(('yg', c), yg[:, bass.ds(j, 1), CH * c:CH * (c + 1)].rearrange("p a t -> p (a t)"),
                       bank[(0, 1, 6, 7)[c]][:, 0:CH], y_t[:, CH * c:CH * (c + 1)], ALU.mult)
                nc.vector.memset(dz[:, 0:1], 0.0).then_inc(col_free, 1)
            nc.vector.memset(cpb[:, :, 0:2], 0.0).then_inc(conv_step, 2)
            nc.vector.memset(dz[:, 1:2], 0.0).then_inc(conv_step, 4)
            with dve.Fori(0, NJ) as j:
                dve.wait_ge(conv_ev, j * 12 + 12)
                nc.vector.tensor_tensor(cpb[:, 1, 2:], cpb[:, 1, 2:], cpb[:, 2, 2:], ALU.mult).then_inc(conv_step, 1)
                dve.wait_ge(conv_step, j * 6 + 7)
                for w in range(3):
                    scal = vec[:, VEC['conv_w'] + 4 * w:VEC['conv_w'] + 4 * w + 4][:, bass.ds(j, 1)]
                    if w == 0:
                        ins = nc.vector.tensor_scalar(c1[:, :], cpb[:, 1, 0:TOK], scal, None, ALU.mult)
                    else:
                        ins = nc.vector.scalar_tensor_tensor(out=c1[:, :], in0=cpb[:, 1, w:w + TOK], scalar=scal, in1=c1[:, :],
                                                             op0=ALU.mult, op1=ALU.add)
                    ins.then_inc(conv_step, 1)
                    dve.wait_ge(conv_step, j * 6 + 8 + w)
                nc.vector.tensor_tensor(cv[:, bass.ds(j, 1), :].rearrange("p a t -> p (a t)"), cpb[:, 0, 2:], c1[:, :], ALU.mult
                                        ).then_inc(conv_step, 2)
            nc.vector.memset(dz[:, 2:3], 0.0).then_inc(gate_mul, 6)
            with dve.Fori(0, KT) as d:
                for c in range(NCH):
                    s = c % 2
                    dve.wait_ge(gate_sig, d * 8 + 2 * c + 2)
                    for m in range(2):
                        nc.vector.tensor_tensor(gt[:, s, m, :], gt[:, s, m, :], bank[4 * s + 2 + m][:, 0:CH], ALU.mult
                                                ).then_inc(gate_mul, 1)
                    dve.wait_ge(gate_mul, d * 12 + 3 * c + 8)
                    nc.vector.tensor_tensor(mT[:, bass.ds(d, 1), CH * c:CH * (c + 1)].rearrange("p a t -> p (a t)"),
                                            gt[:, s, 0, :], gt[:, s, 1, :], ALU.add).then_inc(gate_mul, 1)
            dve.wait_ge(h_in, 16 * (NT + 1))
            for t in range(NT):
                for n in range(2):
                    dve.wait_ge(wo_ps, 2 * t + n + 1)
                    nc.vector.tensor_tensor(h_all[:, t, 512 * n:512 * (n + 1)], bank[2 * (t % 2) + n][0:TP, :],
                                            h_all[:, t, 512 * n:512 * (n + 1)], ALU.add).then_inc(wo_add, 1)

        def on_tensor(pe):
            pe.wait_ge(pool_c, 2)
            pe.wait_ge(vec_in, 16 * 15)
            nc.tensor.transpose(bank[7][:, 0:84], vrows[:, :], ident[0:84, 0:84]).then_inc(vec_ps, 1)
            for t in range(NT):
                pe.wait_ge(xn_done, t + 1)
                if t >= 2:
                    pe.wait_ge(xnT_done, 2 * (t - 1))
                for k in range(KT):
                    ins = nc.tensor.transpose(bank[2 * (t % 2) + k // 4][:, (k % 4) * TP:(k % 4 + 1) * TP],
                                              xn[:, t % 2, 128 * k:128 * (k + 1)], ident[0:TP, 0:TP])
                ins.then_inc(xnT_ps, 1)
            pe.wait_ge(xnT_done, 2 * NT)
            pe.wait_ge(lmu_done, 3)
            for m in range(2):
                for c in range(NCH):
                    if 4 * m + c >= 2:
                        pe.wait_ge(lora_ev, 2 * (4 * m + c) - 2)
                    for w, b in ((lraw, 0), (lmu, 2)):
                        for k in range(KT):
                            ins = nc.tensor.matmul(bank[b + c % 2][:, 0:CH], w[:, k, 128 * m:128 * (m + 1)],
                                                   xnT[:, k, CH * c:CH * (c + 1)], start=k == 0, stop=k == KT - 1)
                    ins.then_inc(lora_ps, 1)
            pe.wait_ge(lora_done, 3)

            def mm(ps, lhsT, rhs, start=True, stop=True):
                return nc.tensor.matmul(ps, lhsT, rhs, start=start, stop=stop)

            def hp(h):
                return slice(HS * h, HS * (h + 1))

            def tp(c):
                return slice(TP * c, TP * (c + 1))

            def project_keys():
                for c in range(NCH):
                    for k in range(KT):
                        ins = mm(bank[2 + c][:, 0:CH], ring[:, 1, k, :], xnT[:, k, CH * c:CH * (c + 1)], k == 0, k == KT - 1)
                    ins.then_inc(k_ps, 1)

            pe.wait_ge(ring_in[1], 16)
            project_keys()
            with pe.Fori(0, NJ) as j:
                pool_j.done(pe, 'wg2', j)
                pe.wait_ge(col_free, j + 1)
                for c in range(NCH):
                    if c >= 2:
                        act_j.done(pe, ('a', c - 2), j)
                    mm(bank[c % 2][:, 0:CH], w2j[0:64, :], lw[0:64, CH * c:CH * (c + 1)])
                    pe_j.mark(mm(bank[6 + c % 2][:, 0:CH], w2j[64:128, :], lw[64:128, CH * c:CH * (c + 1)]), ('z', c))
                for q in range(2 * NCH):
                    x, c = 'rv'[q // NCH], q % NCH
                    if c == 0:
                        pe.wait_ge(ring_in['rkv'.index(x)], j * 16 + 16)
                    if q < 2:
                        act_j.done(pe, ('z', 2 + c), j)
                    else:
                        act_j.done(pe, ('p', 'rv'[(q - 2) // NCH], (q - 2) % NCH), j)
                    for k in range(KT):
                        ins = mm(bank[c % 2][:, 0:CH], ring[:, 'rkv'.index(x), k, :], xnT[:, k, CH * c:CH * (c + 1)], k == 0, k == KT - 1)
                    pe_j.mark(ins, ('p', x, c))
                    if q == 1:
                        act_j.done(pe, 'sq', j)
                        for b in range(NCH):
                            pe_j.mark(mm(bank[4 + b][:, 0:CH], bones[:, :], nrm[:, CH * b:CH * (b + 1)]), ('n', b))
                dve_j.done(pe, 'bh', j)
                q = 0
                for x in TA:
                    if x == 'v':
                        dve_j.done(pe, 'v', j)
                    for g, (g0, g1) in enumerate(evac_groups()):
                        if q >= 2:
                            act_j.done(pe, ('t', TA[(q - 2) // 3], (q - 2) % 3), j)
                        for c in range(g0, g1):
                            src = dict(v=v_t, b=bh, k=kh)[x][:, tp(c)] if x != 'a' else ar[:, c, 0, :]
                            ins = nc.tensor.transpose(bank[2 + q % 2][0:TP, 128 * (c - g0):128 * (c - g0 + 1)], src, ident[:, :])
                        pe_j.mark(ins, ('t', x, g))
                        q += 1
                for u in range(NU):
                    c, h = u // 2, u % 2
                    if u >= 4:
                        dve_j.done(pe, ('A', u - 4), j)
                    b = bank[4 + u % 4]
                    mm(b[0:TP, 0:2 * TP], bh[hp(h), tp(c)], ar[hp(h), c, :, :].rearrange("p m t -> p (m t)"))
                    pe_j.mark(mm(b[0:TP, 2 * TP:4 * TP], kh[hp(h), tp(c)], ar[hp(h), c, :, :].rearrange("p m t -> p (m t)")),
                              ('A', u))
                dve_j.done(pe, ('A', NU - 1), j)
                act_j.done(pe, ('t', 'v', 2), j)
                pool_j.done(pe, 'R0', j)
                for l in range(LEVELS):
                    for s in range(NB + 1):
                        if s < NB:
                            if l > 0:
                                dve_j.done(pe, ('T', l - 1, s), j)
                                if s < 2:
                                    dve_j.done(pe, ('P', l - 1, 4 - s), j)
                            if s >= 2:
                                dve_j.done(pe, ('P', l, s - 2), j)
                            for m in range(4):
                                u = 4 * s + m
                                ins = mm(bank[2 + s % 2][0:TP, TP * m:TP * (m + 1)], AT[:, u, 0, :], Tm[:, u, :])
                            pe_j.mark(ins, ('P', l, s))
                        if s > 0:
                            b = s - 1
                            dve_j.done(pe, ('P', l, b), j)
                            if b >= 2:
                                dve_j.done(pe, ('R', l, b - 2), j)
                            elif l > 0:
                                dve_j.done(pe, ('R', l - 1, 4 - b), j)
                            for m in range(4):
                                u = 4 * b + m
                                if 0 < l < LEVELS - 1:
                                    mm(bank[4 + b % 2][0:TP, TP * m:TP * (m + 1)], Rm[:, u, :], P1[:, b % 2, m, :])
                                ins = mm(bank[6 + b % 2][0:TP, TP * m:TP * (m + 1)], P1[:, b % 2, m, :], Rm[:, u, :])
                            pe_j.mark(ins, ('D', l, b))
                dve_j.done(pe, ('R', LEVELS - 1, NB - 1), j)
                for g, (g0, g1) in enumerate(((0, 8), (8, 16), (16, 20))):
                    if g == 2:
                        act_j.done(pe, ('xa', 0), j)
                    for u in range(g0, g1):
                        ins = mm(bank[2 + g % 2][0:TP, HS * (u - g0):HS * (u - g0 + 1)], AT[:, u, 2, :], Vt[:, u // 2, hp(u % 2)])
                    pe_j.mark(ins, ('xa', g))
                for g, (g0, g1) in enumerate(evac_groups()):
                    if g == 2:
                        act_j.done(pe, ('xc', 0), j)
                    for c in range(g0, g1):
                        for h in range(2):
                            ins = mm(bank[4 + g % 2][hp(h), TP * (c - g0):TP * (c - g0 + 1)], X[:, 2 * c + h, 0:HS],
                                     Rm[:, 2 * c + h, :])
                    pe_j.mark(ins, ('xc', g))
                act_j.done(pe, ('xa', 2), j)
                for g in range(5):
                    if g >= 2:
                        act_j.done(pe, ('xb', g - 2), j)
                    for m in range(4):
                        u = 4 * g + m
                        ins = mm(bank[6 + g % 2][0:TP, 128 * m:128 * (m + 1)], Rm[:, u, :], X[:, u, :])
                    pe_j.mark(ins, ('xb', g))
                act_j.done(pe, ('xb', 4), j)
                for g in range(2):
                    for c in range(5 * g, 5 * g + 5):
                        for h in range(2):
                            ins = mm(bank[2 + g][hp(h), HS * (c % 5):HS * (c % 5 + 1)], X[:, 2 * c + h, 0:HS], Bt[:, c, hp(h)])
                    pe_j.mark(ins, ('m', g))
                for g in range(2):
                    for c in range(5 * g, 5 * g + 5):
                        for h in range(2):
                            o = bank[4 + g][hp(h), HS * (c % 5):HS * (c % 5 + 1)]
                            mm(o, Bt[:, c, hp(h)], X[:, 2 * c + h, HS:128], True, False)
                            ins = mm(o, Kt[:, c, hp(h)], Vt[:, c, hp(h)], False, True)
                    pe_j.mark(ins, ('nn', g))
                dve_j.done(pe, ('m', 1), j)
                for c in range(1, NT):
                    dve_j.done(pe, ('S', c - 1), j, pe_passed)
                    for h in range(2):
                        ins = mm(bank[6 + c % 2][hp(h), 0:HS], mxt[hp(h), c, :], S[hp(h), c, :])
                    pe_j.mark(ins, ('s', c))
                dve_j.done(pe, ('nn', 1), j)
                for g in range(2):
                    for c in range(5 * g, 5 * g + 5):
                        for h in range(2):
                            ins = mm(bank[2 + 2 * g + h][0:TP, HS * (c % 5):HS * (c % 5 + 1)], x1t[hp(h), c, :], S[hp(h), c, :])
                    pe_j.mark(ins, ('u', g))
                dve_j.done(pe, ('u', 1, 1), j, pe_passed)
                for g, (g0, g1) in enumerate(evac_groups()):
                    if g == 2:
                        act_j.done(pe, ('y', 0), j, pe_passed)
                    for c in range(g0, g1):
                        for h in range(2):
                            u = 2 * c + h
                            o = bank[6 + g % 2][hp(h), TP * (c - g0):TP * (c - g0 + 1)]
                            mm(o, S[hp(h), c, :], ar[hp(h), c, 1, :], True, False)
                            mm(o, U[:, u, :], AT[:, u, 1, :], False, False)
                            ins = mm(o, Vt[:, c, hp(h)], AT[:, u, 3, :], False, True)
                    pe_j.mark(ins, ('y', g))
                for c in range(NCH):
                    pe_j.mark(mm(bank[2 + c][:, 0:CH], bones[:, :], rkb[:, CH * c:CH * (c + 1)]), ('bs', c))
                act_j.done(pe, ('y', 2), j)
                for c in range(NCH):
                    pe_j.mark(mm(bank[(0, 1, 6, 7)[c]][:, 0:CH], wg2j[:, :], lg[:, CH * c:CH * (c + 1)]), ('g', c))
                for c in range(NCH):
                    dve_j.done(pe, ('bo', c), j)
                    pe_j.mark(mm(bank[2 + c][:, 0:CH], bones[:, :], y_t[:, CH * c:CH * (c + 1)]), ('mean', c))
                act_j.done(pe, 'ysq', j)
                for c in range(NCH):
                    if c >= 2:
                        act_j.done(pe, ('var', c - 2), j)
                    pe_j.mark(mm(bank[4 + c % 2][:, 0:CH], bones[:, :], tmp[:, CH * c:CH * (c + 1)]), ('var', c))
                pe.wait_ge(late_free, j + 1)
                pe.wait_ge(ring_in[1], j * 16 + 32)
                project_keys()
            pe.wait_ge(col_free, NJ + 1)
            with pe.Fori(0, NJ) as j:
                for i in range(3):
                    pe.wait_ge(ring_in[i], j * 16 + 16 + 16 * NJ)
                    for c in range(NCH):
                        if 4 * i + c >= 2:
                            pe.wait_ge(conv_ev, j * 12 + 4 * i + c - 1)
                        for k in range(KT):
                            ins = mm(bank[c % 2][:, 0:CH], ring[:, i, k, :], xnT[:, k, CH * c:CH * (c + 1)], k == 0, k == KT - 1)
                        ins.then_inc(conv_ps, 1)
                pe.wait_ge(conv_ev, j * 12 + 12)
            pe.wait_ge(conv_step, 6 * NJ + 6)
            with pe.Fori(0, KT) as d:
                for i in range(2):
                    pe.wait_ge(ring_in[i], d * 16 + 16 + 32 * NJ)
                pe.wait_ge(ring_in[2], d * 32 + 32 + 32 * NJ)
                for c in range(NCH):
                    b = 4 * (c % 2)
                    pe.wait_ge(gate_mul, d * 12 + 3 * c + 3)
                    t = slice(CH * c, CH * (c + 1))
                    for i in range(2):
                        for k in range(KT):
                            mm(bank[b + i][:, 0:CH], ring[:, i, k, :], xnT[:, k, t], k == 0, k == KT - 1)
                    for i, src in enumerate((yg, cv)):
                        for k in range(4):
                            ins = mm(bank[b + 2 + i][:, 0:CH], ring[:, 2, 4 * i + k, :], src[:, k, t], k == 0, k == 3)
                    ins.then_inc(gate_ps, 1)
            pe.wait_ge(gate_mul, 12 * KT + 6)
            pe.wait_ge(wo_in, 16)
            for t in range(NT):
                for n in range(2):
                    if t >= 2:
                        pe.wait_ge(wo_add, 2 * (t - 2) + n + 1)
                    for k in range(KT):
                        ins = mm(bank[2 * (t % 2) + n][0:TP, :], mT[:, k, tp(t)], wo_t[:, k, 512 * n:512 * (n + 1)], k == 0, k == KT - 1)
                    ins.then_inc(wo_ps, 1)



    return on_sync, on_gpsimd, on_scalar, on_vector, on_tensor


def experts_program(nc, ctx, a, bank, shared, out):
    f32 = mybir.dt.float32
    f32r = mybir.dt.float32r
    u32 = mybir.dt.uint32
    ALU = mybir.AluOpType
    ACT = mybir.ActivationFunctionType
    AX = mybir.AxisListType

    D = 1024
    META = 16
    TOK = 1040
    NT = 10
    TP = TOK // NT
    KT = D // 128
    E = 32
    TOPK = 4
    LIMIT = 7.0
    ALPHA = 1.702
    EPS = 1e-5
    ROWS = 128
    MAXR = E + TOK * TOPK // (2 * ROWS) + 1
    MAXB = shared['blocks']
    HK, HC = 4, 512
    NPIECE = 12
    NRING = 4

    if True:
        ident, eps_t, h_all, zero_out, wo_add = shared['ident'], shared['eps_t'], shared['h_all'], shared['zero_out'], shared['wo_add']
        ln2_g, w_router, b_router, lnf_g = a['ln2_g'], a['w_router'], a['b_router'], a['lnf_g']
        w_gate, b_gate, w_up, b_up, w_down, b_down = (a[x] for x in ('w_e_gate', 'b_e_gate', 'w_e_up', 'b_e_up', 'w_e_down', 'b_e_down'))
        hn_d, ys_d, rowtok_d, bias_d = shared['hn_d'], shared['ys_d'], shared['rowtok_d'], shared['bias_d']

        def sem(name):
            return ctx.enter_context(nc.semaphore(name))


        gate_ps, up_ps, y_ps, tx_ps, ta_ps = bank[0:2], bank[2:4], (bank[4:6], bank[2:4]), bank[6], bank[7]

        sb = Plan(nc, shared['after_h'])
        gates, dest = shared["gates"], shared["dest"]
        tok_id = sb("tok_id", [TP, NT], u32)
        table = sb("table", [1, MAXR + 2], u32)
        starts = sb("starts", [1, MAXR + 2], u32)
        kind_row = sb("kind_row", [6, 3, ROWS], f32r)
        fss = sb("fss", [TP, NT])
        frs = sb("frs", [TP, NT])

        dump = sb("dump_e", [128, 16])

        if True:
            rt = Plan(nc, sb.at)
            hn = rt("hn", [TP, 2, D])
            junk = rt("junk_e", [TP, D])
            g2_b = rt("g2_b", [TP, D])
            bias_rows = rt("bias_rows", [E, 3, D])
            bias_hi = rt("bias_hi", [E, 3, D], f32r)
            bias_lo = rt("bias_lo", [E, 3, D], f32r)
            kind_f = rt("kind_f", [6, 3, ROWS])
            wr_t = rt("wr_t", [128, KT, E])
            hnT = rt("hnT", [128, 2, KT, TP])
            ss = rt("ss_e", [TP, NT])
            rstd = rt("rstd_e", [TP, NT])
            top_v = rt("top_v", [TP, NT, 8])
            top_i = rt("top_i", [TP, NT, 8], u32)
            lg = rt("lg", [TP, 2, E])
            br_b = rt("br_b", [TP, E])
            iota_e = rt("iota_e", [TP, E])
            onehot = rt("onehot", [TP, NT * TOPK, E])
            chosen = rt("chosen", [TP, NT, E])
            before = rt("before", [TP, NT + 1, E])
            rank = rt("rank", [TP, NT, E])
            tri = rt("tri", [TP, TP])
            ones = rt("ones", [TP, 128])
            top_f = rt("top_f", [TP, NT * TOPK])
            cnt = rt("cnt", [TP, E])
            over = rt("over", [TP, E])
            pairs = rt("pairs", [TP, E])
            pair_end = rt("pair_end", [TP, E])
            pair_rows = rt("pair_rows", [TP, E])
            pair_base = rt("pair_base", [TP, E])
            singles = rt("singles", [TP, E])
            single_end = rt("single_end", [TP, E])
            single_base = rt("single_base", [TP, E])
            in_single = rt("in_single", [TP, NT, E])
            dest_f = rt("dest_f", [TP, NT * TOPK])
            gsum = rt("gsum", [TP, NT])
            iota_q = rt("iota_q", [1, MAXR + 1])
            ended = rt("ended", [1, MAXR + 1, E])
            table_f = rt("table_f", [1, MAXR + 1])
            table_s = rt("table_s", [1, MAXR + 1])
            start_f = rt("start_f", [1, MAXR + 1])
            total_f = rt("total_f", [1, 1])

        if True:
            ex = Plan(nc, sb.at)
            raw = ex("raw", [128, NRING, HK, HC])
            w_hi = ex("w_hi", [128, NRING, HK, HC], f32r)
            w_lo = ex("w_lo", [128, NRING, HK, HC], f32r)
            x_rows = ex("x_rows", [ROWS, 2, D])
            x_hi = ex("x_hi", [128, 2, KT, ROWS], f32r)
            x_lo = ex("x_lo", [128, 2, KT, ROWS], f32r)
            g_t = ex("g_t", [ROWS, 2, HC])
            s_t = ex("s_t", [ROWS, 2, HC])
            u_t = ex("u_t", [ROWS, 2, HC])
            a_hi = ex("a_hi", [128, 2, KT, ROWS], f32r)
            a_lo = ex("a_lo", [128, 2, KT, ROWS], f32r)
            y_rows = ex("y_rows", [ROWS, 2, D])
            bias_t = ex("bias_t", [6, D], f32r)
            idx_t = ex("idx_t", [ROWS, 2], u32)
            assert ex.at <= 229344, ex.at

        if True:
            fi = Plan(nc, sb.at)
            y_got = fi("y_got", [TP, 2, TOPK, D])
            fin_junk = fi("fin_junk", [TP, D])
            gf_b = fi("gf_b", [TP, D])
            fin = fi("fin", [TP, 2, D])

        const_in = sem("const_in")
        bias_in = sem("bias_in")
        pool_const = sem("pool_const")
        dve_const = sem("dve_const")
        sq_done = sem("sq_done")
        std_done = sem("std_done")
        rstd_done = sem("rstd_done")
        hn_done = sem("hn_done")
        hn_out = [sem("hn_out0"), sem("hn_out1")]
        hnT_ps = sem("hnT_ps")
        hnT_done = sem("hnT_done")
        logit_ps = sem("logit_ps")
        lg_read = sem("lg_read")
        top_done = sem("top_done")
        route = sem("route")
        gexp_in = sem("gexp_in")
        gexp_done = sem("gexp_done")
        chosen_done = sem("chosen_done")
        rank_ps = sem("rank_ps")
        dest_done = sem("dest_done")
        table_done = sem("table_done")
        scattered = sem("scattered")
        bias_hi_done = sem("bias_hi_done")
        bias_lo_done = sem("bias_lo_done")
        bias_out = sem("bias_out")
        kind_done = sem("kind_done")

        def sems(name, n):
            return [sem(f"{name}{i}") for i in range(n)]

        raw_in = sems("raw_in", NRING)
        hi_done = sem("hi_done")
        lo_done = sem("lo_done")
        piece_used = sem("piece_used")
        bias_got = sem("bias_got")
        gu_read = sems("gu_read", 2)
        sig_done = sems("sig_done", 2)
        glu_mid = sems("glu_mid", 2)
        glu_done = sems("glu_done", 2)
        aT_ps = sems("aT_ps", 2)
        ahi_done = sems("ahi_done", 2)
        alo_done = sems("alo_done", 2)
        y_read = sems("y_read", 2)
        pe_passed = sem("pe_passed_e")
        idx_in = sems("idx_in", 2)
        rows_in = sems("rows_in", 2)
        xT_ps = sems("xT_ps", 4)
        xhi_done = sems("xhi_done", 4)
        xlo_done = sems("xlo_done", 4)
        sp_passed = sem("sp_passed_e")
        pool_passed = sem("pool_passed_e")
        y_out = sem("y_out")

        gf_in = sem("gf_in")
        got_in = [sem("got_in0"), sem("got_in1")]
        sum_done = sem("sum_done")
        fsq_done = sem("fsq_done")
        fstd_done = sem("fstd_done")
        frs_done = sem("frs_done")
        fin_done = sem("fin_done")
        out_done = [sem("out_done0"), sem("out_done1")]


        def piece_of(j):
            if j < 8:
                return (w_gate, w_up)[j // 2 % 2], HK * (j % 2), HC * (j // 4)
            return w_down, HK * ((j - 8) // 2), HC * (j % 2)

        def on_sync(sp):
            sp.wait_ge(wo_add, 2 * NT)
            sp.dma_start(g2_b, ln2_g.partition_broadcast(TP)).then_inc(const_in, 16)
            sp.dma_start(br_b, b_router.partition_broadcast(TP)).then_inc(const_in, 16)
            sp.dma_start(wr_t, w_router.rearrange("(k p) e -> p k e", p=128)).then_inc(const_in, 16)
            for a, b in enumerate((b_gate, b_up, b_down)):
                sp.dma_start(bias_rows[:, a, :], b).then_inc(bias_in, 16)
            bias_rows_d = bias_d.rearrange("e (n s) c -> e n s c", s=2)
            sp.wait_ge(bias_hi_done, 1)
            sp.dma_start(bias_rows_d[:, :, 0, :], bias_hi.bitcast(f32)).then_inc(bias_out, 16)
            sp.wait_ge(bias_lo_done, 1)
            sp.dma_start(bias_rows_d[:, :, 1, :], bias_lo.bitcast(f32)).then_inc(bias_out, 16)
            for t in range(NT):
                sp.wait_ge(hn_done, t + 1)
                sp.dma_start(hn_d[TP * t:TP * (t + 1), :], hn[:, t % 2, :]).then_inc(hn_out[t % 2], 16)
            sp.wait_ge(table_done, 1)
            n_pairs = sp.value_load(starts[0:1, MAXR + 1:MAXR + 2], min_val=1, max_val=E)
            rounds = sp.value_load(table[0:1, MAXR + 1:MAXR + 2], min_val=2, max_val=MAXR - 1)
            sp.wait_ge(hn_out[0], 16 * (NT // 2))
            sp.wait_ge(hn_out[1], 16 * (NT // 2))

            sp.wait_ge(bias_out, 32)

            def load(e_reg, n, j):
                w, k0, c0 = piece_of(j)
                sp.wait_ge(lo_done, n + 1)
                sp.sem_inc(sp_passed, 1)
                sp.dma_start(raw[:, j % NRING, :, :],
                             w[bass.ds(e_reg, 1), k0 * 128:(k0 + HK) * 128, c0:c0 + HC].rearrange("a (k p) c -> p (a k) c", p=128)
                             ).then_inc(raw_in[j % NRING], 16)

            e0 = sp.value_load(table[0:1, 0:1], min_val=0, max_val=E - 1)
            for j in range(NRING):
                load(e0, j, j)
            for first, last in ((0, n_pairs), (n_pairs, rounds)):
                with sp.Fori(first, last) as r:
                    e = sp.value_load(table[0:1, bass.ds(r, 1)], min_val=0, max_val=E - 1)
                    e_next = sp.value_load(table[0:1, bass.ds(r + 1, 1)], min_val=0, max_val=E - 1)
                    for j in range(NRING, NPIECE + NRING):
                        load(e if j < NPIECE else e_next, r * NPIECE + j, j % NPIECE)
            sp.wait_ge(piece_used, rounds * NPIECE + NRING)
            sp.sem_inc(sp_passed, 1)
            sp.dma_start(gf_b, lnf_g.partition_broadcast(TP)).then_inc(gf_in, 16)
            for t in range(NT):
                sp.wait_ge(fin_done, t + 1)
                if t == 0:
                    sp.dma_start(out[0:TP - META, :], fin[META:TP, 0, :]).then_inc(out_done[0], 16)
                else:
                    sp.dma_start(out[TP * t - META:TP * (t + 1) - META, :], fin[:, t % 2, :]).then_inc(out_done[t % 2], 16)
            sp.wait_ge(out_done[0], 16 * (NT // 2))
            sp.wait_ge(out_done[1], 16 * (NT // 2))

        def on_gpsimd(pool):
            pool.wait_ge(wo_add, 2 * NT)
            nc.gpsimd.memset(tri, 1.0).then_inc(pool_const, 1)
            pool.wait_ge(pool_const, 1)
            nc.gpsimd.affine_select(out=tri, in_=tri, compare_op=ALU.is_gt, fill=0.0, base=0,
                                    pattern=[[1, TP]], channel_multiplier=-1).then_inc(pool_const, 1)
            nc.gpsimd.iota(tok_id[:, :], pattern=[[TP, NT]], base=0, channel_multiplier=1).then_inc(pool_const, 1)
            nc.gpsimd.iota(iota_e, pattern=[[1, E]], base=0, channel_multiplier=0,
                           allow_small_or_imprecise_dtypes=True).then_inc(pool_const, 1)
            nc.gpsimd.iota(iota_q, pattern=[[1, MAXR + 1]], base=0, channel_multiplier=0,
                           allow_small_or_imprecise_dtypes=True).then_inc(pool_const, 1)
            nc.gpsimd.memset(kind_f, 1.0).then_inc(pool_const, 1)
            pool.wait_ge(pool_const, 6)
            nc.gpsimd.affine_select(out=kind_f, in_=kind_f, compare_op=ALU.is_ge, fill=0.0, base=0,
                                    pattern=[[-2, 3], [0, ROWS]], channel_multiplier=1).then_inc(pool_const, 1)
            pool.wait_ge(pool_const, 7)
            nc.gpsimd.affine_select(out=kind_f, in_=kind_f, compare_op=ALU.is_ge, fill=0.0, base=1,
                                    pattern=[[2, 3], [0, ROWS]], channel_multiplier=-1).then_inc(pool_const, 1)
            pool.wait_ge(zero_out, shared['zeroed'])
            pool.wait_ge(dest_done, 1)
            pool.wait_ge(pool_const, 5)
            for t in range(NT):
                for k in range(TOPK):
                    a = t * TOPK + k
                    nc.gpsimd.indirect_dma_start(out=rowtok_d, out_offset=bass.IndirectOffsetOnAxis(ap=dest[:, a:a + 1], axis=0),
                                                 in_=tok_id[:, t:t + 1], in_offset=None).then_inc(scattered, 16)
            pool.wait_ge(table_done, 1)
            n_pairs = pool.value_load(starts[0:1, MAXR + 1:MAXR + 2], min_val=1, max_val=E)
            rounds = pool.value_load(table[0:1, MAXR + 1:MAXR + 2], min_val=2, max_val=MAXR - 1)
            pool.wait_ge(scattered, 16 * NT * TOPK)
            pool.wait_ge(hn_out[0], 16 * (NT // 2))
            pool.wait_ge(hn_out[1], 16 * (NT // 2))

            pool.wait_ge(bias_out, 32)

            def gather(r, tiles):
                start = pool.value_load(starts[0:1, bass.ds(r, 1)], min_val=0, max_val=(MAXB - 2) * ROWS)
                for b in range(tiles):
                    pool.dma_start(idx_t[:, b:b + 1], rowtok_d[bass.ds(start + b * ROWS, ROWS), :]).then_inc(idx_in[b], 16)
                for b in range(tiles):
                    pool.wait_ge(idx_in[b], r * 16 + 16)
                    pool.sem_inc(pool_passed, 1)
                    nc.gpsimd.indirect_dma_start(out=x_rows[:, b, :], out_offset=None, in_=hn_d,
                                                 in_offset=bass.IndirectOffsetOnAxis(ap=idx_t[:, b:b + 1], axis=0)
                                                 ).then_inc(rows_in[b], 16)

            def get_biases(r):
                e = pool.value_load(table[0:1, bass.ds(r, 1)], min_val=0, max_val=E - 1)
                pool.dma_start(bias_t, bias_d[bass.ds(e, 1), :, :].rearrange("a n c -> (a n) c")).then_inc(bias_got, 16)

            gather(0, 2)
            get_biases(0)
            for first, last, tiles in ((0, n_pairs, 2), (n_pairs, rounds, 1)):
                with pool.Fori(first, last) as r:
                    for b in range(tiles):
                        pool.wait_ge(rows_in[b], r * 16 + 16)
                    pool.wait_ge(xT_ps[2 * tiles - 1], r + 1)
                    gather(r + 1, tiles)
                    pool.wait_ge(piece_used, r * NPIECE + 10 + NRING)
                    pool.sem_inc(pool_passed, 1)
                    get_biases(r + 1)
            pool.wait_ge(y_out, rounds * 16 + 16)
            pool.wait_ge(bias_got, rounds * 16 + 16)
            pool.wait_ge(lo_done, rounds * NPIECE + NRING + NRING)
            pool.sem_inc(pool_passed, 1)
            for t in range(NT):
                if t >= 2:
                    pool.wait_ge(sum_done, TOPK * (t - 1))
                for k in range(TOPK):
                    a = t * TOPK + k
                    nc.gpsimd.indirect_dma_start(out=y_got[:, t % 2, k, :], out_offset=None, in_=ys_d,
                                                 in_offset=bass.IndirectOffsetOnAxis(ap=dest[:, a:a + 1], axis=0)
                                                 ).then_inc(got_in[t % 2], 16)

        def on_scalar(act):
            for t in range(NT):
                act.wait_ge(wo_add, 2 * NT)
                if t >= 1:
                    act.wait_ge(sq_done, t)
                nc.scalar.activation(junk, h_all[:, t, :], ACT.Square, accum_out=ss[:, t:t + 1]).then_inc(sq_done, 1)
            act.wait_ge(sq_done, NT)
            nc.scalar.activation(rstd[:, :], ss[:, :], ACT.Sqrt, bias=eps_t[0:TP, :], scale=1.0 / D).then_inc(std_done, 1)
            act.wait_ge(bias_in, 48)
            nc.scalar.activation(bias_hi, bias_rows, ACT.Copy).then_inc(bias_hi_done, 1)
            act.wait_ge(pool_const, 8)
            nc.scalar.activation(kind_row, kind_f, ACT.Copy).then_inc(kind_done, 1)
            for t in range(NT):
                act.wait_ge(hnT_ps, t + 1)
                if t >= 2:
                    act.wait_ge(logit_ps, t - 1)
                for h in range(2):
                    nc.scalar.activation(hnT[:, t % 2, 4 * h:4 * h + 4, :],
                                         bank[2 + 2 * (t % 2) + h][:, 0:4 * TP].rearrange("p (k t) -> p k t", k=4),
                                         ACT.Copy).then_inc(hnT_done, 1)
            act.wait_ge(gexp_in, 1)
            nc.scalar.activation(gates[:, :, :], gates[:, :, :], ACT.Exp).then_inc(gexp_done, 1)

            act.wait_ge(table_done, 1)
            n_pairs = act.value_load(starts[0:1, MAXR + 1:MAXR + 2], min_val=1, max_val=E)
            rounds = act.value_load(table[0:1, MAXR + 1:MAXR + 2], min_val=2, max_val=MAXR - 1)

            def split_hi(n, use, j):
                act.wait_ge(raw_in[j % NRING], use)
                act.wait_ge(piece_used, n + 1)
                nc.scalar.activation(w_hi[:, j % NRING, :, :], raw[:, j % NRING, :, :], ACT.Copy).then_inc(hi_done, 1)

            def x_hi_part(r, f):
                act.wait_ge(xT_ps[f], r + 1)
                nc.scalar.activation(x_hi[:, f // 2, 4 * (f % 2):4 * (f % 2) + 4, :], tx_ps[:, :].rearrange("p (k s) -> p k s", k=4),
                                     ACT.Copy).then_inc(xhi_done[f], 1)

            def a_hi_part(r, h, t):
                act.wait_ge(aT_ps[t], r * 2 + h + 2)
                nc.scalar.activation(a_hi[:, t, 4 * h:4 * h + 4, :], ta_ps[:, :].rearrange("p (k s) -> p k s", k=4),
                                     ACT.Copy).then_inc(ahi_done[t], 1)

            for f in range(4):
                x_hi_part(0, f)
            for j in range(NRING):
                split_hi(j, 16, j)
            for first, last, tiles in ((0, n_pairs, 2), (n_pairs, rounds, 1)):
                with act.Fori(first, last) as r:
                    for j in range(NPIECE):
                        jn = j + NRING
                        if j in (10, 11):
                            split_hi(r * NPIECE + jn, r * 48 + 16 * (jn // NRING) + 16, jn % NPIECE)
                            if j == 10:
                                act.wait_ge(y_out, r * 16 + 16)
                            act.wait_ge(piece_used, r * NPIECE + j + 1 + NRING)
                            for t in range(tiles):
                                nc.scalar.activation(y_rows[:, t, HC * (j - 10):HC * (j - 9)], y_ps[j - 10][t][:, :], ACT.Copy
                                                     ).then_inc(y_read[t], 1)
                            if j == 10 and tiles == 2:
                                x_hi_part(r + 1, 3)
                            continue
                        split_hi(r * NPIECE + jn, r * 48 + 16 * (jn // NRING) + 16, jn % NPIECE)
                        if j in (1, 5):
                            h = j // 4
                            for t in range(tiles):
                                act.wait_ge(gu_read[t], r * 4 + 2 * h + 3)
                                act.wait_ge(glu_done[t], r * 2 + h + 1)
                                nc.scalar.activation(s_t[:, t, :], g_t[:, t, :], ACT.Sigmoid, scale=ALPHA).then_inc(sig_done[t], 1)
                        if j == 4:
                            a_hi_part(r, 0, 0)
                        if j == 5 and tiles == 2:
                            a_hi_part(r, 0, 1)
                        if 7 <= j < 7 + 2 * tiles:
                            x_hi_part(r + 1, j - 7)
                        if 8 <= j < 8 + tiles:
                            a_hi_part(r, 1, j - 8)
                    for t in range(tiles):
                        act.wait_ge(y_read[t], r * 2 + 3)
                    start = act.value_load(starts[0:1, bass.ds(r, 1)], min_val=0, max_val=(MAXB - 2 - tiles) * ROWS)
                    act.dma_start(ys_d[bass.ds(start, tiles * ROWS), :].rearrange("(b p) d -> p b d", b=tiles),
                                  y_rows[:, 0:tiles, :]).then_inc(y_out, 16)
            for t in range(NT):
                act.wait_ge(sum_done, TOPK * (t + 1))
                if t >= 1:
                    act.wait_ge(fsq_done, t)
                nc.scalar.activation(fin_junk, h_all[:, t, :], ACT.Square, accum_out=fss[:, t:t + 1]).then_inc(fsq_done, 1)
                act.wait_ge(fsq_done, t + 1)
                nc.scalar.activation(frs[:, t:t + 1], fss[:, t:t + 1], ACT.Sqrt, bias=eps_t[0:TP, :], scale=1.0 / D
                                     ).then_inc(fstd_done, 1)

        def on_vector(dve):
            steps = [0]

            def link(ins):
                steps[0] += 1
                ins.then_inc(route, 1)
                dve.wait_ge(route, steps[0])

            dve.wait_ge(wo_add, 2 * NT)
            nc.vector.memset(ones, 1.0).then_inc(dve_const, 1)
            free = [(lo_done, NRING), (piece_used, NRING), (y_out, 16)]
            free += [(s[t], n) for t in range(2) for s, n in ((gu_read, 2), (glu_done, 1), (aT_ps, 1), (alo_done, 1), (y_read, 1))]
            for i, (s, n) in enumerate(free):
                nc.vector.memset(dump[:, i:i + 1], 0.0).then_inc(s, n)
            dve.wait_ge(std_done, 1)
            nc.vector.reciprocal(rstd[:, :], rstd[:, :]).then_inc(rstd_done, 1)
            dve.wait_ge(bias_hi_done, 1)
            nc.vector.tensor_tensor(bias_lo, bias_rows, bias_hi.bitcast(f32), ALU.subtract).then_inc(bias_lo_done, 1)
            dve.wait_ge(rstd_done, 1)
            dve.wait_ge(const_in, 48)
            for t in range(NT):
                if t >= 2:
                    dve.wait_ge(hn_out[t % 2], 16 * (t // 2))
                    dve.wait_ge(hnT_ps, t - 1)
                nc.vector.scalar_tensor_tensor(out=hn[:, t % 2, :], in0=h_all[:, t, :], scalar=rstd[:, t:t + 1], in1=g2_b,
                                               op0=ALU.mult, op1=ALU.mult).then_inc(hn_done, 1)
                if t >= 1:
                    u = t - 1
                    dve.wait_ge(logit_ps, u + 1)
                    nc.vector.tensor_tensor(lg[:, u % 2, :], bank[6 + u % 2][0:TP, 0:E], br_b, ALU.add).then_inc(lg_read, 1)
                    dve.wait_ge(lg_read, u + 1)
                    link(nc.vector.max(top_v[:, u, :], lg[:, u % 2, :]))
                    nc.vector.max_index(top_i[:, u, :], top_v[:, u, :], lg[:, u % 2, :]).then_inc(top_done, 1)
            u = NT - 1
            dve.wait_ge(logit_ps, u + 1)
            nc.vector.tensor_tensor(lg[:, u % 2, :], bank[6 + u % 2][0:TP, 0:E], br_b, ALU.add).then_inc(lg_read, 1)
            dve.wait_ge(lg_read, u + 1)
            link(nc.vector.max(top_v[:, u, :], lg[:, u % 2, :]))
            nc.vector.max_index(top_i[:, u, :], top_v[:, u, :], lg[:, u % 2, :]).then_inc(top_done, 1)
            dve.wait_ge(top_done, NT)
            nc.vector.tensor_tensor(gates[:, :, :], top_v[:, :, 0:TOPK], top_v[:, :, 0:1].to_broadcast([TP, NT, TOPK]),
                                    ALU.subtract).then_inc(gexp_in, 1)
            link(nc.vector.tensor_copy(top_f.rearrange("p (t k) -> p t k", k=TOPK), top_i[:, :, 0:TOPK]))
            dve.wait_ge(pool_const, 5)
            link(nc.vector.tensor_tensor(onehot, iota_e.unsqueeze(1).to_broadcast([TP, NT * TOPK, E]),
                                         top_f.unsqueeze(2).to_broadcast([TP, NT * TOPK, E]), ALU.is_equal))
            link(nc.vector.tensor_reduce(chosen, onehot.rearrange("p (t k) e -> p t e k", k=TOPK), axis=AX.X, op=ALU.add))
            link(nc.vector.memset(before[:, 0, :], 0.0))
            for t in range(NT):
                ins = nc.vector.tensor_tensor(before[:, t + 1, :], before[:, t, :], chosen[:, t, :], ALU.add)
                if t == NT - 1:
                    ins.then_inc(chosen_done, 1)
                else:
                    link(ins)
            dve.wait_ge(gexp_done, 1)
            link(nc.vector.tensor_reduce(gsum, gates[:, :, :], axis=AX.X, op=ALU.add))
            link(nc.vector.reciprocal(gsum, gsum))
            link(nc.vector.tensor_tensor(gates[:, :, :], gates[:, :, :], gsum.unsqueeze(2).to_broadcast([TP, NT, TOPK]),
                                         ALU.mult))
            dve.wait_ge(rank_ps, 2)
            link(nc.vector.tensor_copy(cnt, bank[1][0:TP, 0:E]))
            link(nc.vector.tensor_copy(rank, bank[0][0:TP, 0:NT * E].rearrange("p (t e) -> p t e", e=E)))
            link(nc.vector.tensor_scalar(pairs, cnt, float(ROWS), None, ALU.is_gt))
            for m in range(1, (TOK - ROWS - 1) // (2 * ROWS) + 1):
                link(nc.vector.scalar_tensor_tensor(out=pairs, in0=cnt, scalar=float((2 * m + 1) * ROWS), in1=pairs,
                                                    op0=ALU.is_gt, op1=ALU.add))
            link(nc.vector.tensor_scalar(pair_rows, pairs, float(2 * ROWS), None, ALU.mult))
            link(nc.vector.tensor_tensor(singles, cnt, pair_rows, ALU.is_gt))
            link(nc.vector.memset(over, 1.0))
            link(nc.vector.tensor_tensor_scan(pair_end, over, pairs, 0.0, ALU.mult, ALU.add))
            link(nc.vector.tensor_tensor_scan(single_end, over, singles, 0.0, ALU.mult, ALU.add))
            link(nc.vector.tensor_tensor(pair_base, pair_end, pairs, ALU.subtract))
            link(nc.vector.tensor_scalar(pair_base, pair_base, float(2 * ROWS), None, ALU.mult))
            link(nc.vector.tensor_tensor(single_base, single_end, singles, ALU.subtract))
            link(nc.vector.scalar_tensor_tensor(out=single_base, in0=pair_end[:, E - 1:E].to_broadcast([TP, E]), scalar=2.0,
                                                in1=single_base, op0=ALU.mult, op1=ALU.add))
            link(nc.vector.tensor_scalar(single_base, single_base, float(ROWS), None, ALU.mult))
            link(nc.vector.tensor_tensor(single_base, single_base, pair_rows, ALU.subtract))
            link(nc.vector.tensor_tensor(single_base, single_base, pair_base, ALU.subtract))
            link(nc.vector.tensor_tensor(in_single, rank, pair_rows.unsqueeze(1).to_broadcast([TP, NT, E]), ALU.is_ge))
            link(nc.vector.tensor_tensor(in_single, in_single, single_base.unsqueeze(1).to_broadcast([TP, NT, E]), ALU.mult))
            link(nc.vector.tensor_tensor(rank, rank, in_single, ALU.add))
            link(nc.vector.tensor_tensor(rank, rank, pair_base.unsqueeze(1).to_broadcast([TP, NT, E]), ALU.add))
            oh4 = onehot.rearrange("p (t k) e -> p t k e", k=TOPK)
            for t in range(NT):
                link(nc.vector.tensor_tensor(oh4[:, t, :, :], oh4[:, t, :, :],
                                             rank[:, t, :].unsqueeze(1).to_broadcast([TP, TOPK, E]), ALU.mult))
            link(nc.vector.tensor_reduce(dest_f, onehot, axis=AX.X, op=ALU.add))
            nc.vector.tensor_copy(dest[:, :], dest_f).then_inc(dest_done, 1)
            link(nc.vector.tensor_tensor(ended, iota_q.unsqueeze(2).to_broadcast([1, MAXR + 1, E]),
                                         pair_end[0:1, :].unsqueeze(1).to_broadcast([1, MAXR + 1, E]), ALU.is_ge))
            link(nc.vector.tensor_reduce(table_f, ended, axis=AX.X, op=ALU.add))
            n_pairs_f = pair_end[0:1, E - 1:E]
            link(nc.vector.tensor_scalar(single_end[0:1, :], single_end[0:1, :], n_pairs_f, None, ALU.add))
            link(nc.vector.tensor_tensor(ended, iota_q.unsqueeze(2).to_broadcast([1, MAXR + 1, E]),
                                         single_end[0:1, :].unsqueeze(1).to_broadcast([1, MAXR + 1, E]), ALU.is_ge))
            link(nc.vector.tensor_reduce(table_s, ended, axis=AX.X, op=ALU.add))
            link(nc.vector.tensor_tensor(table_f, table_f, table_s, ALU.add))
            link(nc.vector.tensor_scalar(table_s, iota_q, n_pairs_f, float(-E), ALU.is_ge, ALU.mult))
            link(nc.vector.tensor_tensor(table_f, table_f, table_s, ALU.add))
            link(nc.vector.tensor_scalar(table[0:1, 0:MAXR + 1], table_f, float(E - 1), None, ALU.min))
            link(nc.vector.tensor_scalar(start_f, iota_q, n_pairs_f, None, ALU.min))
            link(nc.vector.tensor_tensor(start_f, start_f, iota_q, ALU.add))
            link(nc.vector.tensor_scalar(starts[0:1, 0:MAXR + 1], start_f, float(ROWS), float((MAXB - 2) * ROWS), ALU.mult, ALU.min))
            link(nc.vector.tensor_copy(starts[0:1, MAXR + 1:MAXR + 2], n_pairs_f))
            link(nc.vector.tensor_scalar(total_f, n_pairs_f, 1.0, None, ALU.add))
            link(nc.vector.tensor_tensor(total_f, total_f, single_end[0:1, E - 1:E], ALU.max))
            nc.vector.tensor_copy(table[0:1, MAXR + 1:MAXR + 2], total_f).then_inc(table_done, 1)
            dve.wait_ge(table_done, 1)
            n_pairs = dve.value_load(starts[0:1, MAXR + 1:MAXR + 2], min_val=1, max_val=E)
            rounds = dve.value_load(table[0:1, MAXR + 1:MAXR + 2], min_val=2, max_val=MAXR - 1)

            def split_lo(n, j):
                dve.wait_ge(hi_done, n + 1)
                nc.vector.tensor_tensor(w_lo[:, j % NRING, :, :], raw[:, j % NRING, :, :],
                                        w_hi[:, j % NRING, :, :].bitcast(f32), ALU.subtract).then_inc(lo_done, 1)

            def x_lo_part(r, f):
                dve.wait_ge(xhi_done[f], r + 1)
                part = (slice(None), f // 2, slice(4 * (f % 2), 4 * (f % 2) + 4), slice(None))
                nc.vector.tensor_tensor(x_lo[part], tx_ps[:, :].rearrange("p (k s) -> p k s", k=4), x_hi[part].bitcast(f32),
                                        ALU.subtract).then_inc(xlo_done[f], 1)

            def a_lo_part(r, h, t):
                dve.wait_ge(ahi_done[t], r * 2 + h + 1)
                part = (slice(None), t, slice(4 * h, 4 * h + 4), slice(None))
                nc.vector.tensor_tensor(a_lo[part], ta_ps[:, :].rearrange("p (k s) -> p k s", k=4), a_hi[part].bitcast(f32),
                                        ALU.subtract).then_inc(alo_done[t], 1)

            for f in range(4):
                x_lo_part(0, f)
            for j in range(NRING):
                split_lo(j, j)
            for first, last, tiles in ((0, n_pairs, 2), (n_pairs, rounds, 1)):
                with dve.Fori(first, last) as r:
                    for j in range(NPIECE):
                        h = j // 4
                        if j in (1, 5):
                            dve.wait_ge(piece_used, r * NPIECE + j + 1 + NRING)
                            for t in range(tiles):
                                nc.vector.tensor_scalar(g_t[:, t, :], gate_ps[t][:, :], LIMIT, None, ALU.min
                                                        ).then_inc(gu_read[t], 1)
                        if j in (3, 7):
                            dve.wait_ge(piece_used, r * NPIECE + j + 1 + NRING)
                            for t in range(tiles):
                                dve.wait_ge(aT_ps[t], r * 2 + h + 1)
                                nc.vector.tensor_scalar(u_t[:, t, :], up_ps[t][:, :], LIMIT, -LIMIT, ALU.min, ALU.max
                                                        ).then_inc(gu_read[t], 1)
                            for t in range(tiles):
                                dve.wait_ge(gu_read[t], r * 4 + 2 * h + 4)
                                nc.vector.scalar_tensor_tensor(out=u_t[:, t, :], in0=u_t[:, t, :], scalar=1.0, in1=g_t[:, t, :],
                                                               op0=ALU.add, op1=ALU.mult).then_inc(glu_mid[t], 1)
                            for t in range(tiles):
                                dve.wait_ge(glu_mid[t], r * 2 + h + 1)
                                dve.wait_ge(sig_done[t], r * 2 + h + 1)
                                nc.vector.tensor_tensor(u_t[:, t, :], u_t[:, t, :], s_t[:, t, :], ALU.mult).then_inc(glu_done[t], 1)
                        split_lo(r * NPIECE + j + NRING, (j + NRING) % NPIECE)
                        if j == 4:
                            a_lo_part(r, 0, 0)
                        if j == 5 and tiles == 2:
                            a_lo_part(r, 0, 1)
                        if 7 <= j < 7 + 2 * tiles:
                            x_lo_part(r + 1, j - 7)
                        if 8 <= j < 8 + tiles:
                            a_lo_part(r, 1, j - 8)
            dve.wait_ge(gf_in, 16)

            def finish(t):
                dve.wait_ge(fstd_done, t + 1)
                nc.vector.reciprocal(frs[:, t:t + 1], frs[:, t:t + 1]).then_inc(frs_done, 1)
                dve.wait_ge(frs_done, t + 1)
                if t >= 2:
                    dve.wait_ge(out_done[t % 2], 16 * (t // 2))
                nc.vector.scalar_tensor_tensor(out=fin[:, t % 2, :], in0=h_all[:, t, :], scalar=frs[:, t:t + 1], in1=gf_b,
                                               op0=ALU.mult, op1=ALU.mult).then_inc(fin_done, 1)

            for t in range(NT):
                dve.wait_ge(got_in[t % 2], 16 * TOPK * (t // 2 + 1))
                for k in range(TOPK):
                    if t or k:
                        dve.wait_ge(sum_done, TOPK * t + k)
                    ins = nc.vector.scalar_tensor_tensor(out=h_all[:, t, :], in0=y_got[:, t % 2, k, :], scalar=gates[:, t, k:k + 1],
                                                         in1=h_all[:, t, :], op0=ALU.mult, op1=ALU.add)
                    ins.then_inc(sum_done, 1)
                if t >= 1:
                    finish(t - 1)
            finish(NT - 1)

        def on_tensor(pe):
            pe.wait_ge(wo_add, 2 * NT)
            pe.wait_ge(const_in, 48)
            for t in range(NT):
                pe.wait_ge(hn_done, t + 1)
                if t >= 2:
                    pe.wait_ge(hnT_done, 2 * (t - 1))
                for k in range(KT):
                    ins = nc.tensor.transpose(bank[2 + 2 * (t % 2) + k // 4][:, (k % 4) * TP:(k % 4 + 1) * TP],
                                              hn[:, t % 2, k * 128:(k + 1) * 128], ident[0:TP, 0:TP])
                ins.then_inc(hnT_ps, 1)
                pe.wait_ge(hnT_done, 2 * (t + 1))
                if t >= 2:
                    pe.wait_ge(lg_read, t - 1)
                for k in range(KT):
                    ins = nc.tensor.matmul(bank[6 + t % 2][0:TP, 0:E], hnT[:, t % 2, k, :], wr_t[:, k, :],
                                           start=k == 0, stop=k == KT - 1)
                ins.then_inc(logit_ps, 1)
            pe.wait_ge(chosen_done, 1)
            pe.wait_ge(pool_const, 2)
            pe.wait_ge(dve_const, 1)
            nc.tensor.matmul(bank[0][0:TP, 0:NT * E], tri, chosen.rearrange("p t e -> p (t e)"), start=True, stop=False)
            nc.tensor.matmul(bank[0][0:TP, 0:NT * E], ones[:, 0:TP], before[:, 0:NT, :].rearrange("p t e -> p (t e)"),
                             start=False, stop=True).then_inc(rank_ps, 1)
            nc.tensor.matmul(bank[1][0:TP, 0:E], ones[:, 0:TP], before[:, NT, :], start=True, stop=True).then_inc(rank_ps, 1)
            pe.wait_ge(table_done, 1)
            n_pairs = pe.value_load(starts[0:1, MAXR + 1:MAXR + 2], min_val=1, max_val=E)
            rounds = pe.value_load(table[0:1, MAXR + 1:MAXR + 2], min_val=2, max_val=MAXR - 1)
            pe.wait_ge(kind_done, 1)

            def x_part(r, f):
                t = f // 2
                pe.wait_ge(rows_in[t], r * 16 + 16)
                if f >= 1:
                    pe.wait_ge(xlo_done[f - 1], r + 1)
                for k in range(4):
                    c = (4 * (f % 2) + k) * 128
                    ins = nc.tensor.transpose(tx_ps[:, k * 128:(k + 1) * 128], x_rows[:, t, c:c + 128], ident[:, :])
                ins.then_inc(xT_ps[f], 1)

            def a_part(r, h, t, tiles):
                pe.wait_ge(glu_done[t], r * 2 + h + 2)
                if t == 1:
                    pe.wait_ge(alo_done[0], r * 2 + h + 2)
                else:
                    pe.wait_ge(alo_done[tiles - 1], r * 2 + h + 1)
                for k in range(4):
                    ins = nc.tensor.transpose(ta_ps[:, k * 128:(k + 1) * 128], u_t[:, t, k * 128:(k + 1) * 128], ident[:, :])
                ins.then_inc(aT_ps[t], 1)

            def product(ps, m_hi, m_lo, slot, k, start, stop=False):
                nc.tensor.matmul(ps, m_hi, w_hi[:, slot, k, :], start=start, stop=False)
                nc.tensor.matmul(ps, m_hi, w_lo[:, slot, k, :], start=False, stop=False)
                return nc.tensor.matmul(ps, m_lo, w_hi[:, slot, k, :], start=False, stop=stop)

            for f in range(4):
                x_part(0, f)
            for first, last, tiles in ((0, n_pairs, 2), (n_pairs, rounds, 1)):
                with pe.Fori(first, last) as r:
                    for j in range(8):
                        g, h = j // 2, j // 4
                        ps = (gate_ps, up_ps)[g % 2]
                        pe.wait_ge(lo_done, r * NPIECE + j + 1 + NRING)
                        if j == 0:
                            for f in range(2 * tiles):
                                pe.wait_ge(xlo_done[f], r + 1)
                        for t in range(tiles):
                            if j == 2:
                                pe.wait_ge(y_read[t], r * 2 + 1)
                            elif j % 2 == 0:
                                pe.wait_ge(gu_read[t], r * 4 + g + 1)
                            for k in range(HK):
                                kk = HK * (j % 2) + k
                                ins = product(ps[t][:, :], x_hi[:, t, kk, :], x_lo[:, t, kk, :], j % NRING, k, kk == 0)
                            if j % 2 == 1:
                                if j == 1 and t == 0:
                                    pe.wait_ge(bias_got, r * 16 + 16)
                                ins = nc.tensor.matmul(ps[t][:, :], kind_row[:, g % 2, :], bias_t[:, HC * h:HC * (h + 1)],
                                                       start=False, stop=True)
                        ins.then_inc(piece_used, 1)
                        if j in (4, 5) and j - 4 < tiles:
                            a_part(r, 0, j - 4, tiles)
                    for j in range(8, NPIECE):
                        if j - 8 < 2 * tiles:
                            x_part(r + 1, j - 8)
                        if 0 <= j - 9 < tiles:
                            a_part(r, 1, j - 9, tiles)
                        pe.wait_ge(lo_done, r * NPIECE + j + 1 + NRING)
                        for t in range(tiles):
                            pe.wait_ge(alo_done[t], r * 2 + 2 + (j - 8) // 2)
                            ps = y_ps[j % 2][t][:, :]
                            if j == 9:
                                pe.wait_ge(gu_read[t], r * 4 + 6)
                            if j < 10:
                                nc.tensor.matmul(ps, kind_row[:, 2, :], bias_t[:, HC * (j - 8):HC * (j - 7)],
                                                 start=True, stop=False)
                            for k in range(HK):
                                kk = HK * ((j - 8) // 2) + k
                                ins = product(ps, a_hi[:, t, kk, :], a_lo[:, t, kk, :], j % NRING, k, False, kk == KT - 1)
                        ins.then_inc(piece_used, 1)
                if tiles == 2:
                    pe.wait_ge(alo_done[1], n_pairs * 2 + 1)
                    for f in (2, 3):
                        pe.wait_ge(xlo_done[f], n_pairs + 1)
                    pe.sem_inc(pe_passed, 1)

    return on_sync, on_gpsimd, on_scalar, on_vector, on_tensor


def program(nc, a, out):
    f32 = mybir.dt.float32
    u32 = mybir.dt.uint32
    TOK, D, E, TOPK, ROWS = 1040, 1024, 32, 4, 128
    TP, NT = 104, 10
    MINB = -(-TOK * TOPK // ROWS)
    MAXB = (TOK * TOPK + E * (ROWS - 1)) // ROWS + 2
    with ExitStack() as ctx:
        bank = [ctx.enter_context(nc.psum_tensor(f"bank{i}", [128, 512], f32)) for i in range(8)]
        hn_d = nc.dram_tensor("hn_d", (TOK, D), f32).ap()
        ys_d = nc.dram_tensor("ys_d", ((MAXB - 1) * ROWS, D), f32).ap()
        rowtok_d = nc.dram_tensor("rowtok_d", (MAXB * ROWS, 1), u32).ap()
        bias_d = nc.dram_tensor("bias_d", (E, 6, D), f32).ap()
        keep = Plan(nc, (nc.sbuf_base + 63) // 64 * 64)
        shared = dict(ident=keep("ident", [128, 128]), eps_t=keep("eps_t", [128, 1]))
        shared.update(gates=keep("gates", [TP, NT, TOPK]), dest=keep("dest", [TP, NT * TOPK], u32))
        shared['start'] = keep.at + 256
        at_h = Plan(nc, shared['start'])
        shared['h_all'] = at_h("h_all", [TP, NT, D])
        shared['after_h'] = at_h.at
        shared['zero_out'] = ctx.enter_context(nc.semaphore("zero_out"))
        shared['wo_add'] = ctx.enter_context(nc.semaphore("wo_add"))
        ys_rest = [ys_d[b * ROWS:(b + 2) * ROWS, :].rearrange("(p b) d -> p (b d)", b=2) for b in range(MINB, MAXB - 1, 2)]
        shared.update(hn_d=hn_d, ys_d=ys_d, rowtok_d=rowtok_d, bias_d=bias_d, blocks=MAXB, ys_rest=ys_rest,
                      rowtok_rows=rowtok_d.rearrange("(q s) a -> q (s a)", s=ROWS), zeroed=16 * (1 + len(ys_rest)))
        mixing = mixing_program(nc, ctx, a, bank, keep, shared)
        assert keep.at <= shared['start']
        experts = experts_program(nc, ctx, a, bank, shared, out)

        block = ctx.enter_context(nc.Block())

        @block.sync
        def _(sp):
            for part in (mixing, experts):
                part[0](sp)

        @block.gpsimd
        def _(pool):
            for part in (mixing, experts):
                part[1](pool)

        @block.scalar
        def _(act):
            for part in (mixing, experts):
                part[2](act)

        @block.vector
        def _(dve):
            for part in (mixing, experts):
                part[3](dve)

        @block.tensor
        def _(pe):
            for part in (mixing, experts):
                part[4](pe)


_INS = ['x', 'meta_tokens', 'ln1_g', 'w_in', 'mu_r', 'mu_k', 'mu_v', 'mu_w', 'mu_a', 'mu_g', 'w0', 'w_w1', 'w_w2', 'a0', 'w_a1', 'w_a2',
        'w_g1', 'w_g2', 'k_k', 'k_a', 'r_k', 'lnx_g', 'lnx_b', 'w_o_rwkv', 'conv_w', 'w_o_conv', 'w_o', 'ln2_g', 'w_router', 'b_router',
        'w_e_gate', 'b_e_gate', 'w_e_up', 'b_e_up', 'w_e_down', 'b_e_down', 'lnf_g']


def kernel(**inputs):
    import numpy as _np
    import concourse.bacc as _bacc
    from concourse import mybir as _mybir
    from concourse.bass_utils import run_bass_kernel_spmd as _run

    nc = _bacc.Bacc("TRN2", target_bir_lowering=False, num_devices=1)
    arrays, a = {}, {}
    for name in _INS:
        x = _np.ascontiguousarray(inputs[name])
        arrays[f"in_{name}"] = x
        ap = nc.dram_tensor(f"in_{name}", x.shape, _mybir.dt.from_np(x.dtype), kind="ExternalInput").ap()
        a[name] = ap if name in ('meta_tokens', 'lnf_g') else ap[0]
    out = nc.dram_tensor("out_0", (1024, 1024), _mybir.dt.float32, kind="ExternalOutput").ap()
    program(nc, a, out)
    r = _run(nc, [arrays], core_ids=[0])
    return r.results[0]["out_0"].reshape(1, 1024, 1024)
```

```python
from contextlib import ExitStack

import concourse.bass as bass
from concourse import mybir


class Plan:

    def __init__(self, nc, at):
        self.nc, self.at = nc, at

    def __call__(self, name, shape, dt=mybir.dt.float32):
        size = 4
        for n in shape[1:]:
            size *= n
        t = self.nc.alloc_sbuf_tensor_at(name, shape, dt, offset=self.at)
        self.at += (size + 31) // 32 * 32
        return t[(slice(None),) * len(shape)]


def mixing_program(nc, ctx, a, bank, keep, shared):
    f32 = mybir.dt.float32
    f32r = mybir.dt.float32r
    u32 = mybir.dt.uint32
    ALU = mybir.AluOpType
    ACT = mybir.ActivationFunctionType
    AX = mybir.AxisListType

    D = 1024
    META = 16
    TOK = 1040
    NT = 10
    TP = TOK // NT
    KT = D // 128
    RW = 512
    NJ = RW // 128
    HS = 64
    NCH = 4
    CH = TOK // NCH
    NU = 2 * NT
    NB = NU // 4
    LEVELS = 7
    EPS = 1e-5
    LNX_EPS = 64e-5
    DECAY = 0.6065306597126334

    def sem(name):
        return ctx.enter_context(nc.semaphore(name))

    ident, eps_t, h_all, zero_out, wo_add = shared['ident'], shared['eps_t'], shared['h_all'], shared['zero_out'], shared['wo_add']
    epsx_t = keep("epsx_t", [128, 1])
    dz = keep("dz", [128, 8])
    ones_t = keep("ones_t", [128, 1])
    START = shared['start']

    wk = Plan(nc, START)
    AT = wk("AT", [TP, NU, 4, TP])
    Tm = wk("Tm", [TP, NU, TP])
    Rm = wk("Rm", [TP, NU, TP])
    P1 = wk("P1", [TP, 2, 4, TP])
    Vt = wk("Vt", [TP, NT, 128])
    Bt = wk("Bt", [TP, NT, 128])
    Kt = wk("Kt", [TP, NT, 128])
    X = wk("X", [TP, NU, 128])
    x1t = wk("x1t", [128, NT, TP])
    mxt = wk("mxt", [128, NT, HS])
    np_ = wk("np_", [128, NT, HS])
    S = wk("S", [128, NT + 1, HS])
    U = wk("U", [TP, NU, HS])
    pr = Plan(nc, START)
    pb = pr("pb", [128, 3, TOK + 2])
    r_t = pr("r_t", [128, TOK])
    k_t = pr("k_t", [128, TOK])
    sg = pr("sg", [128, TOK])
    cs = pr("cs", [128, TOK])
    e0 = pr("e0", [128, TOK])
    e1 = pr("e1", [128, TOK])
    e2 = pr("e2", [128, TOK])
    a_t = pr("a_t", [128, TOK])
    kk = pr("kk", [128, TOK])
    tmp = pr("tmp", [128, TOK])
    nrm = pr("nrm", [128, TOK])
    assert pr.at <= wk.at
    s0 = Plan(nc, START)
    x_in = s0("x_in", [TP, NT, D])
    xn = s0("xn", [TP, 2, D])
    junk = s0("junk", [TP, D])
    ss = s0("ss", [TP, NT])
    rstd = s0("rstd", [TP, NT])
    lraw = s0("lraw", [128, KT, 256])
    lmu = s0("lmu", [128, KT, 256])
    o1 = s0("o1", [128, 2, TOK])
    o2 = s0("o2", [128, 2, TOK + 1])
    vrows = s0("vrows", [84, 128])
    assert s0.at <= wk.at
    s1 = Plan(nc, shared['after_h'])
    mT = s1("mT", [128, KT, TOK])
    cv = s1("cv", [128, NJ, TOK])
    assert s1.at <= wk.at
    s2 = Plan(nc, START)
    cpb = s2("cpb", [128, 3, TOK + 2])
    c1 = s2("c1", [128, TOK])
    gt = s2("gt", [128, 2, 2, CH])
    ring_hi = s2("ring_hi", [128, 3, KT, 128], f32r)
    ring2_hi = [Plan(nc, s2.at)("ring2_hi1", [128, KT, 128], f32r)]
    s2.at += 4 * KT * 128
    assert s2.at <= START + 4 * NT * D
    ring2 = Plan(nc, START)("ring2", [128, 3, KT, 128])
    ring2_hi.insert(0, Plan(nc, START + 4 * 3 * KT * 128)("ring2_hi0", [128, KT, 128], f32r))
    assert 4 * KT * 128 <= 3 * (TOK + 2) + TOK
    ring2_lo = Plan(nc, START)("ring2_lo", [128, 3, KT, 128], f32r)

    com = Plan(nc, wk.at)
    xnT = com("xnT", [128, KT, TOK])
    yg = com("yg", [128, NJ, TOK])
    ring_at = com.at
    ring = com("ring", [128, 3, KT, 128])
    bones = com("bones", [128, 128])
    mask4 = com("mask4", [TP, 4, TP])
    mlev = com("mlev", [TP, LEVELS, 128])
    id2 = com("id2", [128, HS])
    vec = com("vec", [128, 84])
    vj = com("vj", [128, 12])
    pc = com("pc", [128, NT])
    J0 = com.at
    lw = com("lw", [128, TOK])
    lg = com("lg", [128, TOK])
    w2 = com("w2", [128, RW])
    wg2 = com("wg2", [128, RW])
    w2j = com("w2j", [128, 128])
    wg2j = com("wg2j", [128, 128])
    v_t = com("v_t", [128, TOK])
    rkb = com("rkb", [128, TOK])
    y_t = com("y_t", [128, TOK])
    ar = com("ar", [128, NT, 2, TP])
    zero = ar.rearrange("p c m t -> p (c m t)")
    bh = com("bh", [128, TOK])
    kh = com("kh", [128, TOK])
    ring_lo = Plan(nc, ring_at)("ring_lo", [128, 3, KT, 128], f32r)
    xm_hi = Plan(nc, J0)("xm_hi", [128, KT, TOK], f32r)
    xm_lo = Plan(nc, wk.at)("xm_lo", [128, KT, TOK], f32r)
    assert J0 + 4 * KT * TOK <= com.at
    wo_t = Plan(nc, wk.at)("wo_t", [128, KT, D])
    shared.update(mT=mT, wo_t=wo_t, after_wo=wk.at + 4 * KT * D)

    VEC = {}
    at = 0
    for name, n in (('mu_w', 8), ('mu_a', 8), ('mu_g', 8), ('ln1_g', 8), ('mu_r', 4), ('mu_k', 4), ('mu_v', 4), ('w0', 4),
                    ('a0', 4), ('k_k', 4), ('k_a', 4), ('r_k', 4), ('lnx_g', 4), ('lnx_b', 4), ('conv_w', 12)):
        VEC[name] = at
        at += n
    assert at == 84
    JV = {name: i for i, name in enumerate(('mu_r', 'mu_k', 'mu_v', 'w0', 'a0', 'k_k', 'k_a', 'r_k', 'lnx_g', 'lnx_b'))}

    def pj(name):
        return vj[:, JV[name]:JV[name] + 1]

    TA = 'bkav'
    PE_J = ([('z', c) for c in range(NCH)] + [('p', 'r', 0), ('p', 'r', 1)] + [('n', c) for c in range(NCH)]
            + [('p', 'r', 2), ('p', 'r', 3)] + [('p', 'v', c) for c in range(NCH)] + [('t', x, g) for x in TA for g in range(3)]
            + [('A', u) for u in range(NU)])
    for l in range(LEVELS):
        for s in range(NB + 1):
            if s < NB:
                PE_J.append(('P', l, s))
            if s > 0:
                PE_J.append(('D', l, s - 1))
    PE_J += ([('xa', g) for g in range(3)] + [('xc', g) for g in range(3)] + [('xb', g) for g in range(5)]
             + [('m', g) for g in range(2)] + [('nn', g) for g in range(2)] + [('s', c) for c in range(1, NT)]
             + [('u', g) for g in range(2)] + [('y', g) for g in range(3)]
             + [('bs', c) for c in range(NCH)] + [('g', c) for c in range(NCH)]
             + [('mean', c) for c in range(NCH)] + [('var', c) for c in range(NCH)])
    ACT_J = ([('p', 'k', c) for c in range(NCH)] + [(x, c) for c in range(NCH) for x in 'za'] + ['sq', ('p', 'r', 0), ('p', 'r', 1)]
             + [('n', c) for c in range(NCH)] + [('p', 'r', 2), ('p', 'r', 3), ('p', 'v', 0), ('p', 'v', 1)]
             + ['E1', 'E2', 'E0', ('p', 'v', 2), ('p', 'v', 3)] + [('t', x, g) for x in TA for g in range(3)]
             + [('xa', g) for g in range(3)] + [('xc', g) for g in range(3)] + [('xb', g) for g in range(5)]
             + [('y', g) for g in range(3)] + ['ysq'] + [('var', c) for c in range(NCH)])
    DVE_J = (['k_d', 'k', 'kkr'] + [('cs', c) for c in range(NT)]
             + ['csx', 'km', 'kmod', 'nmax', 'nrec', 'kk', 'at', 'ba', 'bh', 'kh', 'pc', 'r_d', 'r', 'rkb', 'rt', 'v_d', 'v']
             + [('A', u) for u in range(NU)])
    for l in range(LEVELS):
        for s in range(NB + 1):
            if s < NB:
                DVE_J.append(('P', l, s))
            if s > 0:
                DVE_J += [('T', l, s - 1)] * (l < LEVELS - 1) + [('R', l, s - 1)]
    DVE_J += ([('m', g) for g in range(2)] + [('nn', g) for g in range(2)] + ['S0'] + [('S', c) for c in range(NT)]
              + [('u', g, h) for g in range(2) for h in range(2)] + [('bo', c) for c in range(NCH)]
              + [('yc', c) for c in range(NCH)] + ['yrec', 'yn', 'yaff', 'ysum'] + [('yg', c) for c in range(NCH)])
    POOL_J = ['vj', 'w2', 'wg2', 'T0', 'R0']

    class Order:
        def __init__(self, sem, labels):
            self.sem, self.labels, self.next = sem, {x: i for i, x in enumerate(labels)}, 0
            assert len(self.labels) == len(labels)

        def done(self, eng, label, j, passed=None):
            eng.wait_ge(self.sem, j * len(self.labels) + self.labels[label] + 1)
            if passed is not None:
                eng.sem_inc(passed, 1)

        def mark(self, ins, label):
            assert self.labels[label] == self.next, label
            self.next = (self.next + 1) % len(self.labels)
            ins.then_inc(self.sem, 1)

    pe_j = Order(sem("pe_j"), PE_J)
    act_j = Order(sem("act_j"), ACT_J)
    dve_j = Order(sem("dve_j"), DVE_J)
    pool_j = Order(sem("pool_j"), POOL_J)

    vec_in = sem("vec_in")
    x_got = [sem(f"x_got{t}") for t in range(NT)]
    lora_in = sem("lora_in")
    w2_in = sem("w2_in")
    ring_in = [sem(f"ring_in{s}") for s in range(3)]
    ring2_in = [sem(f"ring2_in{s}") for s in range(3)]
    h_in, wo_in, gate_mul = shared['h_in'], shared['wo_in'], shared['gate_mul']
    pool_c = sem("pool_c")
    dve_c = sem("dve_c")
    vec_ps = sem("vec_ps")
    vec_done = sem("vec_done")
    sq0_done = sem("sq0_done")
    std0_done = sem("std0_done")
    rstd0_done = sem("rstd0_done")
    xn_done = sem("xn_done")
    xnT_ps = sem("xnT_ps")
    xnT_done = sem("xnT_done")
    lmu_done = sem("lmu_done")
    lora_ps = sem("lora_ps")
    lora_ev = sem("lora_ev")
    lora_mix = sem("lora_mix")
    lora_done = sem("lora_done")
    conv_ps = sem("conv_ps")
    conv_ev = sem("conv_ev")
    conv_step = sem("conv_step")
    gate_ps = sem("gate_ps")
    gate_sig = sem("gate_sig")
    sp_passed = sem("sp_passed")
    pool_passed = sem("pool_passed")
    pe_passed = sem("pe_passed")
    col_free = sem("col_free")
    xm_hi_done = sem("xm_hi_done")
    xm_lo_done = sem("xm_lo_done")
    ring_hi_done = sem("ring_hi_done")
    ring_lo_done = sem("ring_lo_done")
    ring2_hi_done = sem("ring2_hi_done")
    ring2_lo_done = sem("ring2_lo_done")
    k_ps = sem("k_ps")
    late_free = sem("late_free")
    pbz = sem("pbz")

    w_in = a['w_in']

    def cols(w, c0, n=128):
        return w[:, bass.ds(c0, n)].rearrange("(k p) c -> p k c", p=128)

    def x_tile(t):
        if t == 0:
            return [((0, META), a['meta_tokens']), ((META, TP), a['x'][0:TP - META, :])]
        return [((0, TP), a['x'][TP * t - META:TP * (t + 1) - META, :])]

    def on_sync(sp):
        for t in range(NT):
            for (p0, p1), src in x_tile(t):
                sp.dma_start(x_in[p0:p1, t, :], src).then_inc(x_got[t], 16)
        for name in ('mu_w', 'mu_a', 'mu_g', 'ln1_g', 'mu_r', 'mu_k', 'mu_v', 'w0', 'a0', 'k_k', 'k_a', 'r_k', 'lnx_g', 'lnx_b'):
            n = a[name].shape[0] // 128
            sp.dma_start(vrows[VEC[name]:VEC[name] + n, :], a[name].rearrange("(k p) -> k p", p=128)).then_inc(vec_in, 16)
        sp.dma_start(vrows[VEC['conv_w']:VEC['conv_w'] + 12, :], a['conv_w'].rearrange("w (k p) -> (w k) p", p=128)
                     ).then_inc(vec_in, 16)
        sp.wait_ge(dve_c, 6)
        sp.dma_start(shared['rowtok_rows'], zero[0:shared['rowtok_rows'].shape[0], 0:shared['rowtok_rows'].shape[1]].bitcast(u32)).then_inc(zero_out, 16)
        sp.dma_start(lraw[:, :, 0:64], cols(a['w_w1'], 0, 64)).then_inc(lora_in, 16)
        sp.dma_start(lraw[:, :, 64:128], cols(a['w_a1'], 0, 64)).then_inc(lora_in, 16)
        sp.dma_start(lraw[:, :, 128:256], cols(a['w_g1'], 0, 128)).then_inc(lora_in, 16)
        sp.dma_start(w2[0:64, :], a['w_w2']).then_inc(w2_in, 16)
        sp.dma_start(w2[64:128, :], a['w_a2']).then_inc(w2_in, 16)
        sp.dma_start(wg2[:, :], a['w_g2']).then_inc(w2_in, 16)
        for rows in shared['ys_rest']:
            sp.dma_start(rows, zero[0:rows.shape[0], 0:rows.shape[1]]).then_inc(zero_out, 16)

        def load(i, c0):
            sp.dma_start(ring[:, i, :, :], cols(w_in, c0)).then_inc(ring_in[i], 16)

        for i in range(3):
            load(i, RW * i)
        with sp.Fori(0, NJ - 1) as j:
            sp.wait_ge(k_ps, j * NCH + NCH)
            sp.sem_inc(sp_passed, 1)
            load(1, (j + 1) * 128 + RW)
            for i, x in ((0, 'r'), (2, 'v')):
                pe_j.done(sp, ('p', x, NCH - 1), j, sp_passed)
                load(i, (j + 1) * 128 + RW * i)
        sp.wait_ge(k_ps, NJ * NCH)
        load(1, RW * (3 + 1))
        for i, x in ((0, 'r'), (2, 'v')):
            pe_j.done(sp, ('p', x, NCH - 1), NJ - 1)
            load(i, RW * (3 + i))
        with sp.Fori(0, NJ - 1) as j:
            for i in range(3):
                sp.wait_ge(conv_ps, j * 12 + 4 * i + 4)
                sp.sem_inc(sp_passed, 1)
                load(i, (j + 1) * 128 + RW * (3 + i))

        def load_gate(d, into, arrived, i):
            if i < 2:
                sp.dma_start(into[:, i, :, :], cols(w_in, d * 128 + 6 * RW + D * i)).then_inc(arrived[i], 16)
            else:
                sp.dma_start(into[:, 2, 0:4, :], cols(a['w_o_rwkv'], d * 128)).then_inc(arrived[2], 16)
                sp.dma_start(into[:, 2, 4:8, :], cols(a['w_o_conv'], d * 128)).then_inc(arrived[2], 16)

        def load_gates(d, into, arrived):
            for i in range(3):
                load_gate(d, into, arrived, i)

        for i in range(3):
            sp.wait_ge(conv_ps, 12 * (NJ - 1) + 4 * i + 4)
            load_gate(0, ring, ring_in, i)
        sp.wait_ge(conv_step, 6 * NJ + 6)
        load_gates(1, ring2, ring2_in)
        with sp.Fori(0, KT // 2 - 1) as dd:
            for s, (into, arrived) in enumerate(((ring, ring_in), (ring2, ring2_in))):
                sp.wait_ge(gate_ps, dd * 8 + 4 * s + 4)
                sp.sem_inc(sp_passed, 1)
                load_gates(2 * dd + 2 + s, into, arrived)
        sp.wait_ge(gate_mul, 3 * KT * NCH + 6)
        w_o = a['w_o'].rearrange("(k p) c -> p k c", p=128)
        sp.dma_start(wo_t[:, :, 0:512], w_o[:, :, 0:512]).then_inc(wo_in[0], 16)
        for t in range(NT):
            if t == 2:
                sp.dma_start(wo_t[:, :, 512:1024], w_o[:, :, 512:1024]).then_inc(wo_in[1], 16)
            for (p0, p1), src in x_tile(t):
                sp.dma_start(h_all[p0:p1, t, :], src).then_inc(h_in[t // 2], 16)

    def on_gpsimd(pool):
        n = [0]

        def step(ins):
            n[0] += 1
            ins.then_inc(pool_c, 1)
            pool.wait_ge(pool_c, n[0])

        def select(out, op, base, pattern, cm, fill):
            step(nc.gpsimd.affine_select(out=out, in_=out, compare_op=op, fill=fill, base=base, pattern=pattern,
                                         channel_multiplier=cm))

        step(nc.gpsimd.memset(ident[:, :], 0.0))
        select(ident[:, :], ALU.not_equal, 0, [[-1, 128]], 1, 1.0)
        step(nc.gpsimd.memset(id2[:, :], 0.0))
        select(id2[:, :], ALU.not_equal, 0, [[-1, HS]], 1, 1.0)
        select(id2[:, :], ALU.not_equal, -HS, [[-1, HS]], 1, 1.0)
        step(nc.gpsimd.memset(bones[:, :], 0.0))
        step(nc.gpsimd.memset(bones[0:HS, 0:HS], 1.0))
        step(nc.gpsimd.memset(bones[HS:128, HS:128], 1.0))
        step(nc.gpsimd.memset(mask4[:, :, :], 1.0))
        for m in range(4):
            select(mask4[:, m, :], ALU.is_gt if m % 2 == 0 else ALU.is_ge, 0, [[1, TP]], -1, 0.0)
        step(nc.gpsimd.memset(mlev[:, :, :], 1.0))
        for l in range(LEVELS):
            b = 2 << l
            h = b // 2
            v = mlev[:, l, :]
            pat = [[-b, 128 // b], [0, b]]
            select(v, ALU.is_ge, -h, pat, 1, 0.0)
            select(v, ALU.is_gt, b, [[b, 128 // b], [0, b]], -1, 0.0)
            select(v, ALU.is_gt, h, [[0, 128 // b], [-1, b]], 0, 0.0)

        pool.wait_ge(vec_done, 1)
        pool.wait_ge(w2_in, 48)
        with pool.Fori(0, NJ) as j:
            pool.wait_ge(col_free, j + 1)
            pool.sem_inc(pool_passed, 1)
            pool_j.mark(nc.gpsimd.tensor_copy(vj[:, 0:10], vec[:, VEC['mu_r']:VEC['mu_r'] + 40].rearrange(
                "p (a k) -> p a k", k=4)[:, :, bass.ds(j, 1)].rearrange("p a k -> p (a k)")), 'vj')
            pool_j.mark(nc.gpsimd.tensor_copy(w2j[:, :], w2[:, bass.ds(j * 128, 128)]), 'w2')
            pool_j.mark(nc.gpsimd.tensor_copy(wg2j[:, :], wg2[:, bass.ds(j * 128, 128)]), 'wg2')
            dve_j.done(pool, 'v', j, pool_passed)
            for m, x in ((Tm, 'T0'), (Rm, 'R0')):
                pool_j.mark(nc.gpsimd.tensor_copy(m[:, :, :], ident[0:TP, 0:TP].unsqueeze(1).to_broadcast([TP, NU, TP])), x)

    def evac_groups():
        return ((0, 4), (4, 8), (8, 10))

    def on_scalar(act):
        for t in range(NT):
            act.wait_ge(x_got[t], 16 * len(x_tile(t)))
            if t:
                act.wait_ge(sq0_done, t)
            nc.scalar.activation(junk[:, :], x_in[:, t, :], ACT.Square, accum_out=ss[:, t:t + 1]).then_inc(sq0_done, 1)
            act.wait_ge(sq0_done, t + 1)
            act.wait_ge(dve_c, 6)
            nc.scalar.activation(rstd[:, t:t + 1], ss[:, t:t + 1], ACT.Sqrt, bias=eps_t[0:TP, :], scale=1.0 / D
                                 ).then_inc(std0_done, 1)
            if t == 1:
                act.wait_ge(vec_ps, 1)
                nc.scalar.activation(vec[:, :], bank[7][:, 0:84], ACT.Copy).then_inc(vec_done, 1)
        for m in range(2):
            for c in range(NCH):
                act.wait_ge(lora_ps, 4 * m + c + 1)
                nc.scalar.activation(o1[:, m, CH * c:CH * (c + 1)], bank[c % 2][:, 0:CH], ACT.Copy).then_inc(lora_ev, 1)
                nc.scalar.activation(o2[:, m, 1 + CH * c:1 + CH * (c + 1)], bank[2 + c % 2][:, 0:CH], ACT.Copy).then_inc(lora_ev, 1)
        act.wait_ge(lora_mix, 4)
        nc.scalar.activation(lw[0:64, :], o1[0:64, 0, :], ACT.Tanh).then_inc(lora_done, 1)
        nc.scalar.activation(lw[64:128, :], o1[64:128, 0, :], ACT.Copy).then_inc(lora_done, 1)
        nc.scalar.activation(lg[:, :], o1[:, 1, :], ACT.Sigmoid).then_inc(lora_done, 1)

        with act.Fori(0, NJ) as j:
            act.wait_ge(col_free, j + 1)
            pool_j.done(act, 'vj', j)

            def project_out(x, c, bk):
                act_j.mark(nc.scalar.activation(pb[:, 'rkv'.index(x), 2 + CH * c:2 + CH * (c + 1)], bank[bk][:, 0:CH], ACT.Copy),
                           ('p', x, c))

            for c in range(NCH):
                act.wait_ge(k_ps, j * NCH + c + 1)
                project_out('k', c, 2 + c)
            for c in range(NCH):
                pe_j.done(act, ('z', c), j)
                act_j.mark(nc.scalar.activation(sg[:, CH * c:CH * (c + 1)], bank[c % 2][:, 0:CH], ACT.Sigmoid,
                                                bias=pj('w0')), ('z', c))
                act_j.mark(nc.scalar.activation(a_t[:, CH * c:CH * (c + 1)], bank[6 + c % 2][:, 0:CH], ACT.Sigmoid,
                                                bias=pj('a0')), ('a', c))
            dve_j.done(act, 'kkr', j)
            act_j.mark(nc.scalar.activation(nrm[:, :], kk[:, :], ACT.Square), 'sq')
            for c in range(NCH):
                if c == 2:
                    pe_j.done(act, ('n', NCH - 1), j)
                    for b in range(NCH):
                        act_j.mark(nc.scalar.activation(nrm[:, CH * b:CH * (b + 1)], bank[4 + b][:, 0:CH], ACT.Sqrt), ('n', b))
                pe_j.done(act, ('p', 'r', c), j)
                project_out('r', c, c % 2)
            for c in range(NCH):
                if c == 2:
                    dve_j.done(act, 'csx', j)
                    act_j.mark(nc.scalar.activation(e1[:, :], cs[:, :], ACT.Exp, scale=-DECAY), 'E1')
                    act_j.mark(nc.scalar.activation(e2[:, :], cs[:, :], ACT.Exp, scale=DECAY), 'E2')
                    act_j.mark(nc.scalar.activation(e0[:, :], tmp[:, :], ACT.Exp, scale=-DECAY), 'E0')
                pe_j.done(act, ('p', 'v', c), j)
                project_out('v', c, c % 2)
            dve_j.done(act, 'v', j)
            q = 0
            for x in TA:
                for g, (g0, g1) in enumerate(evac_groups()):
                    pe_j.done(act, ('t', x, g), j)
                    src = bank[2 + q % 2][0:TP, 0:128 * (g1 - g0)]
                    if x == 'a':
                        dst = X[:, 2 * g0:2 * g1, 0:HS]
                        src = src.rearrange("p (u n) -> p u n", n=HS)
                    else:
                        dst = dict(v=Vt, b=Bt, k=Kt)[x][:, g0:g1, :]
                        src = src.rearrange("p (c n) -> p c n", n=128)
                    act_j.mark(nc.scalar.activation(dst, src, ACT.Copy), ('t', x, g))
                    q += 1
            for g, (g0, g1) in enumerate(((0, 8), (8, 16), (16, 20))):
                pe_j.done(act, ('xa', g), j)
                act_j.mark(nc.scalar.activation(X[:, g0:g1, HS:128], bank[2 + g % 2][0:TP, 0:HS * (g1 - g0)].rearrange(
                    "p (u n) -> p u n", n=HS), ACT.Copy), ('xa', g))
            for g, (g0, g1) in enumerate(evac_groups()):
                pe_j.done(act, ('xc', g), j)
                act_j.mark(nc.scalar.activation(x1t[:, g0:g1, :], bank[4 + g % 2][:, 0:TP * (g1 - g0)].rearrange(
                    "p (c n) -> p c n", n=TP), ACT.Copy), ('xc', g))
            for g in range(5):
                pe_j.done(act, ('xb', g), j)
                act_j.mark(nc.scalar.activation(X[:, 4 * g:4 * g + 4, :], bank[6 + g % 2][0:TP, :].rearrange(
                    "p (u n) -> p u n", n=128), ACT.Copy), ('xb', g))
            for g, (g0, g1) in enumerate(evac_groups()):
                pe_j.done(act, ('y', g), j)
                act_j.mark(nc.scalar.activation(y_t[:, TP * g0:TP * g1], bank[6 + g % 2][:, 0:TP * (g1 - g0)], ACT.Copy),
                           ('y', g))
            dve_j.done(act, ('yc', NCH - 1), j)
            act_j.mark(nc.scalar.activation(tmp[:, :], y_t[:, :], ACT.Square), 'ysq')
            for c in range(NCH):
                pe_j.done(act, ('var', c), j)
                act_j.mark(nc.scalar.activation(nrm[:, CH * c:CH * (c + 1)], bank[4 + c % 2][:, 0:CH], ACT.Sqrt,
                                                bias=epsx_t[:, :], scale=1.0 / HS), ('var', c))
        def tokens_hi(c):
            nc.scalar.activation(xm_hi[:, :, CH * c:CH * (c + 1)], xnT[:, :, CH * c:CH * (c + 1)], ACT.Copy
                                 ).then_inc(xm_hi_done, 1)

        def weights_hi(i, arrived):
            act.wait_ge(ring_in[i], arrived)
            nc.scalar.activation(ring_hi[:, i, :, :], ring[:, i, :, :], ACT.Copy).then_inc(ring_hi_done, 1)

        def weights2_hi(i, arrived):
            act.wait_ge(ring2_in[i], arrived)
            nc.scalar.activation(ring2_hi[i][:, :, :], ring2[:, i, :, :], ACT.Copy).then_inc(ring2_hi_done, 1)

        act.wait_ge(col_free, NJ + 1)
        tokens_hi(0)
        weights_hi(0, 16 * NJ + 16)
        weights_hi(1, 16 * NJ + 16)
        for c in range(1, NCH):
            tokens_hi(c)
        with act.Fori(0, NJ) as j:
            for i in range(3):
                act.wait_ge(conv_step, j * 6 + 6)
                for c in range(NCH):
                    act.wait_ge(conv_ps, j * 12 + 4 * i + c + 1)
                    nc.scalar.activation(cpb[:, i, 2 + CH * c:2 + CH * (c + 1)], bank[c % 2][:, 0:CH], ACT.Copy
                                         ).then_inc(conv_ev, 1)
                if i == 0:
                    weights_hi(2, j * 16 + 16 * NJ + 16)
                else:
                    weights_hi(i - 1, j * 16 + 16 * NJ + 32)

        def gate_steps(dd, last):
            for s in range(2):
                for c in range(NCH):
                    b = c % 2
                    act.wait_ge(gate_mul, dd * 24 + 12 * s + 3 * c + 3)
                    act.wait_ge(gate_ps, dd * 8 + 4 * s + c + 1)
                    for m in range(2):
                        nc.scalar.activation(gt[:, b, m, :], bank[4 * b + m][:, 0:CH], ACT.Sigmoid).then_inc(gate_sig, 1)
                    if c in (1, 2):
                        if s == 0:
                            weights2_hi(c - 1, dd * 16 + 16)
                        elif not last:
                            weights_hi(c - 1, dd * 16 + 32 * NJ + 32)

        with act.Fori(0, KT // 2 - 1) as dd:
            gate_steps(dd, False)
        gate_steps(KT // 2 - 1, True)

    def on_vector(dve):
        def xnT_copy(t):
            dve.wait_ge(xnT_ps, t + 1)
            for h in range(2):
                nc.vector.tensor_tensor(xnT[:, 4 * h:4 * h + 4, TP * t:TP * (t + 1)],
                                        bank[2 * (t % 2) + h][:, 0:4 * TP].rearrange("p (k t) -> p k t", k=4),
                                        vec[:, VEC['ln1_g'] + 4 * h:VEC['ln1_g'] + 4 * h + 4].unsqueeze(2).to_broadcast(
                                            [128, 4, TP]), ALU.mult).then_inc(xnT_done, 1)

        nc.vector.memset(eps_t[:, :], EPS).then_inc(dve_c, 1)
        nc.vector.memset(zero, 0.0).then_inc(dve_c, 1)
        nc.vector.memset(epsx_t[:, :], LNX_EPS).then_inc(dve_c, 1)
        nc.vector.memset(o2[:, :, 0:1], 0.0).then_inc(dve_c, 1)
        nc.vector.memset(ones_t[:, :], 1.0).then_inc(dve_c, 1)
        nc.vector.memset(pc[:, 1:2], 0.0).then_inc(col_free, 1)
        nc.vector.memset(pc[:, 2:3], 0.0).then_inc(dve_c, 1)
        for t in range(NT):
            dve.wait_ge(std0_done, t + 1)
            nc.vector.reciprocal(rstd[:, t:t + 1], rstd[:, t:t + 1]).then_inc(rstd0_done, 1)
            dve.wait_ge(rstd0_done, t + 1)
            if t >= 2:
                dve.wait_ge(xnT_ps, t - 1)
            nc.vector.tensor_scalar(xn[:, t % 2, :], x_in[:, t, :], rstd[:, t:t + 1], None, ALU.mult).then_inc(xn_done, 1)
            if t == 0:
                dve.wait_ge(vec_done, 1)
            if t >= 1:
                xnT_copy(t - 1)
        xnT_copy(NT - 1)
        dve.wait_ge(lora_in, 48)
        for m, (c0, c1_) in enumerate(((0, 64), (64, 128), (128, 256))):
            nc.vector.tensor_tensor(lmu[:, :, c0:c1_], lraw[:, :, c0:c1_],
                                    vec[:, 8 * m:8 * m + 8].unsqueeze(2).to_broadcast([128, KT, c1_ - c0]), ALU.mult
                                    ).then_inc(lmu_done, 1)
        for m in range(2):
            dve.wait_ge(lora_ev, 8 * (m + 1))
            nc.vector.tensor_tensor(o1[:, m, :], o1[:, m, :], o2[:, m, 1:TOK + 1], ALU.subtract).then_inc(lora_mix, 1)
            dve.wait_ge(lora_mix, 2 * m + 1)
            nc.vector.tensor_tensor(o1[:, m, :], o1[:, m, :], o2[:, m, 0:TOK], ALU.add).then_inc(lora_mix, 1)
        dve.wait_ge(lora_done, 3)
        dve.wait_ge(zero_out, shared['zeroed'])

        def tt(label, out, a_, b_, op):
            dve_j.mark(nc.vector.tensor_tensor(out, a_, b_, op), label)

        def stt(label, out, in0, s, in1, op0, op1):
            dve_j.mark(nc.vector.scalar_tensor_tensor(out=out, in0=in0, scalar=s, in1=in1, op0=op0, op1=op1), label)

        def chunks(x):
            return x.rearrange("p (c t) -> p c t", t=TP)

        with dve.Fori(0, NJ) as j:
            nc.vector.memset(pb[:, :, 0:2], 0.0).then_inc(pbz, 1)
            dve.wait_ge(pbz, j + 1)

            def shift_mix(x, dst):
                i = 'rkv'.index(x)
                act_j.done(dve, ('p', x, NCH - 1), j)
                tt(x + '_d', dst[:, :], pb[:, i, 1:TOK + 1], pb[:, i, 2:TOK + 2], ALU.subtract)
                dve_j.done(dve, x + '_d', j)
                stt(x, dst[:, :], dst[:, :], pj('mu_' + x), pb[:, i, 2:TOK + 2], ALU.mult, ALU.add)

            pool_j.done(dve, 'vj', j)
            shift_mix('k', k_t)
            dve_j.done(dve, 'k', j)
            dve_j.mark(nc.vector.tensor_scalar(kk[:, :], k_t[:, :], pj('k_k'), None, ALU.mult), 'kkr')
            for c in range(NT):
                act_j.done(dve, ('z', min(NCH - 1, (TP * (c + 1) - 1) // CH)), j)
                dve_j.mark(nc.vector.tensor_tensor_scan(cs[:, TP * c:TP * (c + 1)], ones_t.to_broadcast([128, TP]), sg[:, TP * c:TP * (c + 1)],
                                                        0.0, ALU.mult, ALU.add), ('cs', c))
            dve_j.done(dve, ('cs', NT - 1), j)
            tt('csx', tmp[:, :], cs[:, :], sg[:, :], ALU.subtract)
            act_j.done(dve, ('a', NCH - 1), j)
            dve_j.mark(nc.vector.tensor_scalar(pb[:, 1, 2:], a_t[:, :], 1.0, pj('k_a'), ALU.subtract, ALU.mult), 'km')
            dve_j.done(dve, 'km', j)
            stt('kmod', k_t[:, :], pb[:, 1, 2:], 1.0, k_t[:, :], ALU.add, ALU.mult)
            act_j.done(dve, ('n', NCH - 1), j)
            dve_j.mark(nc.vector.tensor_scalar(nrm[:, :], nrm[:, :], 1e-12, None, ALU.max), 'nmax')
            dve_j.done(dve, 'nmax', j)
            dve_j.mark(nc.vector.reciprocal(nrm[:, :], nrm[:, :]), 'nrec')
            dve_j.done(dve, 'nrec', j)
            tt('kk', kk[:, :], kk[:, :], nrm[:, :], ALU.mult)
            dve_j.done(dve, 'kk', j)
            act_j.done(dve, 'E0', j)
            stt('at', ar[:, :, 0, :], chunks(kk[:, :]), -1.0, chunks(e0[:, :]), ALU.mult, ALU.mult)
            tt('ba', tmp[:, :], kk[:, :], a_t[:, :], ALU.mult)
            dve_j.done(dve, 'ba', j)
            tt('bh', bh[:, :], tmp[:, :], e2[:, :], ALU.mult)
            tt('kh', kh[:, :], k_t[:, :], e2[:, :], ALU.mult)
            dve_j.mark(nc.vector.tensor_copy(pc[:, :], chunks(e1[:, :])[:, :, TP - 1]), 'pc')
            shift_mix('r', r_t)
            dve_j.done(dve, 'r', j)
            stt('rkb', rkb[:, :], r_t[:, :], pj('r_k'), k_t[:, :], ALU.mult, ALU.mult)
            tt('rt', ar[:, :, 1, :], chunks(r_t[:, :]), chunks(e1[:, :]), ALU.mult)
            shift_mix('v', v_t)
            for u in range(NU):
                pe_j.done(dve, ('A', u), j)
                if u == 0:
                    dve_j.done(dve, 'v', j)
                tt(('A', u), AT[:, u, :, :], bank[4 + u % 4][0:TP, 0:4 * TP].rearrange("p (m t) -> p m t", m=4), mask4[:, :, :],
                   ALU.mult)
            for l in range(LEVELS):
                for s in range(NB + 1):
                    if s < NB:
                        pe_j.done(dve, ('P', l, s), j)
                        if l == 0 and s >= 2:
                            dve_j.done(dve, ('T', 0, s - 2), j)
                        elif l == 1 and s < 2:
                            dve_j.done(dve, ('T', 0, 4 - s), j)
                        tt(('P', l, s), P1[:, s % 2, :, :], bank[2 + s % 2][0:TP, 0:4 * TP].rearrange("p (m t) -> p m t", m=4),
                           mlev[:, l, 0:TP].unsqueeze(1).to_broadcast([TP, 4, TP]), ALU.mult)
                    if s > 0:
                        b = s - 1
                        pe_j.done(dve, ('D', l, b), j)
                        if l > 0:
                            dve_j.done(dve, ('R', l - 1, b), j)
                        else:
                            pool_j.done(dve, 'R0', j)
                        for x, m, bk in (('T', Tm, 4), ('R', Rm, 6)):
                            if l == LEVELS - 1 and x == 'T':
                                continue
                            new = bank[bk + b % 2][0:TP, 0:4 * TP].rearrange("p (m t) -> p m t", m=4)
                            if l == 0 and x == 'T':
                                new = P1[:, b % 2, :, :]
                                dve_j.done(dve, ('P', l, b), j)
                            tt((x, l, b), m[:, 4 * b:4 * b + 4, :], new, m[:, 4 * b:4 * b + 4, :], ALU.add)
            for g in range(2):
                pe_j.done(dve, ('m', g), j)
                tt(('m', g), mxt[:, 5 * g:5 * g + 5, :], bank[2 + g][:, 0:5 * HS].rearrange("p (c n) -> p c n", n=HS),
                   id2.unsqueeze(1).to_broadcast([128, 5, HS]), ALU.add)
            for g in range(2):
                pe_j.done(dve, ('nn', g), j)
                tt(('nn', g), np_[:, 5 * g:5 * g + 5, :], bank[4 + g][:, 0:5 * HS].rearrange("p (c n) -> p c n", n=HS),
                   pc[:, 5 * g:5 * g + 5].unsqueeze(2).to_broadcast([128, 5, HS]), ALU.mult)
            dve_j.mark(nc.vector.memset(S[:, 0, :], 0.0), 'S0')
            dve_j.done(dve, ('nn', 0), j)
            dve_j.mark(nc.vector.tensor_copy(S[:, 1, :], np_[:, 0, :]), ('S', 0))
            for c in range(1, NT):
                pe_j.done(dve, ('s', c), j)
                if c == 5:
                    dve_j.done(dve, ('nn', 1), j)
                stt(('S', c), S[:, c + 1, :], bank[6 + c % 2][:, 0:HS], pc[:, c:c + 1], np_[:, c, :], ALU.mult, ALU.add)
            for g in range(2):
                pe_j.done(dve, ('u', g), j)
                for h in range(2):
                    tt(('u', g, h), U.rearrange("p (c h) n -> p c h n", h=2)[:, 5 * g:5 * g + 5, h, :],
                       bank[2 + 2 * g + h][0:TP, 0:5 * HS].rearrange("p (c n) -> p c n", n=HS),
                       X.rearrange("p (c h) n -> p c h n", h=2)[:, 5 * g:5 * g + 5, h, HS:128], ALU.add)
            for c in range(NCH):
                pe_j.done(dve, ('bs', c), j)
                tt(('bo', c), kk[:, CH * c:CH * (c + 1)], bank[2 + c][:, 0:CH], v_t[:, CH * c:CH * (c + 1)], ALU.mult)
            for c in range(NCH):
                pe_j.done(dve, ('mean', c), j)
                stt(('yc', c), y_t[:, CH * c:CH * (c + 1)], bank[2 + c][:, 0:CH], -1.0 / HS, y_t[:, CH * c:CH * (c + 1)],
                    ALU.mult, ALU.add)
            act_j.done(dve, ('var', NCH - 1), j)
            nc.vector.memset(dz[:, 3:4], 0.0).then_inc(late_free, 1)
            dve_j.mark(nc.vector.reciprocal(nrm[:, :], nrm[:, :]), 'yrec')
            dve_j.done(dve, 'yrec', j)
            tt('yn', y_t[:, :], y_t[:, :], nrm[:, :], ALU.mult)
            dve_j.done(dve, 'yn', j)
            dve_j.mark(nc.vector.tensor_scalar(y_t[:, :], y_t[:, :], pj('lnx_g'), pj('lnx_b'), ALU.mult, ALU.add), 'yaff')
            dve_j.done(dve, 'yaff', j)
            tt('ysum', y_t[:, :], y_t[:, :], kk[:, :], ALU.add)
            dve_j.done(dve, 'ysum', j)
            for c in range(NCH):
                pe_j.done(dve, ('g', c), j)
                tt(('yg', c), yg[:, bass.ds(j, 1), CH * c:CH * (c + 1)].rearrange("p a t -> p (a t)"),
                   bank[(0, 1, 6, 7)[c]][:, 0:CH], y_t[:, CH * c:CH * (c + 1)], ALU.mult)
            nc.vector.memset(dz[:, 0:1], 0.0).then_inc(col_free, 1)
        def tokens_lo(c):
            dve.wait_ge(xm_hi_done, c + 1)
            t = slice(CH * c, CH * (c + 1))
            nc.vector.tensor_tensor(xm_lo[:, :, t], xnT[:, :, t], xm_hi[:, :, t].bitcast(f32), ALU.subtract
                                    ).then_inc(xm_lo_done, 1)

        def weights_lo(i, n):
            dve.wait_ge(ring_hi_done, n)
            nc.vector.tensor_tensor(ring_lo[:, i, :, :], ring[:, i, :, :], ring_hi[:, i, :, :].bitcast(f32), ALU.subtract
                                    ).then_inc(ring_lo_done, 1)

        def weights2_lo(i, n):
            dve.wait_ge(ring2_hi_done, n)
            nc.vector.tensor_tensor(ring2_lo[:, i, :, :], ring2[:, i, :, :], ring2_hi[i][:, :, :].bitcast(f32), ALU.subtract
                                    ).then_inc(ring2_lo_done, 1)

        dve.wait_ge(k_ps, NCH * (NJ + 1))
        tokens_lo(0)
        weights_lo(0, 1)
        weights_lo(1, 2)
        for c in range(1, NCH):
            tokens_lo(c)
        nc.vector.memset(cpb[:, :, 0:2], 0.0).then_inc(conv_step, 2)
        nc.vector.memset(dz[:, 1:2], 0.0).then_inc(conv_step, 4)
        with dve.Fori(0, NJ) as j:
            weights_lo(2, j * 3 + 3)
            weights_lo(0, j * 3 + 4)
            dve.wait_ge(conv_ev, j * 12 + 12)
            nc.vector.tensor_tensor(cpb[:, 1, 2:], cpb[:, 1, 2:], cpb[:, 2, 2:], ALU.mult).then_inc(conv_step, 1)
            dve.wait_ge(conv_step, j * 6 + 7)
            for w in range(3):
                scal = vec[:, VEC['conv_w'] + 4 * w:VEC['conv_w'] + 4 * w + 4][:, bass.ds(j, 1)]
                if w == 0:
                    ins = nc.vector.tensor_scalar(c1[:, :], cpb[:, 1, 0:TOK], scal, None, ALU.mult)
                else:
                    ins = nc.vector.scalar_tensor_tensor(out=c1[:, :], in0=cpb[:, 1, w:w + TOK], scalar=scal, in1=c1[:, :],
                                                         op0=ALU.mult, op1=ALU.add)
                ins.then_inc(conv_step, 1)
                dve.wait_ge(conv_step, j * 6 + 8 + w)
            nc.vector.tensor_tensor(cv[:, bass.ds(j, 1), :].rearrange("p a t -> p (a t)"), cpb[:, 0, 2:], c1[:, :], ALU.mult
                                    ).then_inc(conv_step, 2)
            weights_lo(1, j * 3 + 5)
        nc.vector.memset(dz[:, 2:3], 0.0).then_inc(gate_mul, 6)

        def gate_steps(dd, last):
            for s in range(2):
                for c in range(NCH):
                    b = c % 2
                    dve.wait_ge(gate_sig, dd * 16 + 8 * s + 2 * c + 2)
                    for m in range(2):
                        nc.vector.tensor_tensor(gt[:, b, m, :], gt[:, b, m, :], bank[4 * b + 2 + m][:, 0:CH], ALU.mult
                                                ).then_inc(gate_mul, 1)
                    dve.wait_ge(gate_mul, dd * 24 + 12 * s + 3 * c + 8)
                    nc.vector.tensor_tensor(mT[:, bass.ds(2 * dd + s, 1), CH * c:CH * (c + 1)].rearrange("p a t -> p (a t)"),
                                            gt[:, b, 0, :], gt[:, b, 1, :], ALU.add).then_inc(gate_mul, 1)
                    if c in (1, 2):
                        if s == 0:
                            weights2_lo(c - 1, dd * 2 + c)
                        elif not last:
                            weights_lo(c - 1, dd * 2 + 3 * NJ + 2 + c)

        with dve.Fori(0, KT // 2 - 1) as dd:
            gate_steps(dd, False)
        gate_steps(KT // 2 - 1, True)

    def on_tensor(pe):
        pe.wait_ge(pool_c, 2)
        pe.wait_ge(vec_in, 16 * 15)
        nc.tensor.transpose(bank[7][:, 0:84], vrows[:, :], ident[0:84, 0:84]).then_inc(vec_ps, 1)
        for t in range(NT):
            pe.wait_ge(xn_done, t + 1)
            if t >= 2:
                pe.wait_ge(xnT_done, 2 * (t - 1))
            for k in range(KT):
                ins = nc.tensor.transpose(bank[2 * (t % 2) + k // 4][:, (k % 4) * TP:(k % 4 + 1) * TP],
                                          xn[:, t % 2, 128 * k:128 * (k + 1)], ident[0:TP, 0:TP])
            ins.then_inc(xnT_ps, 1)
        pe.wait_ge(xnT_done, 2 * NT)
        pe.wait_ge(lmu_done, 3)
        for m in range(2):
            for c in range(NCH):
                if 4 * m + c >= 2:
                    pe.wait_ge(lora_ev, 2 * (4 * m + c) - 2)
                for w, b in ((lraw, 0), (lmu, 2)):
                    for k in range(KT):
                        ins = nc.tensor.matmul(bank[b + c % 2][:, 0:CH], w[:, k, 128 * m:128 * (m + 1)],
                                               xnT[:, k, CH * c:CH * (c + 1)], start=k == 0, stop=k == KT - 1)
                ins.then_inc(lora_ps, 1)
        def mm(ps, lhsT, rhs, start=True, stop=True):
            return nc.tensor.matmul(ps, lhsT, rhs, start=start, stop=stop)

        def hp(h):
            return slice(HS * h, HS * (h + 1))

        def tp(c):
            return slice(TP * c, TP * (c + 1))

        def project_keys():
            for c in range(NCH):
                for k in range(KT):
                    ins = mm(bank[2 + c][:, 0:CH], ring[:, 1, k, :], xnT[:, k, CH * c:CH * (c + 1)], k == 0, k == KT - 1)
                ins.then_inc(k_ps, 1)

        pe.wait_ge(ring_in[1], 16)
        pe.wait_ge(lora_ev, 16)
        project_keys()
        pe.wait_ge(lora_done, 3)
        with pe.Fori(0, NJ) as j:
            pool_j.done(pe, 'wg2', j)
            pe.wait_ge(col_free, j + 1)
            for c in range(NCH):
                if c >= 2:
                    act_j.done(pe, ('a', c - 2), j)
                mm(bank[c % 2][:, 0:CH], w2j[0:64, :], lw[0:64, CH * c:CH * (c + 1)])
                pe_j.mark(mm(bank[6 + c % 2][:, 0:CH], w2j[64:128, :], lw[64:128, CH * c:CH * (c + 1)]), ('z', c))
            for q in range(2 * NCH):
                x, c = 'rv'[q // NCH], q % NCH
                if c == 0:
                    pe.wait_ge(ring_in['rkv'.index(x)], j * 16 + 16)
                if q < 2:
                    act_j.done(pe, ('z', 2 + c), j)
                else:
                    act_j.done(pe, ('p', 'rv'[(q - 2) // NCH], (q - 2) % NCH), j)
                for k in range(KT):
                    ins = mm(bank[c % 2][:, 0:CH], ring[:, 'rkv'.index(x), k, :], xnT[:, k, CH * c:CH * (c + 1)], k == 0, k == KT - 1)
                pe_j.mark(ins, ('p', x, c))
                if q == 1:
                    act_j.done(pe, 'sq', j)
                    for b in range(NCH):
                        pe_j.mark(mm(bank[4 + b][:, 0:CH], bones[:, :], nrm[:, CH * b:CH * (b + 1)]), ('n', b))
            dve_j.done(pe, 'bh', j)
            q = 0
            for x in TA:
                if x == 'v':
                    dve_j.done(pe, 'v', j)
                for g, (g0, g1) in enumerate(evac_groups()):
                    if q >= 2:
                        act_j.done(pe, ('t', TA[(q - 2) // 3], (q - 2) % 3), j)
                    for c in range(g0, g1):
                        src = dict(v=v_t, b=bh, k=kh)[x][:, tp(c)] if x != 'a' else ar[:, c, 0, :]
                        ins = nc.tensor.transpose(bank[2 + q % 2][0:TP, 128 * (c - g0):128 * (c - g0 + 1)], src, ident[:, :])
                    pe_j.mark(ins, ('t', x, g))
                    q += 1
            for u in range(NU):
                c, h = u // 2, u % 2
                if u >= 4:
                    dve_j.done(pe, ('A', u - 4), j)
                b = bank[4 + u % 4]
                mm(b[0:TP, 0:2 * TP], bh[hp(h), tp(c)], ar[hp(h), c, :, :].rearrange("p m t -> p (m t)"))
                pe_j.mark(mm(b[0:TP, 2 * TP:4 * TP], kh[hp(h), tp(c)], ar[hp(h), c, :, :].rearrange("p m t -> p (m t)")),
                          ('A', u))
            dve_j.done(pe, ('A', NU - 1), j)
            act_j.done(pe, ('t', 'v', 2), j)
            pool_j.done(pe, 'R0', j)
            for l in range(LEVELS):
                for s in range(NB + 1):
                    if s < NB:
                        if l > 0:
                            dve_j.done(pe, ('T', l - 1, s), j)
                            if s < 2:
                                dve_j.done(pe, ('P', l - 1, 4 - s), j)
                        if s >= 2:
                            dve_j.done(pe, ('P', l, s - 2), j)
                        for m in range(4):
                            u = 4 * s + m
                            ins = mm(bank[2 + s % 2][0:TP, TP * m:TP * (m + 1)], AT[:, u, 0, :], Tm[:, u, :])
                        pe_j.mark(ins, ('P', l, s))
                    if s > 0:
                        b = s - 1
                        dve_j.done(pe, ('P', l, b), j)
                        if b >= 2:
                            dve_j.done(pe, ('R', l, b - 2), j)
                        elif l > 0:
                            dve_j.done(pe, ('R', l - 1, 4 - b), j)
                        for m in range(4):
                            u = 4 * b + m
                            if 0 < l < LEVELS - 1:
                                mm(bank[4 + b % 2][0:TP, TP * m:TP * (m + 1)], Rm[:, u, :], P1[:, b % 2, m, :])
                            ins = mm(bank[6 + b % 2][0:TP, TP * m:TP * (m + 1)], P1[:, b % 2, m, :], Rm[:, u, :])
                        pe_j.mark(ins, ('D', l, b))
            dve_j.done(pe, ('R', LEVELS - 1, NB - 1), j)
            for g, (g0, g1) in enumerate(((0, 8), (8, 16), (16, 20))):
                if g == 2:
                    act_j.done(pe, ('xa', 0), j)
                for u in range(g0, g1):
                    ins = mm(bank[2 + g % 2][0:TP, HS * (u - g0):HS * (u - g0 + 1)], AT[:, u, 2, :], Vt[:, u // 2, hp(u % 2)])
                pe_j.mark(ins, ('xa', g))
            for g, (g0, g1) in enumerate(evac_groups()):
                if g == 2:
                    act_j.done(pe, ('xc', 0), j)
                for c in range(g0, g1):
                    for h in range(2):
                        ins = mm(bank[4 + g % 2][hp(h), TP * (c - g0):TP * (c - g0 + 1)], X[:, 2 * c + h, 0:HS],
                                 Rm[:, 2 * c + h, :])
                pe_j.mark(ins, ('xc', g))
            act_j.done(pe, ('xa', 2), j)
            for g in range(5):
                if g >= 2:
                    act_j.done(pe, ('xb', g - 2), j)
                for m in range(4):
                    u = 4 * g + m
                    ins = mm(bank[6 + g % 2][0:TP, 128 * m:128 * (m + 1)], Rm[:, u, :], X[:, u, :])
                pe_j.mark(ins, ('xb', g))
            act_j.done(pe, ('xb', 4), j)
            for g in range(2):
                for c in range(5 * g, 5 * g + 5):
                    for h in range(2):
                        ins = mm(bank[2 + g][hp(h), HS * (c % 5):HS * (c % 5 + 1)], X[:, 2 * c + h, 0:HS], Bt[:, c, hp(h)])
                pe_j.mark(ins, ('m', g))
            for g in range(2):
                for c in range(5 * g, 5 * g + 5):
                    for h in range(2):
                        o = bank[4 + g][hp(h), HS * (c % 5):HS * (c % 5 + 1)]
                        mm(o, Bt[:, c, hp(h)], X[:, 2 * c + h, HS:128], True, False)
                        ins = mm(o, Kt[:, c, hp(h)], Vt[:, c, hp(h)], False, True)
                pe_j.mark(ins, ('nn', g))
            dve_j.done(pe, ('m', 1), j)
            for c in range(1, NT):
                dve_j.done(pe, ('S', c - 1), j, pe_passed)
                for h in range(2):
                    ins = mm(bank[6 + c % 2][hp(h), 0:HS], mxt[hp(h), c, :], S[hp(h), c, :])
                pe_j.mark(ins, ('s', c))
            dve_j.done(pe, ('nn', 1), j)
            for g in range(2):
                for c in range(5 * g, 5 * g + 5):
                    for h in range(2):
                        ins = mm(bank[2 + 2 * g + h][0:TP, HS * (c % 5):HS * (c % 5 + 1)], x1t[hp(h), c, :], S[hp(h), c, :])
                pe_j.mark(ins, ('u', g))
            dve_j.done(pe, ('u', 1, 1), j, pe_passed)
            for g, (g0, g1) in enumerate(evac_groups()):
                if g == 2:
                    act_j.done(pe, ('y', 0), j, pe_passed)
                for c in range(g0, g1):
                    for h in range(2):
                        u = 2 * c + h
                        o = bank[6 + g % 2][hp(h), TP * (c - g0):TP * (c - g0 + 1)]
                        mm(o, S[hp(h), c, :], ar[hp(h), c, 1, :], True, False)
                        mm(o, U[:, u, :], AT[:, u, 1, :], False, False)
                        ins = mm(o, Vt[:, c, hp(h)], AT[:, u, 3, :], False, True)
                pe_j.mark(ins, ('y', g))
            for c in range(NCH):
                pe_j.mark(mm(bank[2 + c][:, 0:CH], bones[:, :], rkb[:, CH * c:CH * (c + 1)]), ('bs', c))
            act_j.done(pe, ('y', 2), j)
            for c in range(NCH):
                pe_j.mark(mm(bank[(0, 1, 6, 7)[c]][:, 0:CH], wg2j[:, :], lg[:, CH * c:CH * (c + 1)]), ('g', c))
            for c in range(NCH):
                dve_j.done(pe, ('bo', c), j)
                pe_j.mark(mm(bank[2 + c][:, 0:CH], bones[:, :], y_t[:, CH * c:CH * (c + 1)]), ('mean', c))
            act_j.done(pe, 'ysq', j)
            for c in range(NCH):
                if c >= 2:
                    act_j.done(pe, ('var', c - 2), j)
                pe_j.mark(mm(bank[4 + c % 2][:, 0:CH], bones[:, :], tmp[:, CH * c:CH * (c + 1)]), ('var', c))
            pe.wait_ge(late_free, j + 1)
            pe.wait_ge(ring_in[1], j * 16 + 32)
            project_keys()
        pe.wait_ge(col_free, NJ + 1)

        def three(ps, w_hi, w_lo, t, start, stop):
            mm(ps, w_hi, xm_hi[:, t[0], t[1]], start, False)
            mm(ps, w_hi, xm_lo[:, t[0], t[1]], False, False)
            return mm(ps, w_lo, xm_hi[:, t[0], t[1]], False, stop)

        with pe.Fori(0, NJ) as j:
            for i in range(3):
                pe.wait_ge(ring_lo_done, j * 3 + i + 1)
                for c in range(NCH):
                    if i == 0:
                        pe.wait_ge(xm_lo_done, c + 1)
                    if 4 * i + c >= 2:
                        pe.wait_ge(conv_ev, j * 12 + 4 * i + c - 1)
                    for k in range(KT):
                        ins = three(bank[c % 2][:, 0:CH], ring_hi[:, i, k, :], ring_lo[:, i, k, :],
                                    (k, slice(CH * c, CH * (c + 1))), k == 0, k == KT - 1)
                    ins.then_inc(conv_ps, 1)
            pe.wait_ge(conv_ev, j * 12 + 12)
        pe.wait_ge(conv_step, 6 * NJ + 6)

        def gate_steps(dd):
            for s in range(2):
                if s == 0:
                    pe.wait_ge(ring_in[2], dd * 32 + 32 + 32 * NJ)
                    pe.wait_ge(ring_lo_done, dd * 2 + 3 * NJ + 2)
                else:
                    pe.wait_ge(ring2_in[2], dd * 32 + 32)
                    pe.wait_ge(ring2_lo_done, dd * 2 + 2)
                for c in range(NCH):
                    b = 4 * (c % 2)
                    pe.wait_ge(gate_mul, dd * 24 + 12 * s + 3 * c + 3)
                    t = slice(CH * c, CH * (c + 1))
                    for i in range(2):
                        for k in range(KT):
                            if s == 0:
                                w_hi, w_lo = ring_hi[:, i, k, :], ring_lo[:, i, k, :]
                            else:
                                w_hi, w_lo = ring2_hi[i][:, k, :], ring2_lo[:, i, k, :]
                            three(bank[b + i][:, 0:CH], w_hi, w_lo, (k, t), k == 0, k == KT - 1)
                    for i, src in enumerate((yg, cv)):
                        for k in range(4):
                            ins = mm(bank[b + 2 + i][:, 0:CH], (ring, ring2)[s][:, 2, 4 * i + k, :], src[:, k, t],
                                     k == 0, k == 3)
                    ins.then_inc(gate_ps, 1)

        with pe.Fori(0, KT // 2 - 1) as dd:
            gate_steps(dd)
        gate_steps(KT // 2 - 1)

    return on_sync, on_gpsimd, on_scalar, on_vector, on_tensor


def experts_program(nc, ctx, a, bank, shared, out):
    f32 = mybir.dt.float32
    f32r = mybir.dt.float32r
    u32 = mybir.dt.uint32
    ALU = mybir.AluOpType
    ACT = mybir.ActivationFunctionType
    AX = mybir.AxisListType

    D = 1024
    META = 16
    TOK = 1040
    NT = 10
    TP = TOK // NT
    KT = D // 128
    E = 32
    TOPK = 4
    LIMIT = 7.0
    ALPHA = 1.702
    EPS = 1e-5
    ROWS = 128
    MAXR = E + TOK * TOPK // (2 * ROWS) + 1
    MAXB = shared['blocks']
    HK, HC = 4, 512
    NPIECE = 12
    NRING = 4
    NGOT = 5

    ident, eps_t, h_all, zero_out, wo_add = shared['ident'], shared['eps_t'], shared['h_all'], shared['zero_out'], shared['wo_add']
    ln2_g, w_router, b_router, lnf_g = a['ln2_g'], a['w_router'], a['b_router'], a['lnf_g']
    w_gate, b_gate, w_up, b_up, w_down, b_down = (a[x] for x in ('w_e_gate', 'b_e_gate', 'w_e_up', 'b_e_up', 'w_e_down', 'b_e_down'))
    hn_d, ys_d, rowtok_d, bias_d = shared['hn_d'], shared['ys_d'], shared['rowtok_d'], shared['bias_d']

    def sem(name):
        return ctx.enter_context(nc.semaphore(name))

    gate_ps, up_ps, y_ps, tx_ps, ta_ps = bank[0:2], bank[2:4], (bank[4:6], bank[2:4]), bank[6], bank[7]

    mT, wo_t = shared['mT'], shared['wo_t']
    raw_at = shared['after_h']
    sb = Plan(nc, raw_at + (4 * KT * TOK + 31) // 32 * 32)
    gates, dest = shared["gates"], shared["dest"]
    tok_id = sb("tok_id", [TP, NT], u32)
    table = sb("table", [1, MAXR + 2], u32)
    starts = sb("starts", [1, MAXR + 2], u32)
    kind_row = sb("kind_row", [6, 3, ROWS], f32r)
    fss = sb("fss", [TP, NT])
    frs = sb("frs", [TP, NT])

    dump = sb("dump_e", [128, 16])

    rt = Plan(nc, sb.at)
    hn = rt("hn", [TP, 2, D])
    junk = rt("junk_e", [TP, D])
    g2_b = rt("g2_b", [TP, D])
    assert rt.at <= shared['after_wo'] - 4 * KT * D
    rt = Plan(nc, shared['after_wo'])
    bias_rows = rt("bias_rows", [E, 3, D])
    bias_hi = rt("bias_hi", [E, 3, D], f32r)
    bias_lo = rt("bias_lo", [E, 3, D], f32r)
    kind_f = rt("kind_f", [6, 3, ROWS])
    wr_t = rt("wr_t", [128, KT, E])
    hnT = rt("hnT", [128, 2, KT, TP])
    ss = rt("ss_e", [TP, NT])
    rstd = rt("rstd_e", [TP, NT])
    top_v = rt("top_v", [TP, NT, 8])
    top_i = rt("top_i", [TP, NT, 8], u32)
    lg = rt("lg", [TP, 2, E])
    br_b = rt("br_b", [TP, E])
    iota_e = rt("iota_e", [TP, E])
    onehot = rt("onehot", [TP, NT * TOPK, E])
    chosen = rt("chosen", [TP, NT, E])
    before = rt("before", [TP, NT + 1, E])
    rank = rt("rank", [TP, NT, E])
    tri = rt("tri", [TP, TP])
    ones = rt("ones", [TP, 128])
    top_f = rt("top_f", [TP, NT * TOPK])
    cnt = rt("cnt", [TP, E])
    over = rt("over", [TP, E])
    pairs = rt("pairs", [TP, E])
    pair_end = rt("pair_end", [TP, E])
    pair_rows = rt("pair_rows", [TP, E])
    pair_base = rt("pair_base", [TP, E])
    singles = rt("singles", [TP, E])
    single_end = rt("single_end", [TP, E])
    single_base = rt("single_base", [TP, E])
    in_single = rt("in_single", [TP, NT, E])
    dest_f = rt("dest_f", [TP, NT * TOPK])
    gsum = rt("gsum", [TP, NT])
    iota_q = rt("iota_q", [1, MAXR + 1])
    ended = rt("ended", [1, MAXR + 1, E])
    table_f = rt("table_f", [1, MAXR + 1])
    table_s = rt("table_s", [1, MAXR + 1])
    start_f = rt("start_f", [1, MAXR + 1])
    total_f = rt("total_f", [1, 1])
    assert rt.at <= 229344, rt.at

    raw = Plan(nc, raw_at)("raw", [128, NRING, HK, HC])
    assert NRING * HK * HC <= KT * TOK
    ex = Plan(nc, sb.at)
    w_hi = ex("w_hi", [128, NRING, HK, HC], f32r)
    w_lo = ex("w_lo", [128, NRING, HK, HC], f32r)
    x_rows = ex("x_rows", [ROWS, 2, D])
    x_hi = ex("x_hi", [128, 2, KT, ROWS], f32r)
    x_lo = ex("x_lo", [128, 2, KT, ROWS], f32r)
    g_t = ex("g_t", [ROWS, 2, HC])
    s_t = ex("s_t", [ROWS, 2, HC])
    u_t = ex("u_t", [ROWS, 2, HC])
    a_hi = ex("a_hi", [128, 2, KT, ROWS], f32r)
    a_lo = ex("a_lo", [128, 2, KT, ROWS], f32r)
    y_rows = ex("y_rows", [ROWS, 2, D])
    bias_t = ex("bias_t", [6, D], f32r)
    idx_t = ex("idx_t", [ROWS, 2], u32)
    assert ex.at <= 229344, ex.at

    fi = Plan(nc, sb.at)
    y_got = fi("y_got", [TP, NGOT, TOPK, D])
    fin_junk = fi("fin_junk", [TP, D])
    gf_b = fi("gf_b", [TP, D])
    fin = fi("fin", [TP, 2, D])

    h_in, wo_in, gate_mul = shared['h_in'], shared['wo_in'], shared['gate_mul']
    wo_ps = sem("wo_ps")
    const_in = sem("const_in")
    bias_in = sem("bias_in")
    pool_const = sem("pool_const")
    dve_const = sem("dve_const")
    sq_done = sem("sq_done")
    std_done = sem("std_done")
    rstd_done = sem("rstd_done")
    hn_done = sem("hn_done")
    hn_out = [sem("hn_out0"), sem("hn_out1")]
    hnT_ps = sem("hnT_ps")
    hnT_done = sem("hnT_done")
    logit_ps = sem("logit_ps")
    lg_read = sem("lg_read")
    top_done = sem("top_done")
    route = sem("route")
    gexp_in = sem("gexp_in")
    gexp_done = sem("gexp_done")
    chosen_done = sem("chosen_done")
    rank_ps = sem("rank_ps")
    dest_done = sem("dest_done")
    table_done = sem("table_done")
    scattered = sem("scattered")
    bias_hi_done = sem("bias_hi_done")
    bias_lo_done = sem("bias_lo_done")
    bias_out = sem("bias_out")
    kind_done = sem("kind_done")

    def sems(name, n):
        return [sem(f"{name}{i}") for i in range(n)]

    raw_in = sems("raw_in", NRING)
    hi_done = sem("hi_done")
    lo_done = sem("lo_done")
    piece_used = sem("piece_used")
    bias_got = sem("bias_got")
    gu_read = sems("gu_read", 2)
    sig_done = sems("sig_done", 2)
    glu_mid = sems("glu_mid", 2)
    glu_done = sems("glu_done", 2)
    aT_ps = sems("aT_ps", 2)
    ahi_done = sems("ahi_done", 2)
    alo_done = sems("alo_done", 2)
    y_read = sems("y_read", 2)
    pe_passed = sem("pe_passed_e")
    idx_in = sems("idx_in", 2)
    rows_in = sems("rows_in", 2)
    xT_ps = sems("xT_ps", 4)
    xhi_done = sems("xhi_done", 4)
    xlo_done = sems("xlo_done", 4)
    sp_passed = sem("sp_passed_e")
    pool_passed = sem("pool_passed_e")
    y_out = sem("y_out")

    gf_in = sem("gf_in")
    got_in = [sem(f"got_in{s}") for s in range(NGOT)]
    sum_done = sem("sum_done")
    fsq_done = sem("fsq_done")
    fstd_done = sem("fstd_done")
    frs_done = sem("frs_done")
    fin_done = sem("fin_done")
    out_done = [sem("out_done0"), sem("out_done1")]

    X_AFTER = {1: (7, 9), 2: (7, 8, 9, 10)}

    def piece_of(j):
        if j < 8:
            return (w_gate, w_up)[j // 2 % 2], HK * (j % 2), HC * (j // 4)
        return w_down, HK * ((j - 8) // 2), HC * (j % 2)

    def on_sync(sp):
        sp.dma_start(g2_b, ln2_g.partition_broadcast(TP)).then_inc(const_in, 16)
        sp.dma_start(br_b, b_router.partition_broadcast(TP)).then_inc(const_in, 16)
        sp.dma_start(wr_t, w_router.rearrange("(k p) e -> p k e", p=128)).then_inc(const_in, 16)
        for a, b in enumerate((b_gate, b_up, b_down)):
            sp.dma_start(bias_rows[:, a, :], b).then_inc(bias_in, 16)
        bias_rows_d = bias_d.rearrange("e (n s) c -> e n s c", s=2)
        for t in range(NT):
            sp.wait_ge(hn_done, t + 1)
            sp.dma_start(hn_d[TP * t:TP * (t + 1), :], hn[:, t % 2, :]).then_inc(hn_out[t % 2], 16)
            if t == 5:
                sp.wait_ge(bias_hi_done, 1)
                sp.dma_start(bias_rows_d[:, :, 0, :], bias_hi.bitcast(f32)).then_inc(bias_out, 16)
                sp.wait_ge(bias_lo_done, 1)
                sp.dma_start(bias_rows_d[:, :, 1, :], bias_lo.bitcast(f32)).then_inc(bias_out, 16)
        sp.wait_ge(table_done, 1)
        n_pairs = sp.value_load(starts[0:1, MAXR + 1:MAXR + 2], min_val=1, max_val=E)
        rounds = sp.value_load(table[0:1, MAXR + 1:MAXR + 2], min_val=2, max_val=MAXR - 1)
        sp.wait_ge(hn_out[0], 16 * (NT // 2))
        sp.wait_ge(hn_out[1], 16 * (NT // 2))

        sp.wait_ge(bias_out, 32)

        def load(e_reg, n, j):
            w, k0, c0 = piece_of(j)
            sp.wait_ge(lo_done, n + 1)
            sp.sem_inc(sp_passed, 1)
            sp.dma_start(raw[:, j % NRING, :, :],
                         w[bass.ds(e_reg, 1), k0 * 128:(k0 + HK) * 128, c0:c0 + HC].rearrange("a (k p) c -> p (a k) c", p=128)
                         ).then_inc(raw_in[j % NRING], 16)

        e0 = sp.value_load(table[0:1, 0:1], min_val=0, max_val=E - 1)
        for j in range(NRING):
            load(e0, j, j)
        for first, last in ((0, n_pairs), (n_pairs, rounds)):
            with sp.Fori(first, last) as r:
                e = sp.value_load(table[0:1, bass.ds(r, 1)], min_val=0, max_val=E - 1)
                e_next = sp.value_load(table[0:1, bass.ds(r + 1, 1)], min_val=0, max_val=E - 1)
                for j in range(NRING, NPIECE + NRING):
                    load(e if j < NPIECE else e_next, r * NPIECE + j, j % NPIECE)
        sp.wait_ge(piece_used, rounds * NPIECE + NRING)
        sp.sem_inc(sp_passed, 1)
        sp.dma_start(gf_b, lnf_g.partition_broadcast(TP)).then_inc(gf_in, 16)
        for t in range(NT):
            sp.wait_ge(fin_done, t + 1)
            if t == 0:
                sp.dma_start(out[0:TP - META, :], fin[META:TP, 0, :]).then_inc(out_done[0], 16)
            else:
                sp.dma_start(out[TP * t - META:TP * (t + 1) - META, :], fin[:, t % 2, :]).then_inc(out_done[t % 2], 16)
        sp.wait_ge(out_done[0], 16 * (NT // 2))
        sp.wait_ge(out_done[1], 16 * (NT // 2))

    def on_gpsimd(pool):
        pool.wait_ge(gate_mul, 3 * KT * 4 + 6)
        nc.gpsimd.memset(tri, 1.0).then_inc(pool_const, 1)
        pool.wait_ge(pool_const, 1)
        nc.gpsimd.affine_select(out=tri, in_=tri, compare_op=ALU.is_gt, fill=0.0, base=0,
                                pattern=[[1, TP]], channel_multiplier=-1).then_inc(pool_const, 1)
        nc.gpsimd.iota(tok_id[:, :], pattern=[[TP, NT]], base=0, channel_multiplier=1).then_inc(pool_const, 1)
        nc.gpsimd.iota(iota_e, pattern=[[1, E]], base=0, channel_multiplier=0,
                       allow_small_or_imprecise_dtypes=True).then_inc(pool_const, 1)
        nc.gpsimd.iota(iota_q, pattern=[[1, MAXR + 1]], base=0, channel_multiplier=0,
                       allow_small_or_imprecise_dtypes=True).then_inc(pool_const, 1)
        nc.gpsimd.memset(kind_f, 1.0).then_inc(pool_const, 1)
        pool.wait_ge(pool_const, 6)
        nc.gpsimd.affine_select(out=kind_f, in_=kind_f, compare_op=ALU.is_ge, fill=0.0, base=0,
                                pattern=[[-2, 3], [0, ROWS]], channel_multiplier=1).then_inc(pool_const, 1)
        pool.wait_ge(pool_const, 7)
        nc.gpsimd.affine_select(out=kind_f, in_=kind_f, compare_op=ALU.is_ge, fill=0.0, base=1,
                                pattern=[[2, 3], [0, ROWS]], channel_multiplier=-1).then_inc(pool_const, 1)
        pool.wait_ge(zero_out, shared['zeroed'])
        pool.wait_ge(dest_done, 1)
        pool.wait_ge(pool_const, 5)
        for t in range(NT):
            for k in range(TOPK):
                a = t * TOPK + k
                nc.gpsimd.indirect_dma_start(out=rowtok_d, out_offset=bass.IndirectOffsetOnAxis(ap=dest[:, a:a + 1], axis=0),
                                             in_=tok_id[:, t:t + 1], in_offset=None).then_inc(scattered, 16)
        pool.wait_ge(table_done, 1)
        n_pairs = pool.value_load(starts[0:1, MAXR + 1:MAXR + 2], min_val=1, max_val=E)
        rounds = pool.value_load(table[0:1, MAXR + 1:MAXR + 2], min_val=2, max_val=MAXR - 1)
        pool.wait_ge(scattered, 16 * NT * TOPK)
        pool.wait_ge(hn_out[0], 16 * (NT // 2))
        pool.wait_ge(hn_out[1], 16 * (NT // 2))

        pool.wait_ge(bias_out, 32)

        def gather(r, tiles):
            start = pool.value_load(starts[0:1, bass.ds(r, 1)], min_val=0, max_val=(MAXB - 2) * ROWS)
            for b in range(tiles):
                pool.dma_start(idx_t[:, b:b + 1], rowtok_d[bass.ds(start + b * ROWS, ROWS), :]).then_inc(idx_in[b], 16)
            for b in range(tiles):
                pool.wait_ge(idx_in[b], r * 16 + 16)
                pool.sem_inc(pool_passed, 1)
                nc.gpsimd.indirect_dma_start(out=x_rows[:, b, :], out_offset=None, in_=hn_d,
                                             in_offset=bass.IndirectOffsetOnAxis(ap=idx_t[:, b:b + 1], axis=0)
                                             ).then_inc(rows_in[b], 16)

        def get_biases(r):
            e = pool.value_load(table[0:1, bass.ds(r, 1)], min_val=0, max_val=E - 1)
            pool.dma_start(bias_t, bias_d[bass.ds(e, 1), :, :].rearrange("a n c -> (a n) c")).then_inc(bias_got, 16)

        gather(0, 2)
        get_biases(0)
        for first, last, tiles in ((0, n_pairs, 2), (n_pairs, rounds, 1)):
            with pool.Fori(first, last) as r:
                for b in range(tiles):
                    pool.wait_ge(rows_in[b], r * 16 + 16)
                pool.wait_ge(xT_ps[2 * tiles - 1], r + 1)
                gather(r + 1, tiles)
                pool.wait_ge(piece_used, r * NPIECE + 10 + NRING)
                pool.sem_inc(pool_passed, 1)
                get_biases(r + 1)
        pool.wait_ge(y_out, rounds * 16 + 16)
        pool.wait_ge(bias_got, rounds * 16 + 16)
        pool.wait_ge(lo_done, rounds * NPIECE + NRING + NRING)
        pool.sem_inc(pool_passed, 1)
        for t in range(NT):
            if t >= NGOT:
                pool.wait_ge(sum_done, TOPK * (t - NGOT + 1))
            for k in range(TOPK):
                a = t * TOPK + k
                nc.gpsimd.indirect_dma_start(out=y_got[:, t % NGOT, k, :], out_offset=None, in_=ys_d,
                                             in_offset=bass.IndirectOffsetOnAxis(ap=dest[:, a:a + 1], axis=0)
                                             ).then_inc(got_in[t % NGOT], 16)

    def on_scalar(act):
        for t in range(NT + 1):
            if t == 3:
                act.wait_ge(bias_in, 48)
                nc.scalar.activation(bias_hi, bias_rows, ACT.Copy).then_inc(bias_hi_done, 1)
                act.wait_ge(pool_const, 8)
                nc.scalar.activation(kind_row, kind_f, ACT.Copy).then_inc(kind_done, 1)
            if t >= 1:
                u = t - 1
                act.wait_ge(hnT_ps, u + 1)
                if u >= 2:
                    act.wait_ge(logit_ps, u - 1)
                for h in range(2):
                    nc.scalar.activation(hnT[:, u % 2, 4 * h:4 * h + 4, :],
                                         bank[4 + h][:, 0:4 * TP].rearrange("p (k t) -> p k t", k=4),
                                         ACT.Copy).then_inc(hnT_done, 1)
            if t < NT:
                act.wait_ge(wo_add, 2 * (t + 1))
                if t >= 1:
                    act.wait_ge(sq_done, t)
                nc.scalar.activation(junk, h_all[:, t, :], ACT.Square, accum_out=ss[:, t:t + 1]).then_inc(sq_done, 1)
                act.wait_ge(sq_done, t + 1)
                nc.scalar.activation(rstd[:, t:t + 1], ss[:, t:t + 1], ACT.Sqrt, bias=eps_t[0:TP, :], scale=1.0 / D
                                     ).then_inc(std_done, 1)
        act.wait_ge(gexp_in, 1)
        nc.scalar.activation(gates[:, :, :], gates[:, :, :], ACT.Exp).then_inc(gexp_done, 1)

        act.wait_ge(table_done, 1)
        n_pairs = act.value_load(starts[0:1, MAXR + 1:MAXR + 2], min_val=1, max_val=E)
        rounds = act.value_load(table[0:1, MAXR + 1:MAXR + 2], min_val=2, max_val=MAXR - 1)

        def split_hi(n, use, j):
            act.wait_ge(raw_in[j % NRING], use)
            act.wait_ge(piece_used, n + 1)
            nc.scalar.activation(w_hi[:, j % NRING, :, :], raw[:, j % NRING, :, :], ACT.Copy).then_inc(hi_done, 1)

        def x_hi_part(r, f):
            act.wait_ge(xT_ps[f], r + 1)
            nc.scalar.activation(x_hi[:, f // 2, 4 * (f % 2):4 * (f % 2) + 4, :], tx_ps[:, :].rearrange("p (k s) -> p k s", k=4),
                                 ACT.Copy).then_inc(xhi_done[f], 1)

        def a_hi_part(r, h, t):
            act.wait_ge(aT_ps[t], r * 2 + h + 2)
            nc.scalar.activation(a_hi[:, t, 4 * h:4 * h + 4, :], ta_ps[:, :].rearrange("p (k s) -> p k s", k=4),
                                 ACT.Copy).then_inc(ahi_done[t], 1)

        for j in range(NRING):
            split_hi(j, 16, j)
        for f in range(4):
            x_hi_part(0, f)
        for first, last, tiles in ((0, n_pairs, 2), (n_pairs, rounds, 1)):
            with act.Fori(first, last) as r:
                for j in range(NPIECE):
                    jn = j + NRING
                    if j in (10, 11):
                        split_hi(r * NPIECE + jn, r * 48 + 16 * (jn // NRING) + 16, jn % NPIECE)
                        if j == 10:
                            act.wait_ge(y_out, r * 16 + 16)
                        act.wait_ge(piece_used, r * NPIECE + j + 1 + NRING)
                        for t in range(tiles):
                            nc.scalar.activation(y_rows[:, t, HC * (j - 10):HC * (j - 9)], y_ps[j - 10][t][:, :], ACT.Copy
                                                 ).then_inc(y_read[t], 1)
                        if j == 10 and tiles == 2:
                            x_hi_part(r + 1, 3)
                        continue
                    split_hi(r * NPIECE + jn, r * 48 + 16 * (jn // NRING) + 16, jn % NPIECE)
                    if j in (1, 5):
                        h = j // 4
                        for t in range(tiles):
                            act.wait_ge(gu_read[t], r * 4 + 2 * h + 3)
                            act.wait_ge(glu_done[t], r * 2 + h + 1)
                            nc.scalar.activation(s_t[:, t, :], g_t[:, t, :], ACT.Sigmoid, scale=ALPHA).then_inc(sig_done[t], 1)
                    if j == 4 and tiles == 2:
                        a_hi_part(r, 0, 0)
                    if j == 5:
                        a_hi_part(r, 0, tiles - 1)
                    if j in X_AFTER[tiles]:
                        x_hi_part(r + 1, X_AFTER[tiles].index(j))
                    if j == 8:
                        for t in range(tiles):
                            a_hi_part(r, 1, t)
                for t in range(tiles):
                    act.wait_ge(y_read[t], r * 2 + 3)
                start = act.value_load(starts[0:1, bass.ds(r, 1)], min_val=0, max_val=(MAXB - (4 if tiles == 2 else 2)) * ROWS)
                act.dma_start(ys_d[bass.ds(start, tiles * ROWS), :].rearrange("(b p) d -> p b d", b=tiles),
                              y_rows[:, 0:tiles, :]).then_inc(y_out, 16)
        for t in range(NT):
            act.wait_ge(sum_done, TOPK * (t + 1))
            if t >= 1:
                act.wait_ge(fsq_done, t)
            nc.scalar.activation(fin_junk, h_all[:, t, :], ACT.Square, accum_out=fss[:, t:t + 1]).then_inc(fsq_done, 1)
            act.wait_ge(fsq_done, t + 1)
            nc.scalar.activation(frs[:, t:t + 1], fss[:, t:t + 1], ACT.Sqrt, bias=eps_t[0:TP, :], scale=1.0 / D
                                 ).then_inc(fstd_done, 1)

    def on_vector(dve):
        steps = [0]

        def link(ins):
            steps[0] += 1
            ins.then_inc(route, 1)
            dve.wait_ge(route, steps[0])

        nc.vector.memset(ones, 1.0).then_inc(dve_const, 1)
        free = [(lo_done, NRING), (piece_used, NRING), (y_out, 16)]
        free += [(s[t], n) for t in range(2) for s, n in ((gu_read, 2), (glu_done, 1), (aT_ps, 1), (alo_done, 1), (y_read, 1))]
        for i, (s, n) in enumerate(free):
            nc.vector.memset(dump[:, i:i + 1], 0.0).then_inc(s, n)
        def choose(u):
            dve.wait_ge(logit_ps, u + 1)
            nc.vector.tensor_tensor(lg[:, u % 2, :], bank[6 + u % 2][0:TP, 0:E], br_b, ALU.add).then_inc(lg_read, 1)
            dve.wait_ge(lg_read, u + 1)
            link(nc.vector.max(top_v[:, u, :], lg[:, u % 2, :]))
            nc.vector.max_index(top_i[:, u, :], top_v[:, u, :], lg[:, u % 2, :]).then_inc(top_done, 1)

        for t in range(NT):
            if t % 2 == 0:
                dve.wait_ge(h_in[t // 2], 48 if t == 0 else 32)
            for n in range(2):
                dve.wait_ge(wo_ps, 2 * t + n + 1)
                nc.vector.tensor_tensor(h_all[:, t, 512 * n:512 * (n + 1)], bank[2 * (t % 2) + n][0:TP, :],
                                        h_all[:, t, 512 * n:512 * (n + 1)], ALU.add).then_inc(wo_add, 1)
            dve.wait_ge(std_done, t + 1)
            nc.vector.reciprocal(rstd[:, t:t + 1], rstd[:, t:t + 1]).then_inc(rstd_done, 1)
            dve.wait_ge(rstd_done, t + 1)
            if t == 0:
                dve.wait_ge(const_in, 48)
            if t >= 2:
                dve.wait_ge(hn_out[t % 2], 16 * (t // 2))
                dve.wait_ge(hnT_ps, t - 1)
            nc.vector.scalar_tensor_tensor(out=hn[:, t % 2, :], in0=h_all[:, t, :], scalar=rstd[:, t:t + 1], in1=g2_b,
                                           op0=ALU.mult, op1=ALU.mult).then_inc(hn_done, 1)
            if t >= 1:
                choose(t - 1)
            if t == 4:
                dve.wait_ge(bias_hi_done, 1)
                nc.vector.tensor_tensor(bias_lo, bias_rows, bias_hi.bitcast(f32), ALU.subtract).then_inc(bias_lo_done, 1)
        choose(NT - 1)
        dve.wait_ge(top_done, NT)
        nc.vector.tensor_tensor(gates[:, :, :], top_v[:, :, 0:TOPK], top_v[:, :, 0:1].to_broadcast([TP, NT, TOPK]),
                                ALU.subtract).then_inc(gexp_in, 1)
        link(nc.vector.tensor_copy(top_f.rearrange("p (t k) -> p t k", k=TOPK), top_i[:, :, 0:TOPK]))
        dve.wait_ge(pool_const, 5)
        link(nc.vector.tensor_tensor(onehot, iota_e.unsqueeze(1).to_broadcast([TP, NT * TOPK, E]),
                                     top_f.unsqueeze(2).to_broadcast([TP, NT * TOPK, E]), ALU.is_equal))
        link(nc.vector.tensor_reduce(chosen, onehot.rearrange("p (t k) e -> p t e k", k=TOPK), axis=AX.X, op=ALU.add))
        link(nc.vector.memset(before[:, 0, :], 0.0))
        for t in range(NT):
            ins = nc.vector.tensor_tensor(before[:, t + 1, :], before[:, t, :], chosen[:, t, :], ALU.add)
            if t == NT - 1:
                ins.then_inc(chosen_done, 1)
            else:
                link(ins)
        dve.wait_ge(gexp_done, 1)
        link(nc.vector.tensor_reduce(gsum, gates[:, :, :], axis=AX.X, op=ALU.add))
        link(nc.vector.reciprocal(gsum, gsum))
        link(nc.vector.tensor_tensor(gates[:, :, :], gates[:, :, :], gsum.unsqueeze(2).to_broadcast([TP, NT, TOPK]),
                                     ALU.mult))
        dve.wait_ge(rank_ps, 2)
        link(nc.vector.tensor_copy(cnt, bank[1][0:TP, 0:E]))
        link(nc.vector.tensor_copy(rank, bank[0][0:TP, 0:NT * E].rearrange("p (t e) -> p t e", e=E)))
        link(nc.vector.tensor_scalar(pairs, cnt, float(ROWS), None, ALU.is_gt))
        for m in range(1, (TOK - ROWS - 1) // (2 * ROWS) + 1):
            link(nc.vector.scalar_tensor_tensor(out=pairs, in0=cnt, scalar=float((2 * m + 1) * ROWS), in1=pairs,
                                                op0=ALU.is_gt, op1=ALU.add))
        link(nc.vector.tensor_scalar(pair_rows, pairs, float(2 * ROWS), None, ALU.mult))
        link(nc.vector.tensor_tensor(singles, cnt, pair_rows, ALU.is_gt))
        link(nc.vector.memset(over, 1.0))
        link(nc.vector.tensor_tensor_scan(pair_end, over, pairs, 0.0, ALU.mult, ALU.add))
        link(nc.vector.tensor_tensor_scan(single_end, over, singles, 0.0, ALU.mult, ALU.add))
        link(nc.vector.tensor_tensor(pair_base, pair_end, pairs, ALU.subtract))
        link(nc.vector.tensor_scalar(pair_base, pair_base, float(2 * ROWS), None, ALU.mult))
        link(nc.vector.tensor_tensor(single_base, single_end, singles, ALU.subtract))
        link(nc.vector.scalar_tensor_tensor(out=single_base, in0=pair_end[:, E - 1:E].to_broadcast([TP, E]), scalar=2.0,
                                            in1=single_base, op0=ALU.mult, op1=ALU.add))
        link(nc.vector.tensor_scalar(single_base, single_base, float(ROWS), None, ALU.mult))
        link(nc.vector.tensor_tensor(single_base, single_base, pair_rows, ALU.subtract))
        link(nc.vector.tensor_tensor(single_base, single_base, pair_base, ALU.subtract))
        link(nc.vector.tensor_tensor(in_single, rank, pair_rows.unsqueeze(1).to_broadcast([TP, NT, E]), ALU.is_ge))
        link(nc.vector.tensor_tensor(in_single, in_single, single_base.unsqueeze(1).to_broadcast([TP, NT, E]), ALU.mult))
        link(nc.vector.tensor_tensor(rank, rank, in_single, ALU.add))
        link(nc.vector.tensor_tensor(rank, rank, pair_base.unsqueeze(1).to_broadcast([TP, NT, E]), ALU.add))
        oh4 = onehot.rearrange("p (t k) e -> p t k e", k=TOPK)
        for t in range(NT):
            link(nc.vector.tensor_tensor(oh4[:, t, :, :], oh4[:, t, :, :],
                                         rank[:, t, :].unsqueeze(1).to_broadcast([TP, TOPK, E]), ALU.mult))
        link(nc.vector.tensor_reduce(dest_f, onehot, axis=AX.X, op=ALU.add))
        nc.vector.tensor_copy(dest[:, :], dest_f).then_inc(dest_done, 1)
        link(nc.vector.tensor_tensor(ended, iota_q.unsqueeze(2).to_broadcast([1, MAXR + 1, E]),
                                     pair_end[0:1, :].unsqueeze(1).to_broadcast([1, MAXR + 1, E]), ALU.is_ge))
        link(nc.vector.tensor_reduce(table_f, ended, axis=AX.X, op=ALU.add))
        n_pairs_f = pair_end[0:1, E - 1:E]
        link(nc.vector.tensor_scalar(single_end[0:1, :], single_end[0:1, :], n_pairs_f, None, ALU.add))
        link(nc.vector.tensor_tensor(ended, iota_q.unsqueeze(2).to_broadcast([1, MAXR + 1, E]),
                                     single_end[0:1, :].unsqueeze(1).to_broadcast([1, MAXR + 1, E]), ALU.is_ge))
        link(nc.vector.tensor_reduce(table_s, ended, axis=AX.X, op=ALU.add))
        link(nc.vector.tensor_tensor(table_f, table_f, table_s, ALU.add))
        link(nc.vector.tensor_scalar(table_s, iota_q, n_pairs_f, float(-E), ALU.is_ge, ALU.mult))
        link(nc.vector.tensor_tensor(table_f, table_f, table_s, ALU.add))
        link(nc.vector.tensor_scalar(table[0:1, 0:MAXR + 1], table_f, float(E - 1), None, ALU.min))
        link(nc.vector.tensor_scalar(start_f, iota_q, n_pairs_f, None, ALU.min))
        link(nc.vector.tensor_tensor(start_f, start_f, iota_q, ALU.add))
        link(nc.vector.tensor_scalar(starts[0:1, 0:MAXR + 1], start_f, float(ROWS), float((MAXB - 2) * ROWS), ALU.mult, ALU.min))
        link(nc.vector.tensor_copy(starts[0:1, MAXR + 1:MAXR + 2], n_pairs_f))
        link(nc.vector.tensor_scalar(total_f, n_pairs_f, 1.0, None, ALU.add))
        link(nc.vector.tensor_tensor(total_f, total_f, single_end[0:1, E - 1:E], ALU.max))
        nc.vector.tensor_copy(table[0:1, MAXR + 1:MAXR + 2], total_f).then_inc(table_done, 1)
        dve.wait_ge(table_done, 1)
        n_pairs = dve.value_load(starts[0:1, MAXR + 1:MAXR + 2], min_val=1, max_val=E)
        rounds = dve.value_load(table[0:1, MAXR + 1:MAXR + 2], min_val=2, max_val=MAXR - 1)

        def split_lo(n, j):
            dve.wait_ge(hi_done, n + 1)
            nc.vector.tensor_tensor(w_lo[:, j % NRING, :, :], raw[:, j % NRING, :, :],
                                    w_hi[:, j % NRING, :, :].bitcast(f32), ALU.subtract).then_inc(lo_done, 1)

        def x_lo_part(r, f):
            dve.wait_ge(xhi_done[f], r + 1)
            part = (slice(None), f // 2, slice(4 * (f % 2), 4 * (f % 2) + 4), slice(None))
            nc.vector.tensor_tensor(x_lo[part], tx_ps[:, :].rearrange("p (k s) -> p k s", k=4), x_hi[part].bitcast(f32),
                                    ALU.subtract).then_inc(xlo_done[f], 1)

        def a_lo_part(r, h, t):
            dve.wait_ge(ahi_done[t], r * 2 + h + 1)
            part = (slice(None), t, slice(4 * h, 4 * h + 4), slice(None))
            nc.vector.tensor_tensor(a_lo[part], ta_ps[:, :].rearrange("p (k s) -> p k s", k=4), a_hi[part].bitcast(f32),
                                    ALU.subtract).then_inc(alo_done[t], 1)

        for j in range(NRING):
            split_lo(j, j)
        for f in range(4):
            x_lo_part(0, f)
        for first, last, tiles in ((0, n_pairs, 2), (n_pairs, rounds, 1)):
            with dve.Fori(first, last) as r:
                for j in range(NPIECE):
                    h = j // 4
                    if j in (1, 5):
                        dve.wait_ge(piece_used, r * NPIECE + j + 1 + NRING)
                        for t in range(tiles):
                            nc.vector.tensor_scalar(g_t[:, t, :], gate_ps[t][:, :], LIMIT, None, ALU.min
                                                    ).then_inc(gu_read[t], 1)
                    if j in (3, 7):
                        dve.wait_ge(piece_used, r * NPIECE + j + 1 + NRING)
                        for t in range(tiles):
                            dve.wait_ge(aT_ps[t], r * 2 + h + 1)
                            nc.vector.tensor_scalar(u_t[:, t, :], up_ps[t][:, :], LIMIT, -LIMIT, ALU.min, ALU.max
                                                    ).then_inc(gu_read[t], 1)
                        for t in range(tiles):
                            dve.wait_ge(gu_read[t], r * 4 + 2 * h + 4)
                            nc.vector.scalar_tensor_tensor(out=u_t[:, t, :], in0=u_t[:, t, :], scalar=1.0, in1=g_t[:, t, :],
                                                           op0=ALU.add, op1=ALU.mult).then_inc(glu_mid[t], 1)
                        for t in range(tiles):
                            dve.wait_ge(glu_mid[t], r * 2 + h + 1)
                            dve.wait_ge(sig_done[t], r * 2 + h + 1)
                            nc.vector.tensor_tensor(u_t[:, t, :], u_t[:, t, :], s_t[:, t, :], ALU.mult).then_inc(glu_done[t], 1)
                    split_lo(r * NPIECE + j + NRING, (j + NRING) % NPIECE)
                    if j == 4 and tiles == 2:
                        a_lo_part(r, 0, 0)
                    if j == 5:
                        a_lo_part(r, 0, tiles - 1)
                    if j in X_AFTER[tiles]:
                        x_lo_part(r + 1, X_AFTER[tiles].index(j))
                    if j == 8:
                        for t in range(tiles):
                            a_lo_part(r, 1, t)
        dve.wait_ge(gf_in, 16)

        def finish(t):
            dve.wait_ge(fstd_done, t + 1)
            nc.vector.reciprocal(frs[:, t:t + 1], frs[:, t:t + 1]).then_inc(frs_done, 1)
            dve.wait_ge(frs_done, t + 1)
            if t >= 2:
                dve.wait_ge(out_done[t % 2], 16 * (t // 2))
            nc.vector.scalar_tensor_tensor(out=fin[:, t % 2, :], in0=h_all[:, t, :], scalar=frs[:, t:t + 1], in1=gf_b,
                                           op0=ALU.mult, op1=ALU.mult).then_inc(fin_done, 1)

        for t in range(NT):
            dve.wait_ge(got_in[t % NGOT], 16 * TOPK * (t // NGOT + 1))
            for k in range(TOPK):
                if t or k:
                    dve.wait_ge(sum_done, TOPK * t + k)
                ins = nc.vector.scalar_tensor_tensor(out=h_all[:, t, :], in0=y_got[:, t % NGOT, k, :], scalar=gates[:, t, k:k + 1],
                                                     in1=h_all[:, t, :], op0=ALU.mult, op1=ALU.add)
                ins.then_inc(sum_done, 1)
            if t >= 1:
                finish(t - 1)
        finish(NT - 1)

    def on_tensor(pe):
        def project_out(t, n):
            if t == 0:
                pe.wait_ge(wo_in[n], 16)
            if t >= 2:
                pe.wait_ge(wo_add, 2 * (t - 2) + n + 1)
            for k in range(KT):
                ins = nc.tensor.matmul(bank[2 * (t % 2) + n][0:TP, :], mT[:, k, TP * t:TP * (t + 1)],
                                       wo_t[:, k, 512 * n:512 * (n + 1)], start=k == 0, stop=k == KT - 1)
            ins.then_inc(wo_ps, 1)

        pe.wait_ge(gate_mul, 3 * KT * 4 + 6)
        for t in range(NT + 1):
            u = t - 1
            if t < NT:
                project_out(t, 0)
            if t >= 1:
                pe.wait_ge(hn_done, u + 1)
                if u >= 1:
                    pe.wait_ge(hnT_done, 2 * u)
                for k in range(KT):
                    ins = nc.tensor.transpose(bank[4 + k // 4][:, (k % 4) * TP:(k % 4 + 1) * TP],
                                              hn[:, u % 2, k * 128:(k + 1) * 128], ident[0:TP, 0:TP])
                ins.then_inc(hnT_ps, 1)
            if t < NT:
                project_out(t, 1)
            if t >= 1:
                if u == 0:
                    pe.wait_ge(const_in, 48)
                pe.wait_ge(hnT_done, 2 * (u + 1))
                if u >= 2:
                    pe.wait_ge(lg_read, u - 1)
                for k in range(KT):
                    ins = nc.tensor.matmul(bank[6 + u % 2][0:TP, 0:E], hnT[:, u % 2, k, :], wr_t[:, k, :],
                                           start=k == 0, stop=k == KT - 1)
                ins.then_inc(logit_ps, 1)
        pe.wait_ge(chosen_done, 1)
        pe.wait_ge(pool_const, 2)
        pe.wait_ge(dve_const, 1)
        nc.tensor.matmul(bank[0][0:TP, 0:NT * E], tri, chosen.rearrange("p t e -> p (t e)"), start=True, stop=False)
        nc.tensor.matmul(bank[0][0:TP, 0:NT * E], ones[:, 0:TP], before[:, 0:NT, :].rearrange("p t e -> p (t e)"),
                         start=False, stop=True).then_inc(rank_ps, 1)
        nc.tensor.matmul(bank[1][0:TP, 0:E], ones[:, 0:TP], before[:, NT, :], start=True, stop=True).then_inc(rank_ps, 1)
        pe.wait_ge(table_done, 1)
        n_pairs = pe.value_load(starts[0:1, MAXR + 1:MAXR + 2], min_val=1, max_val=E)
        rounds = pe.value_load(table[0:1, MAXR + 1:MAXR + 2], min_val=2, max_val=MAXR - 1)
        pe.wait_ge(kind_done, 1)

        def x_part(r, f):
            t = f // 2
            pe.wait_ge(rows_in[t], r * 16 + 16)
            if f >= 1:
                pe.wait_ge(xlo_done[f - 1], r + 1)
            for k in range(4):
                c = (4 * (f % 2) + k) * 128
                ins = nc.tensor.transpose(tx_ps[:, k * 128:(k + 1) * 128], x_rows[:, t, c:c + 128], ident[:, :])
            ins.then_inc(xT_ps[f], 1)

        def a_part(r, h, t, tiles):
            pe.wait_ge(glu_done[t], r * 2 + h + 2)
            if t == 1:
                pe.wait_ge(alo_done[0], r * 2 + h + 2)
            else:
                pe.wait_ge(alo_done[tiles - 1], r * 2 + h + 1)
            for k in range(4):
                ins = nc.tensor.transpose(ta_ps[:, k * 128:(k + 1) * 128], u_t[:, t, k * 128:(k + 1) * 128], ident[:, :])
            ins.then_inc(aT_ps[t], 1)

        def product(ps, m_hi, m_lo, slot, k, start, stop=False):
            nc.tensor.matmul(ps, m_hi, w_hi[:, slot, k, :], start=start, stop=False)
            nc.tensor.matmul(ps, m_hi, w_lo[:, slot, k, :], start=False, stop=False)
            return nc.tensor.matmul(ps, m_lo, w_hi[:, slot, k, :], start=False, stop=stop)

        for f in range(4):
            x_part(0, f)
        for first, last, tiles in ((0, n_pairs, 2), (n_pairs, rounds, 1)):
            with pe.Fori(first, last) as r:
                for j in range(8):
                    g, h = j // 2, j // 4
                    ps = (gate_ps, up_ps)[g % 2]
                    pe.wait_ge(lo_done, r * NPIECE + j + 1 + NRING)
                    if j == 0:
                        for f in range(2 * tiles):
                            pe.wait_ge(xlo_done[f], r + 1)
                    for t in range(tiles):
                        if j == 2:
                            pe.wait_ge(y_read[t], r * 2 + 1)
                        elif j % 2 == 0:
                            pe.wait_ge(gu_read[t], r * 4 + g + 1)
                        for k in range(HK):
                            kk = HK * (j % 2) + k
                            ins = product(ps[t][:, :], x_hi[:, t, kk, :], x_lo[:, t, kk, :], j % NRING, k, kk == 0)
                        if j % 2 == 1:
                            if j == 1 and t == 0:
                                pe.wait_ge(bias_got, r * 16 + 16)
                            ins = nc.tensor.matmul(ps[t][:, :], kind_row[:, g % 2, :], bias_t[:, HC * h:HC * (h + 1)],
                                                   start=False, stop=True)
                    ins.then_inc(piece_used, 1)
                    if j == 4 and tiles == 2:
                        a_part(r, 0, 0, tiles)
                    if j == 5:
                        a_part(r, 0, tiles - 1, tiles)
                for j in range(8, NPIECE):
                    if j - 1 in X_AFTER[tiles]:
                        x_part(r + 1, X_AFTER[tiles].index(j - 1))
                    if j == 9:
                        a_part(r, 1, 0, tiles)
                    pe.wait_ge(lo_done, r * NPIECE + j + 1 + NRING)
                    for t in range(tiles):
                        if j == 9 and t == 1:
                            a_part(r, 1, 1, tiles)
                        pe.wait_ge(alo_done[t], r * 2 + 2 + (j - 8) // 2)
                        ps = y_ps[j % 2][t][:, :]
                        if j == 9:
                            pe.wait_ge(gu_read[t], r * 4 + 6)
                        if j < 10:
                            nc.tensor.matmul(ps, kind_row[:, 2, :], bias_t[:, HC * (j - 8):HC * (j - 7)],
                                             start=True, stop=False)
                        for k in range(HK):
                            kk = HK * ((j - 8) // 2) + k
                            ins = product(ps, a_hi[:, t, kk, :], a_lo[:, t, kk, :], j % NRING, k, False, kk == KT - 1)
                    ins.then_inc(piece_used, 1)
            if tiles == 2:
                pe.wait_ge(alo_done[1], n_pairs * 2 + 1)
                for f in (2, 3):
                    pe.wait_ge(xlo_done[f], n_pairs + 1)
                pe.sem_inc(pe_passed, 1)

    return on_sync, on_gpsimd, on_scalar, on_vector, on_tensor


def program(nc, a, out):
    f32 = mybir.dt.float32
    u32 = mybir.dt.uint32
    TOK, D, E, TOPK, ROWS = 1040, 1024, 32, 4, 128
    TP, NT = 104, 10
    MINB = -(-TOK * TOPK // ROWS)
    MAXB = (TOK * TOPK + E * (ROWS - 1)) // ROWS + 2
    with ExitStack() as ctx:
        bank = [ctx.enter_context(nc.psum_tensor(f"bank{i}", [128, 512], f32)) for i in range(8)]
        hn_d = nc.dram_tensor("hn_d", (TOK, D), f32).ap()
        ys_d = nc.dram_tensor("ys_d", ((MAXB - 1) * ROWS, D), f32).ap()
        rowtok_d = nc.dram_tensor("rowtok_d", (MAXB * ROWS, 1), u32).ap()
        bias_d = nc.dram_tensor("bias_d", (E, 6, D), f32).ap()
        keep = Plan(nc, (nc.sbuf_base + 63) // 64 * 64)
        shared = dict(ident=keep("ident", [128, 128]), eps_t=keep("eps_t", [128, 1]))
        shared.update(gates=keep("gates", [TP, NT, TOPK]), dest=keep("dest", [TP, NT * TOPK], u32))
        shared['start'] = keep.at + 256
        at_h = Plan(nc, shared['start'])
        shared['h_all'] = at_h("h_all", [TP, NT, D])
        shared['after_h'] = at_h.at
        shared['zero_out'] = ctx.enter_context(nc.semaphore("zero_out"))
        for name in ("wo_add", "gate_mul"):
            shared[name] = ctx.enter_context(nc.semaphore(name))
        shared["h_in"] = [ctx.enter_context(nc.semaphore(f"h_in{n}")) for n in range(NT // 2)]
        shared["wo_in"] = [ctx.enter_context(nc.semaphore(f"wo_in{n}")) for n in range(2)]
        ys_rest = [ys_d[b * ROWS:(b + 2) * ROWS, :].rearrange("(p b) d -> p (b d)", b=2) for b in range(MINB, MAXB - 1, 2)]
        shared.update(hn_d=hn_d, ys_d=ys_d, rowtok_d=rowtok_d, bias_d=bias_d, blocks=MAXB, ys_rest=ys_rest,
                      rowtok_rows=rowtok_d.rearrange("(q s) a -> q (s a)", s=ROWS), zeroed=16 * (1 + len(ys_rest)))
        mixing = mixing_program(nc, ctx, a, bank, keep, shared)
        assert keep.at <= shared['start']
        experts = experts_program(nc, ctx, a, bank, shared, out)

        block = ctx.enter_context(nc.Block())

        @block.sync
        def _(sp):
            for part in (mixing, experts):
                part[0](sp)

        @block.gpsimd
        def _(pool):
            for part in (mixing, experts):
                part[1](pool)

        @block.scalar
        def _(act):
            for part in (mixing, experts):
                part[2](act)

        @block.vector
        def _(dve):
            for part in (mixing, experts):
                part[3](dve)

        @block.tensor
        def _(pe):
            for part in (mixing, experts):
                part[4](pe)


_INS = ['x', 'meta_tokens', 'ln1_g', 'w_in', 'mu_r', 'mu_k', 'mu_v', 'mu_w', 'mu_a', 'mu_g', 'w0', 'w_w1', 'w_w2', 'a0', 'w_a1', 'w_a2',
        'w_g1', 'w_g2', 'k_k', 'k_a', 'r_k', 'lnx_g', 'lnx_b', 'w_o_rwkv', 'conv_w', 'w_o_conv', 'w_o', 'ln2_g', 'w_router', 'b_router',
        'w_e_gate', 'b_e_gate', 'w_e_up', 'b_e_up', 'w_e_down', 'b_e_down', 'lnf_g']


def kernel(**inputs):
    import numpy as _np
    import concourse.bacc as _bacc
    from concourse import mybir as _mybir
    from concourse.bass_utils import run_bass_kernel_spmd as _run

    nc = _bacc.Bacc("TRN2", target_bir_lowering=False, num_devices=1)
    arrays, a = {}, {}
    for name in _INS:
        x = _np.ascontiguousarray(inputs[name])
        arrays[f"in_{name}"] = x
        ap = nc.dram_tensor(f"in_{name}", x.shape, _mybir.dt.from_np(x.dtype), kind="ExternalInput").ap()
        a[name] = ap if name in ('meta_tokens', 'lnf_g') else ap[0]
    out = nc.dram_tensor("out_0", (1024, 1024), _mybir.dt.float32, kind="ExternalOutput").ap()
    program(nc, a, out)
    r = _run(nc, [arrays], core_ids=[0])
    return r.results[0]["out_0"].reshape(1, 1024, 1024)
```
